# Optimizing a Trainium2 kernel written in Bass

```python
import numpy as np
import jax, jax.numpy as jnp
from jax import lax

D_MODEL = 1024
BATCH = 1
SEQ = 1024
DEPTH = 2

GRID_W = 64
CTX_LEN = 256
HEAD_DIM = 64
RET_HEADS = D_MODEL // (2 * HEAD_DIM)
NA_HEADS = D_MODEL // (2 * HEAD_DIM)
RET_W = RET_HEADS * HEAD_DIM
NA_W = NA_HEADS * HEAD_DIM
MIX_W = RET_W + NA_W
AB_IN = 4 * RET_W + 3 * NA_W
RET_CHUNK = 128
RET_DECAY_BASE = 5.0
GN_EPS = 1e-5
NA_KH = 8
NA_KW = 16
SWA_HEADS = D_MODEL // HEAD_DIM
SWA_KV_HEADS = SWA_HEADS // 4
SWA_WINDOW = 128
SWA_BLOCK = 128
SWA_IN = (SWA_HEADS + 2 * SWA_KV_HEADS) * HEAD_DIM
ROPE_BASE = 10000.0
MOE_GROUPS = 4
MOE_EPG = 8
MOE_EXPERTS = MOE_GROUPS * MOE_EPG
MOE_TOPK = 2
MOE_FF = D_MODEL // 2
MOE_BLOCK = 128
NORM_EPS = 1e-6
NEG_INF = -1e30

kernel_name = 'hybrid_retention_natten_swa_hmoe_dit'

def rms_norm(x, g):
    xf = x.astype(jnp.float32)
    y = xf * lax.rsqrt(jnp.mean(xf * xf, axis=-1, keepdims=True) + NORM_EPS)
    return (y * g.astype(jnp.float32)).astype(x.dtype)

def modulate(h, shift, scale):
    return h * (1 + scale) + shift

def split_heads(t, n):
    return t.reshape(*t.shape[:-1], n, HEAD_DIM)

def axial_rope_tables(L):
    nf = HEAD_DIM // 4
    inv = ROPE_BASE ** (-jnp.arange(nf, dtype=jnp.float32) / nf)
    t = jnp.arange(L)
    row = (t // GRID_W).astype(jnp.float32)
    col = (t % GRID_W).astype(jnp.float32)
    ang = jnp.concatenate([row[:, None] * inv, col[:, None] * inv], axis=-1)
    return jnp.cos(ang), jnp.sin(ang)

def apply_rope(x, cos, sin):
    nf = x.shape[-1] // 4
    xr = x.reshape(*x.shape[:-1], 2, 2, nf)
    x1, x2 = xr[..., 0, :], xr[..., 1, :]
    c = cos.reshape(cos.shape[0], 1, 2, nf).astype(x.dtype)
    s = sin.reshape(sin.shape[0], 1, 2, nf).astype(x.dtype)
    out = jnp.stack([x1 * c - x2 * s, x2 * c + x1 * s], axis=-2)
    return out.reshape(x.shape)

def retention_scan(q, k, v, log_gamma, state0):
    b, h, L, dk = q.shape
    dv = v.shape[-1]
    n = L // RET_CHUNK
    lg = log_gamma.astype(jnp.float32)[:, None]
    pos = jnp.arange(RET_CHUNK, dtype=jnp.float32)
    rel = pos[:, None] - pos[None, :]
    intra = jnp.where(rel >= 0, jnp.exp(lg[:, :, None] * jnp.maximum(rel, 0.0)), 0.0)
    q_decay = jnp.exp(lg * (pos + 1.0))[..., None]
    k_decay = jnp.exp(lg * (RET_CHUNK - 1.0 - pos))[..., None]
    chunk_decay = jnp.exp(lg[:, 0] * RET_CHUNK)[:, None, None]

    def to_chunks(t):
        return t.reshape(b, h, n, RET_CHUNK, t.shape[-1]).transpose(2, 0, 1, 3, 4)

    def step(state, qkv):
        qc, kc, vc = qkv
        s = jnp.einsum('bhnd,bhmd->bhnm', qc, kc) * intra
        out = jnp.einsum('bhnm,bhme->bhne', s, vc) + jnp.einsum('bhnd,bhde->bhne', qc, state) * q_decay
        state = state * chunk_decay + jnp.einsum('bhmd,bhme->bhde', kc * k_decay, vc)
        return state, out

    state, out = lax.scan(step, state0, (to_chunks(q), to_chunks(k), to_chunks(v)))
    return out.transpose(1, 2, 0, 3, 4).reshape(b, h, L, dv), state

def retention_readout(o, gate, gain):
    o = o.transpose(0, 2, 1, 3)
    mu = jnp.mean(o, axis=-1, keepdims=True)
    var = jnp.mean(jnp.square(o - mu), axis=-1, keepdims=True)
    o = ((o - mu) * lax.rsqrt(var + GN_EPS)).reshape(gate.shape) * gain.astype(jnp.float32)
    return (jax.nn.silu(gate.astype(jnp.float32)) * o).astype(gate.dtype)

def context_attention(q, k, v, sink=None):
    b, lc, hq, d = q.shape
    hk = k.shape[2]
    g = hq // hk
    qg = q.reshape(b, lc, hk, g, d)
    s = jnp.einsum('bqkgd,bmkd->bkgqm', qg, k).astype(jnp.float32)
    if sink is not None:
        sink_col = jnp.broadcast_to(sink.astype(jnp.float32).reshape(hk, g, 1, 1), (b, hk, g, lc, 1))
        s = jnp.concatenate([s, sink_col], axis=-1)
    p = jax.nn.softmax(s, axis=-1)[..., :lc].astype(v.dtype)
    o = jnp.einsum('bkgqm,bmkd->bqkgd', p, v)
    return o.reshape(b, lc, hq * d)

def na_column_layout():
    nj = GRID_W // NA_KW
    kb = 2 * NA_KW
    starts = np.clip(np.arange(nj) * NA_KW - NA_KW // 2, 0, GRID_W - kb)
    key_col = starts[:, None] + np.arange(kb)[None, :]
    q_col = np.arange(nj)[:, None] * NA_KW + np.arange(NA_KW)[None, :]
    win = np.clip(q_col - NA_KW // 2, 0, GRID_W - NA_KW)
    kc3 = key_col[:, None, :]
    valid = (kc3 >= win[..., None]) & (kc3 < win[..., None] + NA_KW)
    col_off = np.clip(kc3 - q_col[..., None] + NA_KW - 1, 0, 2 * NA_KW - 2)
    return key_col, valid, col_off

def neighbourhood_attention(q, k, v, kc, vc, rpb):
    b, L, h, d = q.shape
    rows = L // GRID_W
    kh = min(NA_KH, rows)
    key_col, col_valid, col_off = na_column_layout()
    nj, kb = key_col.shape
    grid = lambda t: t.reshape(b, rows, GRID_W, h, d).transpose(0, 3, 1, 2, 4)
    qg, kg, vg = grid(q), grid(k), grid(v)
    kct, vct = kc.transpose(0, 2, 1, 3), vc.transpose(0, 2, 1, 3)
    valid = jnp.asarray(np.broadcast_to(col_valid[:, :, None, :], (nj, NA_KW, kh, kb)).reshape(nj, NA_KW, kh * kb))
    rpb_cols = rpb[:, :, col_off]
    n_loc = kh * kb

    def row_block(r):
        rs = jnp.clip(r - kh // 2, 0, rows - kh)
        q_r = lax.dynamic_index_in_dim(qg, r, axis=2, keepdims=False).reshape(b, h, nj, NA_KW, d)

        def gather(t):
            t = lax.dynamic_slice_in_dim(t, rs, kh, axis=2)[:, :, :, key_col]
            return t.transpose(0, 1, 3, 2, 4, 5).reshape(b, h, nj, n_loc, d)

        k_r, v_r = gather(kg), gather(vg)
        row_off = rs - r + (NA_KH - 1) + jnp.arange(kh)
        bias = rpb_cols[:, row_off].transpose(0, 2, 3, 1, 4).reshape(h, nj, NA_KW, n_loc)
        s_loc = jnp.einsum('bhjqd,bhjkd->bhjqk', q_r, k_r).astype(jnp.float32) + bias.astype(jnp.float32)
        s_loc = jnp.where(valid, s_loc, NEG_INF)
        s_ctx = jnp.einsum('bhjqd,bhkd->bhjqk', q_r, kct).astype(jnp.float32)
        p = jax.nn.softmax(jnp.concatenate([s_loc, s_ctx], axis=-1), axis=-1).astype(v.dtype)
        o = (jnp.einsum('bhjqk,bhjkd->bhjqd', p[..., :n_loc], v_r)
             + jnp.einsum('bhjqk,bhkd->bhjqd', p[..., n_loc:], vct))
        return o.reshape(b, h, GRID_W, d)

    o = lax.map(row_block, jnp.arange(rows))
    return o.transpose(1, 0, 3, 2, 4).reshape(b, L, h * d)

def windowed_sink_attention(q, k, v, kc, vc, sink):
    b, L, hq, d = q.shape
    hk = k.shape[2]
    g = hq // hk
    lc = kc.shape[1]
    nb = L // SWA_BLOCK
    band = SWA_BLOCK + 2 * SWA_WINDOW
    qg = q.reshape(b, L, hk, g, d).transpose(0, 2, 3, 1, 4)
    pad = lambda t: jnp.pad(t.transpose(0, 2, 1, 3), ((0, 0), (0, 0), (SWA_WINDOW, SWA_WINDOW), (0, 0)))
    kp, vp = pad(k), pad(v)
    kct, vct = kc.transpose(0, 2, 1, 3), vc.transpose(0, 2, 1, 3)
    sink_col = jnp.broadcast_to(sink.astype(jnp.float32).reshape(hk, g, 1, 1), (b, hk, g, SWA_BLOCK, 1))
    qq = np.arange(SWA_BLOCK)[:, None]
    kk = np.arange(band)[None, :]
    in_window = np.abs(qq - (kk - SWA_WINDOW)) <= SWA_WINDOW

    def block(i):
        q_b = lax.dynamic_slice_in_dim(qg, i * SWA_BLOCK, SWA_BLOCK, axis=3)
        k_b = lax.dynamic_slice_in_dim(kp, i * SWA_BLOCK, band, axis=2)
        v_b = lax.dynamic_slice_in_dim(vp, i * SWA_BLOCK, band, axis=2)
        key_pos = i * SWA_BLOCK - SWA_WINDOW + jnp.arange(band)
        valid = in_window & (key_pos >= 0) & (key_pos < L)
        s = jnp.einsum('bkgqd,bkmd->bkgqm', q_b, k_b).astype(jnp.float32)
        s = jnp.where(valid, s, NEG_INF)
        s_ctx = jnp.einsum('bkgqd,bkmd->bkgqm', q_b, kct).astype(jnp.float32)
        p = jax.nn.softmax(jnp.concatenate([s, s_ctx, sink_col], axis=-1), axis=-1).astype(v.dtype)
        return (jnp.einsum('bkgqm,bkmd->bkgqd', p[..., :band], v_b)
                + jnp.einsum('bkgqm,bkmd->bkgqd', p[..., band:band + lc], vct))

    o = lax.map(block, jnp.arange(nb))
    return o.transpose(1, 0, 4, 2, 3, 5).reshape(b, L, hq * d)

def retention_na_mixer(hx, hc, w_in, w_out, ret_decay, ret_gn, na_rpb, cos, sin, need_ctx):
    cuts = [RET_W, 2 * RET_W, 3 * RET_W, 4 * RET_W, 4 * RET_W + NA_W, 4 * RET_W + 2 * NA_W]
    rq, rk, rv, rg, nq, nk, nv = jnp.split(hx @ w_in, cuts, axis=-1)
    crq, crk, crv, crg, cnq, cnk, cnv = jnp.split(hc @ w_in, cuts, axis=-1)
    scale = HEAD_DIM ** -0.5
    f32 = lambda t: t.transpose(0, 2, 1, 3).astype(jnp.float32)
    flip = lambda t: t[:, :, ::-1]
    log_gamma = jnp.log1p(-jnp.exp2(-ret_decay.astype(jnp.float32)))
    q = f32(apply_rope(split_heads(rq, RET_HEADS), cos, sin))
    k = f32(apply_rope(split_heads(rk, RET_HEADS), cos, sin)) * scale
    v = f32(split_heads(rv, RET_HEADS))
    cq = f32(split_heads(crq, RET_HEADS))
    ck = f32(split_heads(crk, RET_HEADS)) * scale
    cv = f32(split_heads(crv, RET_HEADS))
    zero = jnp.zeros((hx.shape[0], RET_HEADS, HEAD_DIM, HEAD_DIM), jnp.float32)
    c_f, st_f = retention_scan(cq, ck, cv, log_gamma[0], zero)
    c_b, st_b = retention_scan(flip(cq), flip(ck), flip(cv), log_gamma[1], zero)
    l_f, _ = retention_scan(q, k, v, log_gamma[0], st_f)
    l_b, _ = retention_scan(flip(q), flip(k), flip(v), log_gamma[1], st_b)
    ret_x = retention_readout(l_f + flip(l_b), rg, ret_gn)
    cnk_h, cnv_h = split_heads(cnk, NA_HEADS), split_heads(cnv, NA_HEADS)
    na_x = neighbourhood_attention(split_heads(nq, NA_HEADS) * scale, split_heads(nk, NA_HEADS),
                                   split_heads(nv, NA_HEADS), cnk_h, cnv_h, na_rpb)
    out_x = jnp.concatenate([ret_x, na_x], axis=-1) @ w_out
    out_c = None
    if need_ctx:
        ret_c = retention_readout(c_f + flip(c_b), crg, ret_gn)
        na_c = context_attention(split_heads(cnq, NA_HEADS) * scale, cnk_h, cnv_h)
        out_c = jnp.concatenate([ret_c, na_c], axis=-1) @ w_out
    return out_x, out_c

def swa_mixer(hx, hc, w_in, w_out, sink, cos, sin, need_ctx):
    cuts = [SWA_HEADS * HEAD_DIM, (SWA_HEADS + SWA_KV_HEADS) * HEAD_DIM]
    q, k, v = jnp.split(hx @ w_in, cuts, axis=-1)
    cq, ck, cv = jnp.split(hc @ w_in, cuts, axis=-1)
    scale = HEAD_DIM ** -0.5
    q = apply_rope(split_heads(q, SWA_HEADS), cos, sin) * scale
    k = apply_rope(split_heads(k, SWA_KV_HEADS), cos, sin)
    v = split_heads(v, SWA_KV_HEADS)
    ck, cv = split_heads(ck, SWA_KV_HEADS), split_heads(cv, SWA_KV_HEADS)
    out_x = windowed_sink_attention(q, k, v, ck, cv, sink) @ w_out
    out_c = None
    if need_ctx:
        out_c = context_attention(split_heads(cq, SWA_HEADS) * scale, ck, cv, sink) @ w_out
    return out_x, out_c

def grouped_expert_mlp(h, expert, weight, w_gu, w_down):
    n, d = h.shape
    a = expert.size
    e_flat = expert.reshape(-1)
    tok = jnp.arange(a, dtype=jnp.int32) // MOE_TOPK
    order = jnp.argsort(e_flat)
    e_sorted = e_flat[order]
    counts = jnp.bincount(e_flat, length=MOE_EXPERTS)
    padded = (counts + MOE_BLOCK - 1) // MOE_BLOCK * MOE_BLOCK
    ends = jnp.cumsum(padded)
    dest = (ends - padded)[e_sorted] + jnp.arange(a) - (jnp.cumsum(counts) - counts)[e_sorted]
    n_blocks = (a + MOE_EXPERTS * (MOE_BLOCK - 1) + MOE_BLOCK - 1) // MOE_BLOCK
    slot_tok = jnp.full((n_blocks * MOE_BLOCK,), n, jnp.int32).at[dest].set(tok[order])
    slot_w = jnp.zeros((n_blocks * MOE_BLOCK,), h.dtype).at[dest].set(weight.reshape(-1)[order])
    block_e = jnp.minimum(jnp.searchsorted(ends, jnp.arange(n_blocks) * MOE_BLOCK, side='right'), MOE_EXPERTS - 1)
    h_pad = jnp.concatenate([h, jnp.zeros((1, d), h.dtype)], axis=0)

    def expert_block(args):
        idx, e = args
        gate, up = jnp.split(h_pad[idx] @ w_gu[e], 2, axis=-1)
        return (jax.nn.silu(gate) * up) @ w_down[e]

    y = lax.map(expert_block, (slot_tok.reshape(n_blocks, MOE_BLOCK), block_e))
    y = y.reshape(-1, d) * slot_w[:, None]
    return jnp.zeros((n + 1, d), y.dtype).at[slot_tok].add(y)[:n]

def hierarchical_moe(h, wg, bg, we, be, w_gu, w_down):
    hf = h.astype(jnp.float32)
    pg = jax.nn.softmax(hf @ wg.astype(jnp.float32) + bg.astype(jnp.float32), axis=-1)
    gi = jnp.argmax(pg, axis=-1)
    gw = jnp.max(pg, axis=-1, keepdims=True)
    le = (hf @ we.astype(jnp.float32) + be.astype(jnp.float32)).reshape(-1, MOE_GROUPS, MOE_EPG)
    le = jnp.einsum('ng,nge->ne', jax.nn.one_hot(gi, MOE_GROUPS, dtype=jnp.float32), le)
    tw, ti = lax.top_k(jax.nn.softmax(le, axis=-1), MOE_TOPK)
    tw = tw / jnp.sum(tw, axis=-1, keepdims=True)
    weight = (gw * tw).astype(h.dtype)
    expert = gi[:, None].astype(jnp.int32) * MOE_EPG + ti
    return grouped_expert_mlp(h, expert, weight, w_gu, w_down)

def setup_inputs(seed: int = 0) -> dict:
    key = jax.random.key(seed)
    ks = jax.random.split(key, 22)
    d = D_MODEL
    n_even, n_odd = (DEPTH + 1) // 2, DEPTH // 2
    nrm = lambda k, shape, s: jax.random.normal(k, shape, jnp.float32) * s
    decay = RET_DECAY_BASE + jnp.arange(RET_HEADS, dtype=jnp.float32)
    return {
        'x': nrm(ks[0], (BATCH, SEQ, d), 1.0),
        'c': nrm(ks[1], (BATCH, d), 1.0),
        'ctx': nrm(ks[2], (BATCH, CTX_LEN, d), 1.0),
        'c_ctx': nrm(ks[3], (d,), 1.0),
        'ada_w': nrm(ks[4], (DEPTH, d, 6 * d), 0.5 * d ** -0.5),
        'ada_b': nrm(ks[5], (DEPTH, 6 * d), 0.02),
        'norm_g': 1.0 + nrm(ks[6], (DEPTH, 2, d), 0.02),
        'final_g': 1.0 + nrm(ks[7], (d,), 0.02),
        'ab_w_in': nrm(ks[8], (n_even, d, AB_IN), d ** -0.5),
        'ab_w_out': nrm(ks[9], (n_even, MIX_W, d), MIX_W ** -0.5),
        'ret_decay': decay + nrm(ks[10], (n_even, 2, RET_HEADS), 0.1),
        'ret_gn': 1.0 + nrm(ks[11], (n_even, RET_W), 0.02),
        'na_rpb': nrm(ks[12], (n_even, NA_HEADS, 2 * NA_KH - 1, 2 * NA_KW - 1), 0.1),
        'swa_w_in': nrm(ks[13], (n_odd, d, SWA_IN), d ** -0.5),
        'swa_w_out': nrm(ks[14], (n_odd, SWA_HEADS * HEAD_DIM, d), (SWA_HEADS * HEAD_DIM) ** -0.5),
        'swa_sink': nrm(ks[15], (n_odd, SWA_HEADS), 0.5),
        'router_g_w': nrm(ks[16], (DEPTH, d, MOE_GROUPS), d ** -0.5),
        'router_g_b': nrm(ks[17], (DEPTH, MOE_GROUPS), 0.01),
        'router_e_w': nrm(ks[18], (DEPTH, d, MOE_EXPERTS), d ** -0.5),
        'router_e_b': nrm(ks[19], (DEPTH, MOE_EXPERTS), 0.01),
        'expert_w_gu': nrm(ks[20], (DEPTH, MOE_EXPERTS, d, 2 * MOE_FF), d ** -0.5),
        'expert_w_down': nrm(ks[21], (DEPTH, MOE_EXPERTS, MOE_FF, d), MOE_FF ** -0.5),
    }

def reference(x, c, ctx, c_ctx, ada_w, ada_b, norm_g, final_g, ab_w_in, ab_w_out, ret_decay, ret_gn,
              na_rpb, swa_w_in, swa_w_out, swa_sink, router_g_w, router_g_b, router_e_w, router_e_b,
              expert_w_gu, expert_w_down):
    L = x.shape[1]
    cos, sin = axial_rope_tables(L)
    s_c = jax.nn.silu(c)
    s_cc = jax.nn.silu(c_ctx)
    xc = ctx
    for layer in range(DEPTH):
        last = layer == DEPTH - 1
        sh1, sc1, g1, sh2, sc2, g2 = jnp.split((s_c @ ada_w[layer] + ada_b[layer])[:, None, :], 6, axis=-1)
        csh1, csc1, cg1, csh2, csc2, cg2 = jnp.split((s_cc @ ada_w[layer] + ada_b[layer])[None, None, :], 6, axis=-1)
        hx = modulate(rms_norm(x, norm_g[layer, 0]), sh1, sc1)
        hc = modulate(rms_norm(xc, norm_g[layer, 0]), csh1, csc1)
        if layer % 2 == 0:
            j = layer // 2
            ox, oc = retention_na_mixer(hx, hc, ab_w_in[j], ab_w_out[j], ret_decay[j], ret_gn[j], na_rpb[j],
                                        cos, sin, not last)
        else:
            j = layer // 2
            ox, oc = swa_mixer(hx, hc, swa_w_in[j], swa_w_out[j], swa_sink[j], cos, sin, not last)
        x = x + g1 * ox
        hx = modulate(rms_norm(x, norm_g[layer, 1]), sh2, sc2).reshape(-1, D_MODEL)
        moe_w = (router_g_w[layer], router_g_b[layer], router_e_w[layer], router_e_b[layer],
                 expert_w_gu[layer], expert_w_down[layer])
        if last:
            x = x + g2 * hierarchical_moe(hx, *moe_w).reshape(x.shape)
        else:
            xc = xc + cg1 * oc
            hc = modulate(rms_norm(xc, norm_g[layer, 1]), csh2, csc2).reshape(-1, D_MODEL)
            y = hierarchical_moe(jnp.concatenate([hx, hc], axis=0), *moe_w)
            n_lat = hx.shape[0]
            x = x + g2 * y[:n_lat].reshape(x.shape)
            xc = xc + cg2 * y[n_lat:].reshape(xc.shape)
    return rms_norm(x, final_g)


_drawn_inputs = setup_inputs


def setup_inputs(seed=0):
    import zlib

    import numpy as np

    out = dict(_drawn_inputs(seed))
    spreads = {}
    factors = {'norm_g': 3.157,
     'final_g': 8.203,
     'ret_gn': 8.0,
     'na_rpb': 8.0,
     'swa_sink': 64.0,
     'router_g_b': 8.0,
     'router_e_b': 6.137}
    for name, (base, spread) in spreads.items():
        noise = np.random.default_rng([zlib.crc32(name.encode()), seed]).standard_normal(out[name].shape)
        drawn = base * np.exp(spread * noise) if base else spread * noise
        out[name] = __import__('jax').numpy.asarray(drawn.astype(out[name].dtype))
    for name, factor in factors.items():
        out[name] = (out[name] * factor).astype(out[name].dtype)
    return out
```

```python
from contextlib import ExitStack

import numpy as np

import concourse.bass as bass
from concourse import mybir

ALU = mybir.AluOpType
ACT = mybir.ActivationFunctionType
AXX = mybir.AxisListType.X
F32 = mybir.dt.float32
I32 = mybir.dt.int32

P = 128
D = 1024
KC = D // P
SEQ = 1024
CTX = 256
XT = SEQ // P
CT = CTX // P
NT = XT + CT
TOK = SEQ + CTX
GRID_W = 64
HD = 64
SCALE = HD ** -0.5
NEG = -1e30
NAH = 8
SWH = 16
EXP = 32
GRP = 4
FF = 512
TOPK = 2
OVF = 2 * TOK // P
BLK = EXP + OVF
NLOG = GRP + EXP
EPS = 1e-6
GN_EPS = 1e-5
STAGE = 99

C_ID, C_RF, C_RB, C_DI, C_TRI, C_ONE = 0, 128, 256, 384, 512, 640
C_COL = 768
C_ROW = C_COL + 64
C_PQ = C_ROW + 80
C_PK = C_PQ + 16
C_IO = C_PK + 16
C_IG = C_IO + 32
C_TOK = C_IG + 32
C_N = C_TOK + NT


def key_base(t):
    return min(max(t - 2, 0), XT - 5)


def tables():
    c = np.zeros((P, C_N), np.float32)
    p = np.arange(P)
    c[:, C_ID:C_ID + P] = np.eye(P)
    rel = p[None, :] - p[:, None]
    c[:, C_RF:C_RF + P] = np.maximum(rel, 0)
    c[:, C_RB:C_RB + P] = np.maximum(-rel, 0)
    c[:, C_DI:C_DI + P] = (1 + np.eye(P)) * SCALE
    c[:, C_TRI:C_TRI + P] = p[:, None] < p[None, :]
    c[:, C_ONE:C_ONE + P] = 1
    qc = p % GRID_W
    kc = np.arange(GRID_W)[None, :]
    win = np.clip(qc - 8, 0, GRID_W - 16)[:, None]
    c[:, C_COL:C_COL + 64] = np.where((kc >= win) & (kc < win + 16), 0, NEG)
    for t in range(XT):
        r = 2 * t + p // GRID_W
        rs = np.clip(r - 4, 0, 8)[:, None]
        kr = 2 * key_base(t) + np.arange(10)[None, :]
        c[:, C_ROW + 10 * t:C_ROW + 10 * t + 10] = np.where((kr >= rs) & (kr < rs + 8), 0, NEG)
    kk = np.arange(384)[None, :] - P
    band = np.zeros((P, 256 + 384 + 256), np.float32)
    band[:, 256:640] = np.where(np.abs(p[:, None] - kk) <= P, 0, NEG)
    for d in range(2):
        c[:, C_PQ + d:C_PQ + 16:2] = (p + 1 if d == 0 else P - p)[:, None]
        c[:, C_PK + d:C_PK + 16:2] = (P - 1 - p if d == 0 else p)[:, None]
    c[:, C_IO:C_IO + 32] = np.arange(32)
    c[:, C_IG:C_IG + 32] = np.arange(32) // 8
    c[:, C_TOK:C_TOK + NT] = np.arange(NT)[None, :] * P + p[:, None]
    inv = (np.float32(10000.0) ** (-np.arange(16, dtype=np.float32) / np.float32(16))).astype(np.float32)
    tok = np.arange(SEQ)
    ang = np.stack([(tok // GRID_W).astype(np.float32)[:, None] * inv,
                    (tok % GRID_W).astype(np.float32)[:, None] * inv], 1)
    cos, sin = np.cos(ang), np.sin(ang)
    rope = np.stack([np.stack([cos, cos], 2).reshape(SEQ, 64), np.stack([-sin, sin], 2).reshape(SEQ, 64)], 1)
    rope = rope.reshape(XT, P, P).transpose(1, 0, 2).reshape(P, XT * P)
    return c, band, np.ascontiguousarray(rope.astype(np.float32))


def program(nc, A, out):
    with ExitStack() as ctx:
        def sb(name, shape, dt=F32):
            return ctx.enter_context(nc.sbuf_tensor(name, shape, dt))

        def sem(name):
            return ctx.enter_context(nc.semaphore(name))

        def dram(name, shape, dt=F32):
            return nc.dram_tensor(name, shape, dt, kind="Internal").ap()

        SLOT0, ROWS, SLOT1, WR, TR, END = 10240, 20480, 23552, 35840, 44032, 51456
        ar = sb("ar", [P, END])
        cst = sb("cst", [P, C_N])
        colab = sb("colab", [P, 2, 2, 2, KC])
        dec = sb("dec", [P, 10, 16])
        ssq = sb("ssq", [P, 16])
        PS = ctx.enter_context(nc.psum_tensor("PS", [P, 8, 512], F32))

        def R(a, n):
            return ar[:, a:a + n]

        ident = cst[:, C_ID:C_ID + P]
        mod = dram("mod", (2, 2, 6 * D))
        h2d = dram("h2d", (TOK, D))
        yd = dram("yd", (BLK * P, D))
        slot_tok = [dram(f"slot_tok{l}", (P * BLK, 1), I32) for l in range(2)]
        rpbp = dram("rpbp", (NAH, 19, 127))
        skew = dram("skew", (GRID_W, NAH, 19, GRID_W))

        XR = R(0, NT * D).rearrange("p (t n) -> p t n", t=NT)
        hT = [R(0, KC * TOK).rearrange("p (k n) -> p k n", k=KC),
              R(SLOT0, KC * TOK).rearrange("p (k n) -> p k n", k=KC)]
        RG = R(10240, NT * 512).rearrange("p (t n) -> p t n", t=NT)
        NO = R(15360, NT * 512).rearrange("p (t n) -> p t n", t=NT)
        RV = NO
        QT = R(20480, 4 * TOK).rearrange("p (k n) -> p k n", k=4)
        KT = R(25600, 4 * TOK).rearrange("p (k n) -> p k n", k=4)
        ST = R(30720, NT * 512).rearrange("p (t n) -> p t n", t=NT)
        NV = ST
        QT1 = R(23552, 8 * SEQ).rearrange("p (k n) -> p k n", k=8)
        KT1 = R(31744, 2 * TOK).rearrange("p (k n) -> p k n", k=2)
        V1 = R(34304, NT * 256).rearrange("p (t n) -> p t n", t=NT)
        AO = R(10240, XT * D).rearrange("p (t n) -> p t n", t=XT)
        Wring = [[R(35840 + 4096 * i, 4096).rearrange("p (k n) -> p k n", k=KC) for i in range(2)],
                 [R(36864 + 4096 * i, 4096).rearrange("p (k n) -> p k n", k=KC) for i in range(2)]]
        COS = R(TR + 1024, 1024).rearrange("p (t f n) -> p t f n", t=XT, f=2)
        DM = R(TR, 1024)
        gain = R(TR + 6912, 512)
        xbuf = [R(TR + 2304 + 1024 * i, D) for i in range(3)]
        xn = [[R(TR + 5376 + 1024 * i, D) for i in range(2)], [R(ROWS + 1024 * i, D) for i in range(2)]]
        stage = [R(TR + 2304 + 512 * i, 512) for i in range(2)]
        rt1, rt2 = R(TR + 3328, 512), R(TR + 3840, 512)
        v2 = [R(TR + 4352 + 1024 * i, 1024) for i in range(2)]
        sm = [R(TR + 2304 + 1024 * i, 1024) for i in range(2)]
        txb = R(TR + 4352, 1024)
        ob, cb, sqb = R(TR + 5376, 512), R(TR + 5888, 512), R(TR + 6400, 512)
        run = [[sm[d][:, 256 * i:256 * i + 256] for i in range(2)] for d in range(2)]
        runt = [sm[d][:, 512:768] for d in range(2)]
        TOEP = R(0, NAH * 18 * 64).rearrange("p (h j c) -> p h j c", h=NAH, j=18)
        biasb = [R(36864 + 896 * i, 896) for i in range(3)]
        sxb = [R(39552 + 896 * i, 896) for i in range(3)]
        ptb = [R(42240 + 896 * i, 896) for i in range(2)]
        atts = R(44032, 256)
        BAND = R(TR + 2304, 896)
        WO = R(WR, KC * D).rearrange("p (k n) -> p k n", k=KC)
        rows = R(ROWS, 3 * D).rearrange("p (j n) -> p j n", j=3)
        tmpb = [R(TR + 512 * i, 512) for i in range(2)]
        rw = R(TR + 1024, KC * NLOG).rearrange("p (k n) -> p k n", k=KC)
        rb = R(TR + 1312, NLOG)
        LG = R(TR + 1348, NT * NLOG).rearrange("p (t n) -> p t n", t=NT)
        junk = R(TR + 1708, D)
        PERS = TR + 2732
        wgt = R(PERS, 2 * NT).rearrange("p (j t) -> p j t", j=2)
        dsti = R(PERS + 20, 2 * NT).bitcast(I32).rearrange("p (j t) -> p j t", j=2)
        posi = R(PERS + 40, 2 * NT).bitcast(I32).rearrange("p (j t) -> p j t", j=2)
        toki = R(PERS + 60, NT).bitcast(I32)
        idx = R(PERS + 70, BLK).bitcast(I32)
        idxc = [R(PERS + 122 + i, 1).bitcast(I32) for i in range(2)]
        ctl = R(PERS + 124, 1 + OVF).bitcast(I32)
        mixT = [R(TR + 3072 + 1024 * i, D).rearrange("p (k n) -> p k n", k=KC) for i in range(2)]
        h2 = R(TR + 5120, D)
        h2T = R(TR + 6144, D).rearrange("p (k n) -> p k n", k=KC)
        slot = [SLOT0, SLOT1]
        wgu = [R(s, KC * D).rearrange("p (k n) -> p k n", k=KC) for s in slot]
        wdn = [R(s + KC * D, 4 * D).rearrange("p (k n) -> p k n", k=4) for s in slot]
        hb = [R(WR + 1024 * i, D) for i in range(2)]
        hbT = [R(WR + 2048 + 1024 * i, D).rearrange("p (k n) -> p k n", k=KC) for i in range(2)]
        sg = [R(WR + 4096 + 512 * i, 512) for i in range(2)]
        gub = [R(WR + 5120 + 512 * i, 512) for i in range(2)]
        guT = [R(TR + 3072 + 512 * i, 512).rearrange("p (k n) -> p k n", k=4) for i in range(2)]
        yb = [R(WR + 6144 + 1024 * i, D) for i in range(2)]
        yg = [[R(SLOT0 + 2048 * i + 1024 * j, D) for j in range(2)] for i in range(3)]
        g2row = R(ROWS, 2 * D).rearrange("p (s n) -> p s n", s=2)
        cmb = R(SLOT1, D)
        fgrow = R(SLOT1 + 1024, D)
        outb = [R(SLOT1 + 2048 + 1024 * i, D) for i in range(2)]

        names = {}

        shared = {}

        def share(names_, before, after, total):
            for x in names_:
                shared[x.format(after)] = (x.format(before), total)

        def S(name):
            if name in shared:
                return S(shared[name][0])
            if name not in names:
                names[name] = sem(name)
            return names[name]

        def done(name, count):
            at = name
            while at in shared:
                at, more = shared[at]
                count = count + more
            return S(name), count

        share(("ss{}", "n1_ms{}", "n1_rt{}", "n1_tr{}", "n1_ea{}", "n1_ed{}", "xn{}"), 0, 1, NT)
        share(("{}_s", "{}_bs", "{}_m", "{}_e", "{}_t", "{}_pt", "{}_v"), "na", "sw", NT * NAH)
        share(("{}_o",), "na", "sw", NT)
        share(("{}_mt", "{}_me", "{}_h2", "{}_ht", "{}_he", "{}_r", "{}_lg", "{}_x", "{}_ss", "{}_ms", "{}_rt"), "o0", "o1", NT)
        share(("{}_mm", "{}_pe"), "o0", "o1", 2 * NT)
        share(("{}_rows",), "o0", "o1", 32)
        share(("{}_w",), "o0", "o1", 80)
        share(("{}_h2o",), "o0", "o1", 16 * NT)
        share(("{}_ctl", "{}_c", "{}_mm", "{}_g", "{}_x", "{}_pos"), "r0", "r1", 1)
        share(("{}_e",), "r0", "r1", 2)
        share(("{}_st",), "r0", "r1", 16 * 2 * NT)
        share(("{}_idx",), "r0", "r1", 16)
        share(("{}_wg1", "{}_wd1", "{}_hb1", "{}_yo1"), "m0", "m1", 8 * EXP)
        share(("{}_g",), "c0", "c1", 32)
        share(("{}_used",), "c0", "c1", NT)
        for q in range(3):
            share((f"{{}}_y{q}",), "c0", "c1", 32 * len(range(q, NT, 3)))

        chains = {}

        class Chain:

            def __init__(self, eng, name):
                self.eng, self.sem, self.n = eng, S(name), 0

            def __call__(self, ins):
                self.n += 1
                ins.then_inc(self.sem, 1)
                self.eng.wait_ge(self.sem, self.n)

        def chain(eng):
            key = str(eng.engine)
            if key not in chains:
                chains[key] = Chain(eng, "chain_" + key.split(".")[-1])
            return chains[key]

        def bcast_mid(ap, n):
            return ap.unsqueeze(1).to_broadcast([ap.shape[0], n, ap.shape[1]])

        def bcast_in(ap, n):
            return ap.unsqueeze(len(ap.shape)).to_broadcast(list(ap.shape) + [n])

        def meet(eng, k):
            eng.drain().then_inc(S("phase"), 1)
            eng.wait_ge(*done("phase", 4 * k))

        def after_meet(eng, k):
            eng.wait_ge(*done("phase", 4 * k))

        M_ADA, M_N1, M_PROJ, M_CORE, M_PROJB, M_ATT, M_OUT, M_ROUTE, M_MOE, M_CMB = range(1, 11)
        M2 = {0: 0, 1: 8}

        NADA = 24
        adaw = [R(10240 + 4096 * i, 4096).rearrange("p (k n) -> p k n", k=KC) for i in range(3)]
        modrow = [ar[0:2, 22528 + 6144 * l:22528 + 6144 * (l + 1)] for l in range(2)]
        ngrow = ar[0:2, 0:4 * D].rearrange("p (l j n) -> p l j n", l=2, j=2)
        cin = R(4096, 16).rearrange("p (s k) -> p s k", s=2)
        sT = R(4112, 16).rearrange("p (k s) -> p k s", k=KC)
        zero = R(4352, 2560)

        def ada_sp(sp):
            sp.dma_start(cst[:, :], A["cst"]).then_inc(S("consts"), 16)
            sp.dma_start(cin[:, 0, :], A["c"][0].rearrange("(p k) -> p k", k=KC)).then_inc(S("consts"), 16)
            sp.dma_start(cin[:, 1, :], A["c_ctx"].rearrange("(p k) -> p k", k=KC)).then_inc(S("consts"), 16)
            sp.dma_start(dec[:, 0, :].rearrange("p (d h) -> p d h", d=2),
                         A["ret_decay"][0].partition_broadcast(P)).then_inc(S("consts"), 16)
            sp.dma_start(ngrow, A["norm_g"].partition_broadcast(2)).then_inc(S("consts"), 16)
            for l in range(2):
                sp.dma_start(modrow[l], A["ada_b"][l].partition_broadcast(2)).then_inc(S("consts"), 16)
            for n in range(NADA):
                l, c = divmod(n, 12)
                if n >= 3:
                    sp.wait_ge(*done("ada_mm", n - 2))
                sp.dma_start(adaw[n % 3], A["ada_w"][l].rearrange("(p k) n -> p k n", k=KC)[:, :, c * 512:c * 512 + 512])\
                    .then_inc(S(f"ada_in{n % 3}"), 16)
            sp.wait_ge(*done("zeroed", 1))
            sp.dma_start(rpbp.rearrange("h a b -> h (a b)"), zero[0:NAH, 0:19 * 127]).then_inc(S("zeros_out"), 16)
            for l in range(2):
                sp.dma_start(slot_tok[l].rearrange("(p b) o -> p (b o)", b=BLK), zero[:, 0:BLK].bitcast(I32))\
                    .then_inc(S("zeros_out"), 16)
            sp.dma_start(yd[EXP * P:BLK * P, :].rearrange("(b p) n -> p b n", p=P),
                         zero[:, 0:D].unsqueeze(1).to_broadcast([P, OVF, D])).then_inc(S("zeros_out"), 16)
            sp.wait_ge(*done("zeros_out", 64))
            sp.dma_start(rpbp[:, 2:17, 48:79], A["na_rpb"][0]).then_inc(S("rpb_out"), 16)
            sp.wait_ge(*done("rpb_out", 16))
            for h in range(NAH):
                src = bass.AP(tensor=rpbp.tensor, offset=h * 19 * 127 + 63, ap=[[127, 19], [-1, GRID_W], [1, GRID_W]])
                sp.dma_start(skew[:, h].rearrange("q j k -> j q k"), src).then_inc(S("skew_out"), 16)
            for l in range(2):
                sp.wait_ge(*done("mod_rows", 4 * (l + 1)))
                sp.dma_start(mod[l], modrow[l]).then_inc(S("mod_out"), 16)
            sp.wait_ge(*done("mod_out", 32))
            for l in range(2):
                for s in range(2):
                    sp.dma_start(colab[:, l, s], mod[l, s, 0:2 * D].rearrange("(j p k) -> p j k", j=2, k=KC))\
                        .then_inc(S("cols_in"), 16)

        def ada_act(act):
            act.wait_ge(*done("consts", 16 * 7))
            nc.scalar.activation(sT.rearrange("p k s -> p s k"), cin, ACT.Silu).then_inc(S("silu_c"), 1)
            ch = chain(act)
            E, U, LN, LGM = dec[:, 1], dec[:, 2], dec[:, 3], dec[:, 5]
            ch(nc.scalar.activation(E.rearrange("p (q r d) -> p q r d", q=2, r=4), dec[:, 0].rearrange("p (d r q) -> p q r d", d=2, r=4), ACT.Exp,
                                    scale=-float(np.log(2.0))))
            ch(nc.scalar.activation(U, E, ACT.Copy, scale=-1.0, bias=1.0))
            nc.scalar.activation(LN, U, ACT.Ln).then_inc(S("dec_ln"), 1)
            act.wait_ge(*done("dec_pos", 1))
            for j in (6, 7, 8):
                nc.scalar.activation(dec[:, j], dec[:, j], ACT.Exp)
            nc.scalar.activation(DM, DM, ACT.Exp).then_inc(S("dec_exp"), 1)

        def ada_pe(pe):
            pe.wait_ge(*done("silu_c", 1))
            for n in range(NADA):
                pe.wait_ge(*done(f"ada_in{n % 3}", 16 * (n // 3 + 1)))
                if n >= 2:
                    pe.wait_ge(*done("ada_ev", n - 1))
                for k in range(KC):
                    mm = nc.tensor.matmul(PS[0:2, n % 2, :], sT[:, k, :], adaw[n % 3][:, k, :],
                                          start=(k == 0), stop=(k == KC - 1))
                mm.then_inc(S("ada_mm"), 1)

        def ada_dve(dve):
            dve.wait_ge(*done("consts", 16 * 7))
            nc.vector.memset(zero, 0.0).then_inc(S("zeroed"), 1)
            ch = chain(dve)
            dve.wait_ge(*done("dec_ln", 1))
            E, U, LN, T, LGM = dec[:, 1], dec[:, 2], dec[:, 3], dec[:, 4], dec[:, 5]
            ch(nc.vector.tensor_scalar(T, U, -1.0, 1.0, ALU.mult, ALU.add))
            ch(nc.vector.tensor_scalar(dec[:, 9], T, 0.0, None, ALU.is_equal))
            ch(nc.vector.tensor_tensor(T, T, dec[:, 9], ALU.add))
            ch(nc.vector.reciprocal(T, T))
            ch(nc.vector.tensor_tensor(LN, LN, T, ALU.mult))
            ch(nc.vector.tensor_tensor(LN, LN, dec[:, 9], ALU.subtract))
            ch(nc.vector.tensor_tensor(LGM, LN, E, ALU.mult))
            nc.vector.tensor_tensor(dec[:, 6], LGM, cst[:, C_PQ:C_PQ + 16], ALU.mult)
            nc.vector.tensor_tensor(dec[:, 7], LGM, cst[:, C_PK:C_PK + 16], ALU.mult)
            nc.vector.tensor_scalar(dec[:, 8], LGM, float(P), None, ALU.mult)
            for h in range(8):
                last = nc.vector.tensor_scalar(DM[:, h * P:h * P + P], cst[:, C_RF:C_RF + P], LGM[:, 2 * h:2 * h + 1], None, ALU.mult)
            ch(last)
            for h in range(8):
                d = DM[:, h * P:h * P + P]
                last = nc.vector.scalar_tensor_tensor(out=d, in0=cst[:, C_RB:C_RB + P], scalar=LGM[:, 2 * h + 1:2 * h + 2],
                                                      in1=d, op0=ALU.mult, op1=ALU.add)
            last.then_inc(S("dec_pos"), 1)
            dve.wait_ge(*done("dec_exp", 1))
            DV = DM.rearrange("p (h n) -> p h n", h=8)
            ch(nc.vector.tensor_tensor(DV, DV, bcast_mid(cst[:, C_DI:C_DI + P], 8), ALU.mult))
            nc.vector.tensor_scalar(dec[:, 7], dec[:, 7], SCALE, None, ALU.mult)
            for q in range(2):
                half = slice(64 * q, 64 * q + 64)
                last = nc.vector.tensor_copy(dec[half, 9, 0:8].rearrange("p (r d) -> p r d", d=2),
                                             dec[half, 8, 8 * q:8 * q + 8].rearrange("p (r d) -> p r d", d=2))
            ch(last)
            for n in range(NADA):
                l, c = divmod(n, 12)
                dve.wait_ge(*done("ada_mm", n + 1))
                m = modrow[l][:, c * 512:c * 512 + 512]
                nc.vector.tensor_tensor(m, PS[0:2, n % 2, :], m, ALU.add).then_inc(S("ada_ev"), 1)
                if c == 11:
                    dve.wait_ge(*done("ada_ev", n + 1))
                    for j in range(2):
                        m = modrow[l][:, (3 * j + 1) * D:(3 * j + 2) * D]
                        nc.vector.scalar_tensor_tensor(out=m, in0=m, scalar=1.0, in1=ngrow[:, l, j, :],
                                                       op0=ALU.add, op1=ALU.mult).then_inc(S("mod_rows"), 2)

        def n1_tiles(l):
            return list(range(NT))

        def n1_sp(sp, l):
            if l == 0:
                sp.dma_start(COS, A["rope"].rearrange("p (t f n) -> p t f n", t=XT, f=2)).then_inc(S("cos_in0"), 16)
                for t in range(NT):
                    if t >= 3:
                        sp.wait_ge(*done("xn0", t - 2))
                    src = A["x"][0, t * P:t * P + P] if t < XT else A["ctx"][0, (t - XT) * P:(t - XT + 1) * P]
                    sp.dma_start(xbuf[t % 3], src).then_inc(S(f"x_in{t % 3}"), 16)

        def n1_src(l, t):
            return xbuf[t % 3] if l == 0 else XR[:, t, :]

        def n1_act(act, l):
            def squares(t):
                if l == 0:
                    act.wait_ge(*done(f"x_in{t % 3}", 16 * (t // 3 + 1)))
                nc.scalar.activation(PS[:, 4:6, :].rearrange("p b n -> p (b n)"), n1_src(l, t), ACT.Square,
                                     accum_out=ssq[:, t:t + 1]).then_inc(S(f"ss{l}"), 1)

            def root(t):
                act.wait_ge(*done(f"n1_ms{l}", t + 1))
                nc.scalar.activation(ssq[:, t:t + 1], ssq[:, t:t + 1], ACT.Sqrt).then_inc(S(f"n1_rt{l}"), 1)

            def evict(t):
                act.wait_ge(*done(f"n1_tr{l}", t + 1))
                s = 0 if t < XT else 1
                for k in range(KC // 2):
                    last = nc.scalar.activation(hT[l][:, k, t * P:t * P + P], PS[:, 2 * (t % 2) + k // 4, (k % 4) * P:(k % 4 + 1) * P],
                                                ACT.Identity, bias=colab[:, l, s, 0, k:k + 1], scale=colab[:, l, s, 1, k:k + 1])
                last.then_inc(S(f"n1_ea{l}"), 1)
            act.wait_ge(*done("cols_in", 64))
            for i in range(NT + 1):
                if i < NT:
                    squares(i)
                    root(i)
                if i >= 1:
                    evict(i - 1)

        def n1_dve(dve, l):
            ch = chain(dve)

            def norm(t):
                r = ssq[:, t:t + 1]
                dve.wait_ge(*done(f"ss{l}", t + 1))
                nc.vector.tensor_scalar(r, r, 1.0 / D, EPS, ALU.mult, ALU.add).then_inc(S(f"n1_ms{l}"), 1)
                dve.wait_ge(*done(f"n1_rt{l}", t + 1))
                ch(nc.vector.reciprocal(r, r))
                if t >= 2:
                    dve.wait_ge(*done(f"n1_tr{l}", t - 1))
                nc.vector.tensor_scalar(xn[l][t % 2], n1_src(l, t), r, None, ALU.mult).then_inc(S(f"xn{l}"), 1)

            def evict(t):
                dve.wait_ge(*done(f"n1_tr{l}", t + 1))
                s = 0 if t < XT else 1
                for k in range(KC // 2, KC):
                    last = nc.vector.tensor_scalar(hT[l][:, k, t * P:t * P + P], PS[:, 2 * (t % 2) + k // 4, (k % 4) * P:(k % 4 + 1) * P],
                                                   colab[:, l, s, 1, k:k + 1], colab[:, l, s, 0, k:k + 1], ALU.mult, ALU.add)
                last.then_inc(S(f"n1_ed{l}"), 1)
            dve.wait_ge(*done("cols_in", 64))
            for i in range(NT + 1):
                if i < NT:
                    norm(i)
                if i >= 1:
                    evict(i - 1)

        def n1_pe(pe, l):
            for t in range(NT):
                pe.wait_ge(*done(f"xn{l}", t + 1))
                if t >= 2:
                    pe.wait_ge(*done(f"n1_ea{l}", t - 1))
                    pe.wait_ge(*done(f"n1_ed{l}", t - 1))
                xv = xn[l][t % 2].rearrange("p (m k) -> p k m", k=KC)
                for k in range(KC):
                    tr = nc.tensor.transpose(PS[:, 2 * (t % 2) + k // 4, (k % 4) * P:(k % 4 + 1) * P], xv[:, k, :], ident)
                tr.then_inc(S(f"n1_tr{l}"), 1)

        class Proj:
            def __init__(self, name, w, wring, kinds, l, before):
                self.before = before
                self.name, self.w, self.ring, self.l = name, w, wring, l
                self.units, self.kinds = [], kinds
                n_act = n_dve = n_t = 0
                for c, (kind, col) in enumerate(kinds):
                    for t in range(XT if kind in ("q0", "q1") else NT):
                        rope = kind in ("rk", "rq", "q0", "q1", "kv") and t < XT
                        by_dve = rope or kind == "kv"
                        turned = kind not in ("rv", "rg", "nv")
                        u = dict(c=c, kind=kind, t=t, rope=rope, by_dve=by_dve, turned=turned, j=n_t)
                        if by_dve:
                            n_dve += 1
                            u["ev"] = (f"{name}_ed", n_dve)
                        else:
                            n_act += 1
                            u["ev"] = (f"{name}_ea", n_act)
                        n_t += turned
                        self.units.append(u)

            def loaded(self, c):
                return 16 * (self.before[c % 2] + c // 2 + 1)

            def last_of(self, c):
                return max(i for i, u in enumerate(self.units) if u["c"] == c)

        pa = Proj("pa", A["ab_w_in"][0], Wring[0], [("rv", 1024), ("rk", 512), ("rq", 0), ("rg", 1536)], 0, (0, 0))
        pb = Proj("pb", A["ab_w_in"][0], Wring[0], [("nk", 2560), ("nv", 3072), ("nq", 2048)], 0, (2, 2))
        pc = Proj("pc", A["swa_w_in"][0], Wring[1], [("q0", 0), ("q1", 512), ("kv", 1024)], 1, (4, 3))

        for before, after in ((pa, pb), (pb, pc)):
            a, b = before.name, after.name
            share(("{}_mm",), a, b, len(before.units))
            share(("{}_tr", "{}_te"), a, b, sum(u["turned"] for u in before.units))
            share(("{}_ed",), a, b, sum(u["by_dve"] for u in before.units))
            share(("{}_ea",), a, b, sum(not u["by_dve"] for u in before.units))

        def proj_sp(sp, pr):
            for c, (kind, col) in enumerate(pr.kinds):
                if c >= 2:
                    sp.wait_ge(*done(f"{pr.name}_mm", pr.last_of(c - 2) + 1))
                sp.dma_start(pr.ring[c % 2], pr.w.rearrange("(p k) n -> p k n", k=KC)[:, :, col:col + 512])\
                    .then_inc(S(f"w_in{c % 2}"), 16)

        def proj_pe(pe, pr):
            n = pr.name

            def turn(u):
                sname, cnt = u["ev"]
                pe.wait_ge(*done(sname, cnt))
                if u["j"] >= 2:
                    pe.wait_ge(*done(f"{n}_te", u["j"] - 1))
                st = stage[u["j"] % 2]
                for r in range(2 if u["kind"] == "kv" else 4):
                    tr = nc.tensor.transpose(PS[:, 6 + u["j"] % 2, r * P:r * P + P], st[:, r * P:r * P + P], ident)
                if u["kind"] == "rk":
                    tr.then_inc(S(f"{n}_tr"), 1)
                    t = u["t"]
                    pe.wait_ge(*done("v2", t + 1))
                    if t >= 2:
                        pe.wait_ge(*done("kv_ev", t - 1))
                    for h in range(8):
                        q = 64 * (h % 2)
                        mm = nc.tensor.matmul(PS[q:q + 64, t % 2, (h // 2) * P:(h // 2 + 1) * P], st[:, h * 64:h * 64 + 64],
                                              v2[t % 2][:, 64 * 8 * (h % 2) + (h // 2) * P:][:, 0:P], start=True, stop=True)
                    mm.then_inc(S("kv_mm"), 1)
                else:
                    tr.then_inc(S(f"{n}_tr"), 1)

            for i, u in enumerate(pr.units):
                if u["t"] == 0:
                    pe.wait_ge(*done(f"w_in{u['c'] % 2}", pr.loaded(u["c"])))
                if i >= 2:
                    pe.wait_ge(*done(pr.units[i - 2]["ev"][0], pr.units[i - 2]["ev"][1]))
                for k in range(KC):
                    mm = nc.tensor.matmul(PS[:, 4 + i % 2, :], hT[pr.l][:, k, u["t"] * P:u["t"] * P + P],
                                          pr.ring[u["c"] % 2][:, k, :], start=(k == 0), stop=(k == KC - 1))
                mm.then_inc(S(f"{n}_mm"), 1)
                if i and pr.units[i - 1]["turned"]:
                    turn(pr.units[i - 1])
            if pr.units[-1]["turned"]:
                turn(pr.units[-1])

        def stage_free(eng, n, j, kind_before):
            if j >= 2:
                eng.wait_ge(*done(f"{n}_tr", j - 1))
            if kind_before is not None:
                eng.wait_ge(*done("kv_mm", kind_before))

        def kv_before(pr, i):
            j, seen = pr.units[i]["j"], 0
            for u in pr.units[:i]:
                if u["turned"] and u["j"] <= j - 2 and u["kind"] == "rk":
                    seen = u["t"] + 1
            return seen or None

        def proj_act(act, pr):
            n = pr.name

            def evict(i, u):
                act.wait_ge(*done(f"{n}_mm", i + 1))
                src, t = PS[:, 4 + i % 2, :], u["t"]
                if u["turned"]:
                    stage_free(act, n, u["j"], kv_before(pr, i))
                    ins = nc.scalar.activation(stage[u["j"] % 2], src, ACT.Copy)
                elif u["kind"] == "rg":
                    ins = nc.scalar.activation(RG[:, t, :], src, ACT.Silu)
                else:
                    ins = nc.scalar.activation((RV if u["kind"] == "rv" else NV)[:, t, :], src, ACT.Copy)
                ins.then_inc(S(f"{n}_ea"), 1)

            def evict_turned(u):
                act.wait_ge(*done(f"{n}_tr", u["j"] + 1))
                t, src = u["t"], PS[:, 6 + u["j"] % 2, :]
                cols = slice(t * P, t * P + P)
                k = u["kind"]
                if k == "kv":
                    dst, src = KT1[:, :, cols], src[:, 0:256].rearrange("p (r n) -> p r n", r=2)
                else:
                    dst = QT1[:, 4 * (k == "q1"):4 * (k == "q1") + 4, cols] if k[0] == "q" else \
                        (KT if k[1] == "k" else QT)[:, :, cols]
                    src = src.rearrange("p (r n) -> p r n", r=4)
                nc.scalar.activation(dst, src, ACT.Copy).then_inc(S(f"{n}_te"), 1)
                if k == "rk":
                    act.wait_ge(*done("kv_mm", t + 1))
                    nc.scalar.activation(ST[:, t, :], PS[:, t % 2, :], ACT.Copy).then_inc(S("kv_ev"), 1)

            for i, u in enumerate(pr.units):
                if not u["by_dve"]:
                    evict(i, u)
                if i and pr.units[i - 1]["turned"]:
                    evict_turned(pr.units[i - 1])
            if pr.units[-1]["turned"]:
                evict_turned(pr.units[-1])

        def proj_dve(dve, pr):
            n = pr.name
            ch = chain(dve)
            for i, u in enumerate(pr.units):
                if not u["by_dve"]:
                    continue
                dve.wait_ge(*done(f"{n}_mm", i + 1))
                nh = 4 if u["kind"] == "kv" else 8
                src = PS[:, 4 + i % 2, :]
                st = stage[u["j"] % 2]
                if u["kind"] == "kv":
                    ins = nc.vector.tensor_copy(V1[:, u["t"], :], src[:, 256:512])
                if u["rope"]:
                    w = nh * 64
                    c, s = COS[:, u["t"], 0, :], COS[:, u["t"], 1, :]
                    sv = src[:, 0:w].rearrange("p (h a f i) -> p h a f i", h=nh, a=2, f=2)
                    tv = rt2[:, 0:w].rearrange("p (h a f i) -> p h a f i", h=nh, a=2, f=2)
                    s4 = s.rearrange("p (a f i) -> p a f i", a=2, f=2)
                    nc.vector.tensor_tensor(rt1[:, 0:w].rearrange("p (h n) -> p h n", h=nh), src[:, 0:w].rearrange("p (h n) -> p h n", h=nh),
                                            bcast_mid(c, nh), ALU.mult)
                    for f in range(2):
                        last = nc.vector.tensor_tensor(tv[:, :, :, f, :], sv[:, :, :, 1 - f, :],
                                                       s4[:, :, f, :].unsqueeze(1).to_broadcast([P, nh, 2, 16]), ALU.mult)
                    ch(last)
                    stage_free(dve, n, u["j"], kv_before(pr, i))
                    if u["kind"] == "kv":
                        ins = nc.vector.tensor_tensor(st[:, 0:w], rt1[:, 0:w], rt2[:, 0:w], ALU.add)
                    elif u["kind"] in ("q0", "q1"):
                        by = lambda a: a.rearrange("p (j g d) -> p j g d", j=2, g=4)
                        ins = nc.vector.tensor_tensor(st.rearrange("p (g j d) -> p j g d", g=4, j=2), by(rt1), by(rt2), ALU.add)
                    else:
                        ins = nc.vector.tensor_tensor(st, rt1, rt2, ALU.add)
                else:
                    stage_free(dve, n, u["j"], kv_before(pr, i))
                    ins = nc.vector.tensor_copy(st[:, 0:256], src[:, 0:256])
                ins.then_inc(S(f"{n}_ed"), 1)
                if u["rope"]:
                    dve.wait_ge(*done(f"{n}_ed", u["ev"][1]))

        def proj_pool(pool):
            first_k = 0
            for t in range(NT):
                pool.wait_ge(*done("pa_ea", t + 1))
                if t >= 2:
                    pool.wait_ge(*done("kv_mm", t - 1))
                for q in range(2):
                    kd = dec[:, 7, 8 * q:8 * q + 8].rearrange("p (r d) -> p r d", d=2)
                    vv = RV[:, t, :].rearrange("p (r q e) -> p r q e", r=4, q=2)[:, :, q, :]
                    last = nc.gpsimd.tensor_tensor(v2[t % 2][:, 512 * q:512 * q + 512].rearrange("p (r d e) -> p r d e", r=4, d=2),
                                                   vv.unsqueeze(2).to_broadcast([P, 4, 2, 64]), bcast_in(kd, 64), ALU.mult)
                last.then_inc(S("v2"), 1)

        def scan(eng, ne, d):
            ch = chain(eng)
            seq = [8, 9] + list(range(XT)) if d == 0 else [9, 8] + list(range(XT - 1, -1, -1))
            cd = dec[:, 9, 0:8].rearrange("p (r d) -> p r d", d=2)[:, :, d]
            ch(ne.memset(run[d][0], 0.0))
            for i, t in enumerate(seq):
                old, new = run[d][i % 2].rearrange("p (r e) -> p r e", r=4), run[d][1 - i % 2].rearrange("p (r e) -> p r e", r=4)
                st = ST[:, t, :].rearrange("p (r d e) -> p r d e", r=4, d=2)[:, :, d, :]
                tmp = runt[d].rearrange("p (r e) -> p r e", r=4)
                if i < NT - 1:
                    ch(ne.tensor_tensor(tmp, old, bcast_in(cd, 64), ALU.mult))
                    ch(ne.tensor_tensor(new, tmp, st, ALU.add))
                ch(ne.tensor_copy(st, old))
            eng.drain().then_inc(S("states"), 1)

        def core_pe(pe):
            def scores(t):
                if t >= 1:
                    pe.wait_ge(*done("sm", t))
                for h in range(8):
                    q, r = 64 * (h % 2), h // 2
                    mm = nc.tensor.matmul(PS[:, h % 2, r * P:r * P + P], KT[q:q + 64, r, t * P:t * P + P],
                                          QT[q:q + 64, r, t * P:t * P + P], start=True, stop=True)
                mm.then_inc(S("core_s"), 1)

            def cross(t):
                if t == 0:
                    pe.wait_ge(*done("states", 2))
                if t >= 1:
                    pe.wait_ge(*done("tx", t))
                for h in range(8):
                    q, r = 64 * (h % 2), h // 2
                    mm = nc.tensor.matmul(PS[:, 2 + h % 2, r * P:r * P + P], QT[q:q + 64, r, t * P:t * P + P],
                                          ST[q:q + 64, t, r * P:r * P + P], start=True, stop=True)
                mm.then_inc(S("core_x"), 1)

            def inner(t):
                pe.wait_ge(*done("sm", t + 1))
                if t >= 2:
                    pe.wait_ge(*done("core_o1", t - 1))
                for h in range(8):
                    mm = nc.tensor.matmul(PS[:, 4 + t % 2, h * 64:h * 64 + 64], sm[t % 2][:, (h % 2) * 512 + (h // 2) * P:][:, 0:P],
                                          RV[:, t, h * 64:h * 64 + 64], start=True, stop=True)
                mm.then_inc(S("core_o"), 1)
            pe.wait_ge(*done("states", 2))
            for i in range(NT + 1):
                if i < NT:
                    scores(i)
                    cross(i)
                if i >= 1:
                    inner(i - 1)

        def core_dve(dve):
            ch = chain(dve)
            mu, var = ssq[:, 0:8], ssq[:, 8:16]
            H = lambda a: a.rearrange("p (h e) -> p h e", h=8)
            dve.wait_ge(*done("states", 2))

            def decay(t):
                dve.wait_ge(*done("core_s", t + 1))
                if t >= 2:
                    dve.wait_ge(*done("core_o", t - 1))
                nc.vector.tensor_tensor(sm[t % 2], PS[:, 0:2, :].rearrange("p b n -> p (b n)"), DM, ALU.mult).then_inc(S("sm"), 1)
            decay(0)
            for t in range(NT):
                if t + 1 < NT:
                    decay(t + 1)
                dve.wait_ge(*done("core_x", t + 1))
                nc.vector.tensor_tensor(txb.rearrange("p (h e) -> p h e", e=64),
                                        PS[:, 2:4, :].rearrange("p b (h e) -> p (b h) e", e=64),
                                        bcast_in(dec[:, 6], 64), ALU.mult).then_inc(S("tx"), 1)
                dve.wait_ge(*done("tx", t + 1))
                dve.wait_ge(*done("core_o", t + 1))
                tx4 = txb.rearrange("p (q r d e) -> p r q d e", q=2, r=4, d=2)
                ob4 = ob.rearrange("p (r q e) -> p r q e", r=4, q=2)
                nc.vector.tensor_tensor(ob4, PS[:, 4 + t % 2, :].rearrange("p (r q e) -> p r q e", r=4, q=2), tx4[:, :, :, 0, :], ALU.add).then_inc(S("core_o1"), 1)
                dve.wait_ge(*done("core_o1", t + 1))
                ch(nc.vector.tensor_tensor(ob4, ob4, tx4[:, :, :, 1, :], ALU.add))
                ch(nc.vector.tensor_reduce(mu, H(ob), AXX, ALU.add))
                ch(nc.vector.tensor_scalar(mu, mu, 1.0 / HD, None, ALU.mult))
                nc.vector.tensor_tensor(H(cb), H(ob), bcast_in(mu, 64), ALU.subtract).then_inc(S("core_c"), 1)
                dve.wait_ge(*done("core_sq", t + 1))
                ch(nc.vector.tensor_reduce(var, H(sqb), AXX, ALU.add))
                nc.vector.tensor_scalar(var, var, 1.0 / HD, GN_EPS, ALU.mult, ALU.add).then_inc(S("core_v"), 1)
                dve.wait_ge(*done("core_rt", t + 1))
                ch(nc.vector.reciprocal(var, var))
                ch(nc.vector.tensor_tensor(H(cb), H(cb), bcast_in(var, 64), ALU.mult))
                ch(nc.vector.tensor_tensor(cb, cb, gain, ALU.mult))
                ch(nc.vector.tensor_tensor(RG[:, t, :], RG[:, t, :], cb, ALU.mult))

        def core_act(act):
            for t in range(NT):
                act.wait_ge(*done("core_c", t + 1))
                nc.scalar.activation(sqb, cb, ACT.Square).then_inc(S("core_sq"), 1)
                act.wait_ge(*done("core_v", t + 1))
                nc.scalar.activation(ssq[:, 8:16], ssq[:, 8:16], ACT.Sqrt).then_inc(S("core_rt"), 1)

        def units_na():
            us = []
            for t in range(XT):
                b = key_base(t)
                for h in range(NAH):
                    q = slice(64 * (h % 2), 64 * (h % 2) + 64)
                    r = h // 2
                    us.append(dict(
                        q=QT[q, r, t * P:t * P + P],
                        ks=[(KT[q, r, b * P:b * P + 512], 0), (KT[q, r, b * P + 512:b * P + 640], 512), (KT[q, r, SEQ:TOK], 640)],
                        n=896, nbias=(h, 2 * b - 2 * t + 8, t), bias=None, sink=None,
                        vs=[NV[:, kt, h * 64:h * 64 + 64] for kt in [b, b + 1, b + 2, b + 3, b + 4, 8, 9]],
                        h=h, out=NO[:, t, :]))
            for t in range(XT, NT):
                for h in range(NAH):
                    q = slice(64 * (h % 2), 64 * (h % 2) + 64)
                    r = h // 2
                    us.append(dict(q=QT[q, r, t * P:t * P + P], ks=[(KT[q, r, SEQ:TOK], 0)], n=256, nbias=None,
                                   bias=BAND[:, 0:256], sink=None, vs=[NV[:, kt, h * 64:h * 64 + 64] for kt in (8, 9)],
                                   h=h, out=NO[:, t, :]))
            return us

        def units_swa():
            us = []
            for t in range(XT):
                lo, hi = max(t - 1, 0), min(t + 1, XT - 1)
                loc = (hi - lo + 1) * P
                for h in range(SWH):
                    kv = h // 4
                    q = slice(64 * (kv % 2), 64 * (kv % 2) + 64)
                    r = kv // 2
                    near = KT1[q, r, lo * P:hi * P + P]
                    if t == XT - 1:
                        ks, mcol, kts = [(KT1[q, r, SEQ:TOK], 0), (near, 256)], 0, [8, 9, lo, hi]
                    elif t == 0:
                        ks, mcol, kts = [(near, 0), (KT1[q, r, SEQ:TOK], 256)], 256 + P, [lo, hi, 8, 9]
                    else:
                        ks = [(near, 0), (KT1[q, r, SEQ:SEQ + P], 384), (KT1[q, r, SEQ + P:TOK], 512)]
                        mcol, kts = 256, [lo, t, hi, 8, 9]
                    us.append(dict(q=QT1[q, 4 * (h // 8) + h % 4, t * P:t * P + P], ks=ks, n=loc + 256, nbias=None,
                                   bias=BAND[:, mcol:mcol + loc + 256], sink=h,
                                   vs=[V1[:, kt, kv * 64:kv * 64 + 64] for kt in kts],
                                   h=h % 8, out=AO[:, t, (h // 8) * 512:(h // 8) * 512 + 512]))
            return us

        nmax = atts[:, 0:16].rearrange("p (g h) -> p g h", g=2)
        sums = atts[:, 16:32].rearrange("p (g h) -> p g h", g=2)
        sinkr = atts[:, 32:48]
        sinke = atts[:, 48:64].rearrange("p (g h) -> p g h", g=2)
        amx = atts[:, 64:67]

        def psS(i, a, b):
            return PS[:, 2 * (i % 2):2 * (i % 2) + 2, :].rearrange("p b n -> p (b n)")[:, a:b]

        PT2 = PS[:, 4:6, :].rearrange("p b n -> p (b n)")

        def att_pool(pool, us, n):
            nb = 0
            for i, u in enumerate(us):
                if u["nbias"] is None:
                    continue
                h, j0, t = u["nbias"]
                if nb == 0:
                    pool.wait_ge(*done("toep", 1))
                    for b in biasb:
                        nc.gpsimd.memset(b[:, 640:896], 0.0)
                if nb >= 3:
                    pool.wait_ge(*done(f"{n}_bs", i - 2))
                nc.gpsimd.tensor_tensor(biasb[nb % 3][:, 0:640].rearrange("p (j c) -> p j c", c=64), TOEP[:, h, j0:j0 + 10, :],
                                        bcast_in(cst[:, C_ROW + 10 * t:C_ROW + 10 * t + 10], 64), ALU.add).then_inc(S(f"{n}_bias"), 1)
                nb += 1

        def att_pe(pe, us, n):
            def scores(i):
                u = us[i]
                if i >= 2:
                    pe.wait_ge(*done(f"{n}_bs", i - 1))
                for k, c in u["ks"]:
                    mm = nc.tensor.matmul(psS(i, c, c + k.shape[1]), u["q"], k, start=True, stop=True)
                mm.then_inc(S(f"{n}_s"), 1)

            def turn(i):
                pe.wait_ge(*done(f"{n}_e", i + 1))
                if i >= 1:
                    pe.wait_ge(*done(f"{n}_pt", i))
                for c in range(us[i]["n"] // P):
                    tr = nc.tensor.transpose(PT2[:, c * P:c * P + P], sxb[i % 3][:, c * P:c * P + P], ident)
                tr.then_inc(S(f"{n}_t"), 1)

            def values(i):
                u, g = us[i], i // 8
                pe.wait_ge(*done(f"{n}_pt", i + 1))
                if i % 8 == 0 and g >= 2:
                    pe.wait_ge(*done(f"{n}_o", g - 1))
                m = len(u["vs"])
                for c, v in enumerate(u["vs"]):
                    mm = nc.tensor.matmul(PS[:, 6 + g % 2, u["h"] * 64:u["h"] * 64 + 64], ptb[i % 2][:, c * P:c * P + P], v,
                                          start=(c == 0), stop=(c == m - 1))
                mm.then_inc(S(f"{n}_v"), 1)
            for i in range(len(us) + 2):
                if i < len(us):
                    scores(i)
                if 1 <= i <= len(us):
                    turn(i - 1)
                if i >= 2:
                    values(i - 2)

        def att_dve(dve, us, n):
            ch = chain(dve)

            def soft(i):
                u, g = us[i], i // 8
                nb = sum(1 for v in us[:i + 1] if v["nbias"] is not None)
                dve.wait_ge(*done(f"{n}_s", i + 1))
                if i >= 3:
                    dve.wait_ge(*done(f"{n}_t", i - 2))
                x = sxb[i % 3]
                if u["nbias"] is not None:
                    dve.wait_ge(*done(f"{n}_bias", nb))
                b = biasb[(nb - 1) % 3] if u["nbias"] is not None else u["bias"]
                m = amx[:, i % 3:i % 3 + 1]
                if i >= 3:
                    dve.wait_ge(*done(f"{n}_m", i - 2))
                nc.vector.tensor_tensor_reduce(out=x[:, 0:u["n"]], in0=psS(i, 0, u["n"]), in1=b[:, 0:u["n"]], scale=SCALE, scalar=-3e38,
                                               op0=ALU.add, op1=ALU.max, accum_out=m).then_inc(S(f"{n}_bs"), 1)
                dve.wait_ge(*done(f"{n}_bs", i + 1))
                if i % 8 == 0 and g >= 2:
                    dve.wait_ge(*done(f"{n}_o", g - 1))
                nm = nmax[:, g % 2, u["h"]:u["h"] + 1]
                if u["sink"] is None:
                    ins = nc.vector.tensor_scalar(nm, m, -1.0, None, ALU.mult)
                else:
                    ins = nc.vector.tensor_scalar(nm, m, sinkr[:, u["sink"]:u["sink"] + 1], -1.0, ALU.max, ALU.mult)
                ins.then_inc(S(f"{n}_m"), 1)
                if u["sink"] is not None and i % 8 == 7:
                    dve.wait_ge(*done(f"{n}_m", i + 1))
                    hs = u["sink"] - 7
                    nc.vector.tensor_tensor(sinke[:, g % 2, :], nmax[:, g % 2, :], sinkr[:, hs:hs + 8], ALU.add).then_inc(S(f"{n}_ks"), 1)

            def finish(g):
                u = us[8 * g]
                dve.wait_ge(*done(f"{n}_e", 8 * g + 8))
                s = sums[:, g % 2, :]
                if u["sink"] is not None:
                    dve.wait_ge(*done(f"{n}_ke", g + 1))
                    ch(nc.vector.tensor_tensor(s, s, sinke[:, g % 2, :], ALU.add))
                ch(nc.vector.reciprocal(s, s))
                dve.wait_ge(*done(f"{n}_v", 8 * g + 8))
                nc.vector.tensor_tensor(u["out"].rearrange("p (h e) -> p h e", h=8), PS[:, 6 + g % 2, :].rearrange("p (h e) -> p h e", h=8),
                                        bcast_in(s, 64), ALU.mult).then_inc(S(f"{n}_o"), 1)
                dve.wait_ge(*done(f"{n}_o", g + 1))
            if us[0]["sink"] is not None:
                dve.wait_ge(*done("sink_in", 16))
            for i in range(len(us)):
                soft(i)
                if i % 8 == 2 and i > 8:
                    finish(i // 8 - 1)
            finish(len(us) // 8 - 1)

        def att_act(act, us, n):
            def evict(i):
                act.wait_ge(*done(f"{n}_t", i + 1))
                if i >= 2:
                    act.wait_ge(*done(f"{n}_v", i - 1))
                nc.scalar.activation(ptb[i % 2][:, 0:us[i]["n"]], PT2[:, 0:us[i]["n"]], ACT.Copy).then_inc(S(f"{n}_pt"), 1)

            def exps(i):
                u, g = us[i], i // 8
                act.wait_ge(*done(f"{n}_m", i + 1))
                if i % 8 == 0 and g >= 2:
                    act.wait_ge(*done(f"{n}_o", g - 1))
                x = sxb[i % 3][:, 0:u["n"]]
                nc.scalar.activation(x, x, ACT.Exp, bias=nmax[:, g % 2, u["h"]:u["h"] + 1],
                                     accum_out=sums[:, g % 2, u["h"]:u["h"] + 1]).then_inc(S(f"{n}_e"), 1)
                if u["sink"] is not None and i % 8 == 7:
                    act.wait_ge(*done(f"{n}_ks", g + 1))
                    nc.scalar.activation(sinke[:, g % 2, :], sinke[:, g % 2, :], ACT.Exp).then_inc(S(f"{n}_ke"), 1)
            for i in range(len(us) + 1):
                if i >= 1:
                    evict(i - 1)
                if i < len(us):
                    exps(i)

        def out_tiles(l):
            return ([8, 9] + list(range(XT))) if l == 0 else list(range(XT))

        def out_sp(sp, l):
            n = f"o{l}"
            w = A["ab_w_out"][0] if l == 0 else A["swa_w_out"][0]
            sp.dma_start(WO, w.rearrange("(k p) n -> p k n", p=P)).then_inc(S(f"{n}_w"), 16)
            with nc.allow_non_contiguous_dma("the router's weights, of few columns"):
                sp.dma_start(rw[:, :, 0:GRP], A["router_g_w"][l].rearrange("(k p) n -> p k n", p=P)).then_inc(S(f"{n}_w"), 16)
                sp.dma_start(rw[:, :, GRP:NLOG], A["router_e_w"][l].rearrange("(k p) n -> p k n", p=P)).then_inc(S(f"{n}_w"), 16)
            sp.dma_start(rb[:, 0:GRP], A["router_g_b"][l].partition_broadcast(P)).then_inc(S(f"{n}_w"), 16)
            sp.dma_start(rb[:, GRP:NLOG], A["router_e_b"][l].partition_broadcast(P)).then_inc(S(f"{n}_w"), 16)

            def load_rows(s):
                sp.dma_start(rows[:, 0:3, :], mod[l, s, 2 * D:5 * D].rearrange("(j n) -> j n", j=3).partition_broadcast(P))\
                    .then_inc(S(f"{n}_rows"), 16)
            if l == 0:
                load_rows(1)
                sp.dma_start(XR[:, XT:NT, :], A["ctx"][0].rearrange("(t p) n -> p t n", p=P)).then_inc(S("o0_ctx_in"), 16)
                sp.dma_start(XR[:, 0:XT, :], A["x"][0].rearrange("(t p) n -> p t n", p=P)).then_inc(S("o0_x_in"), 16)
            else:
                load_rows(0)
            for i, t in enumerate(out_tiles(l)):
                sp.wait_ge(*done(f"{n}_h2", i + 1))
                sp.dma_start(h2d[t * P:t * P + P, :], h2).then_inc(S(f"{n}_h2o"), 16)
                if l == 0 and i == 1:
                    load_rows(0)
            sp.wait_ge(*done(f"{n}_h2o", 16 * len(out_tiles(l))))

        def out_pe(pe, l):
            n, ts = f"o{l}", out_tiles(l)

            def mix(i, k):
                if l == 1:
                    return AO[:, ts[i], k * P:k * P + P]
                return (RG if k < 4 else NO)[:, ts[i], (k % 4) * P:(k % 4 + 1) * P]

            def turn(i):
                if i >= 1:
                    pe.wait_ge(*done(f"{n}_me", i))
                for k in range(KC):
                    tr = nc.tensor.transpose(PS[:, k // 4, (k % 4) * P:(k % 4 + 1) * P], mix(i, k), ident)
                tr.then_inc(S(f"{n}_mt"), 1)

            def product(i):
                pe.wait_ge(*done(f"{n}_me", i + 1))
                for half in range(2):
                    if i >= 1:
                        pe.wait_ge(*done(f"{n}_pe", 2 * (i - 1) + half + 1))
                    for k in range(KC):
                        mm = nc.tensor.matmul(PS[:, 2 + half, :], mixT[i % 2][:, k, :], WO[:, k, half * 512:half * 512 + 512],
                                              start=(k == 0), stop=(k == KC - 1))
                    mm.then_inc(S(f"{n}_mm"), 1)

            def turn2(i):
                pe.wait_ge(*done(f"{n}_h2", i + 1))
                if i >= 1:
                    pe.wait_ge(*done(f"{n}_he", i))
                for k in range(KC):
                    tr = nc.tensor.transpose(PS[:, 6 + k // 4, (k % 4) * P:(k % 4 + 1) * P], h2[:, k * P:k * P + P], ident)
                tr.then_inc(S(f"{n}_ht"), 1)

            def router(i):
                pe.wait_ge(*done(f"{n}_he", i + 1))
                if i >= 2:
                    pe.wait_ge(*done(f"{n}_lg", i - 1))
                for k in range(KC):
                    mm = nc.tensor.matmul(PS[:, 4 + i % 2, 0:NLOG], h2T[:, k, :], rw[:, k, :], start=(k == 0), stop=(k == KC - 1))
                mm.then_inc(S(f"{n}_r"), 1)
            pe.wait_ge(*done(f"{n}_w", 80))
            for i in range(len(ts) + 2):
                if i < len(ts):
                    turn(i)
                    product(i)
                if i >= 2:
                    router(i - 2)
                if 1 <= i <= len(ts):
                    turn2(i - 1)

        def out_act(act, l):
            n, ts = f"o{l}", out_tiles(l)

            def evict_mix(i):
                act.wait_ge(*done(f"{n}_mt", i + 1))
                if i >= 2:
                    act.wait_ge(*done(f"{n}_mm", 2 * (i - 1)))
                nc.scalar.activation(mixT[i % 2].rearrange("p k n -> p (k n)"), PS[:, 0:2, :].rearrange("p b n -> p (b n)"), ACT.Copy)\
                    .then_inc(S(f"{n}_me"), 1)

            def stats(i):
                act.wait_ge(*done(f"{n}_x", i + 1))
                nc.scalar.activation(junk, XR[:, ts[i], :], ACT.Square, accum_out=ssq[:, i:i + 1]).then_inc(S(f"{n}_ss"), 1)
                act.wait_ge(*done(f"{n}_ms", i + 1))
                nc.scalar.activation(ssq[:, i:i + 1], ssq[:, i:i + 1], ACT.Sqrt).then_inc(S(f"{n}_rt"), 1)

            def evict_h2(i):
                act.wait_ge(*done(f"{n}_ht", i + 1))
                if i >= 1:
                    act.wait_ge(*done(f"{n}_r", i))
                nc.scalar.activation(h2T.rearrange("p k n -> p (k n)"), PS[:, 6:8, :].rearrange("p b n -> p (b n)"), ACT.Copy)\
                    .then_inc(S(f"{n}_he"), 1)
            evict_mix(0)
            for i in range(len(ts) + 1):
                if i + 1 < len(ts):
                    evict_mix(i + 1)
                if i < len(ts):
                    stats(i)
                if i < len(ts):
                    evict_h2(i)

        def out_dve(dve, l):
            n, ts = f"o{l}", out_tiles(l)
            ch = chain(dve)

            def logits(i):
                dve.wait_ge(*done(f"{n}_r", i + 1))
                nc.vector.tensor_tensor(LG[:, ts[i], :], PS[:, 4 + i % 2, 0:NLOG], rb, ALU.add).then_inc(S(f"{n}_lg"), 1)
            for i, t in enumerate(ts):
                if l == 0:
                    dve.wait_ge(*done("o0_x_in" if t < XT else "o0_ctx_in", 16))
                dve.wait_ge(*done(f"{n}_rows", 32 if (l == 0 and i >= 2) else 16))
                for half in range(2):
                    dve.wait_ge(*done(f"{n}_mm", 2 * i + half + 1))
                    c = slice(half * 512, half * 512 + 512)
                    nc.vector.tensor_tensor(tmpb[half], PS[:, 2 + half, :], rows[:, 0, c], ALU.mult).then_inc(S(f"{n}_pe"), 1)
                    dve.wait_ge(*done(f"{n}_pe", 2 * i + half + 1))
                    ins = nc.vector.tensor_tensor(XR[:, t, c], XR[:, t, c], tmpb[half], ALU.add)
                    if half == 0:
                        ch(ins)
                    else:
                        ins.then_inc(S(f"{n}_x"), 1)
                r = ssq[:, i:i + 1]
                dve.wait_ge(*done(f"{n}_ss", i + 1))
                nc.vector.tensor_scalar(r, r, 1.0 / D, EPS, ALU.mult, ALU.add).then_inc(S(f"{n}_ms"), 1)
                dve.wait_ge(*done(f"{n}_rt", i + 1))
                ch(nc.vector.reciprocal(r, r))
                if i >= 1:
                    dve.wait_ge(*done(f"{n}_ht", i))
                    dve.wait_ge(*done(f"{n}_h2o", 16 * i))
                ch(nc.vector.scalar_tensor_tensor(out=h2, in0=XR[:, t, :], scalar=r, in1=rows[:, 2, :], op0=ALU.mult, op1=ALU.mult))
                nc.vector.tensor_tensor(h2, h2, rows[:, 1, :], ALU.add).then_inc(S(f"{n}_h2"), 1)
                if i >= 1:
                    logits(i - 1)
            logits(len(ts) - 1)

        def tiles_of(l):
            return NT if l == 0 else XT

        def route_views(l):
            nt = tiles_of(l)
            v = {}
            at = WR
            for name, w in (("M1", EXP), ("M2", EXP), ("lm", EXP), ("eq", EXP), ("cand", EXP), ("M", EXP), ("dst", EXP), ("big", EXP), ("g4", GRP), ("e4", GRP)):
                v[name] = R(at, nt * w).rearrange("p (t e) -> p t e", t=nt)
                at += NT * w
            v["C"] = R(at, (NT + 1) * EXP).rearrange("p (t e) -> p t e", t=NT + 1)
            at += (NT + 1) * EXP
            for name in ("gm", "gi", "gs", "gw", "m1", "e1", "m2", "e2", "ex", "rr", "d1", "d2", "pp", "bb"):
                v[name] = R(at, nt)
                at += NT
            for name in ("cnt", "nov", "cum", "hi", "io128"):
                v[name] = R(at, EXP)
                at += EXP
            v["cmp"] = R(at, OVF * EXP).rearrange("p (b e) -> p b e", b=OVF)
            at += OVF * EXP
            v["eo"] = R(at, OVF)
            at += OVF
            v["ii"] = R(at, 2 * NT).bitcast(I32).rearrange("p (j t) -> p j t", j=2)
            at += 2 * NT
            v["tf"] = R(at, NT)
            assert at + NT <= TR
            return v

        def route_dve(dve, l):
            n, nt, v = f"r{l}", tiles_of(l), route_views(l)
            ch = chain(dve)
            V = nc.vector
            iota = bcast_mid(cst[:, C_IO:C_IO + EXP], nt)
            lg, le = LG[:, 0:nt, 0:GRP], LG[:, 0:nt, GRP:NLOG]

            def first_max(x, width, m, e):
                ch(V.tensor_reduce(v[m], x, AXX, ALU.max))
                q, c = (v["eq"], v["cand"]) if width == EXP else (v["g4"], v["e4"])
                ch(V.tensor_tensor(q, x, bcast_in(v[m], width), ALU.is_equal))
                ch(V.tensor_scalar(q, q, -100.0, 100.0, ALU.mult, ALU.add))
                ch(V.tensor_tensor(c, q, bcast_mid(cst[:, C_IO:C_IO + width], nt), ALU.add))
                ch(V.tensor_reduce(v[e], c, AXX, ALU.min))

            first_max(lg, GRP, "gm", "gi")
            V.tensor_tensor(v["e4"], lg, bcast_in(v["gm"], GRP), ALU.subtract).then_inc(S(f"{n}_g"), 1)
            ch(V.tensor_tensor(v["eq"], bcast_mid(cst[:, C_IG:C_IG + EXP], nt), bcast_in(v["gi"], EXP), ALU.is_equal))
            ch(V.tensor_scalar(v["eq"], v["eq"], -NEG, NEG, ALU.mult, ALU.add))
            ch(V.tensor_tensor(v["lm"], le, v["eq"], ALU.add))
            first_max(v["lm"], EXP, "m1", "e1")
            ch(V.tensor_tensor(v["M1"], iota, bcast_in(v["e1"], EXP), ALU.is_equal))
            ch(V.tensor_scalar(v["eq"], v["M1"], 3 * NEG, None, ALU.mult))
            ch(V.tensor_tensor(v["lm"], v["lm"], v["eq"], ALU.add))
            first_max(v["lm"], EXP, "m2", "e2")
            ch(V.tensor_tensor(v["M2"], iota, bcast_in(v["e2"], EXP), ALU.is_equal))
            V.tensor_tensor(v["ex"], v["m2"], v["m1"], ALU.subtract).then_inc(S(f"{n}_x"), 1)
            ch(V.tensor_tensor(v["M"], v["M1"], v["M2"], ALU.add))
            ch(V.memset(v["C"][:, 0, :], 0.0))
            for t in range(nt):
                ins = V.tensor_tensor(v["C"][:, t + 1, :], v["C"][:, t, :], v["M"][:, t, :], ALU.add)
                if t < nt - 1:
                    ch(ins)
            ins.then_inc(S(f"{n}_c"), 1)
            dve.wait_ge(*done(f"{n}_e", 2))
            ch(V.tensor_reduce(v["gs"], v["e4"], AXX, ALU.add))
            ch(V.reciprocal(v["gw"], v["gs"]))
            ch(V.tensor_scalar(v["rr"], v["ex"], 1.0, None, ALU.add))
            ch(V.reciprocal(v["rr"], v["rr"]))
            ch(V.tensor_tensor(wgt[:, 0, 0:nt], v["gw"], v["rr"], ALU.mult))
            ch(V.tensor_tensor(wgt[:, 1, 0:nt], wgt[:, 0, 0:nt], v["ex"], ALU.mult))
            ch(V.tensor_copy(toki, cst[:, C_TOK:C_TOK + NT]))
            dve.wait_ge(*done(f"{n}_mm", 1))
            ch(V.tensor_copy(v["cnt"], PS[:, 1, 0:EXP]))
            ch(V.memset(v["nov"], 0.0))
            for j in range(1, nt):
                ch(V.scalar_tensor_tensor(out=v["nov"], in0=v["cnt"], scalar=float(P * j), in1=v["nov"], op0=ALU.is_gt, op1=ALU.add))
            ch(V.tensor_tensor_scan(v["cum"], cst[:, C_ONE:C_ONE + EXP], v["nov"], 0.0, ALU.mult, ALU.add))
            ch(V.tensor_scalar(v["io128"], cst[:, C_IO:C_IO + EXP], float(P), None, ALU.mult))
            ch(V.tensor_tensor(v["hi"], v["cum"], v["nov"], ALU.subtract))
            ch(V.scalar_tensor_tensor(out=v["hi"], in0=v["hi"], scalar=float(P), in1=v["io128"], op0=ALU.mult, op1=ALU.subtract))
            ch(V.tensor_scalar(v["hi"], v["hi"], float((EXP - 1) * P), None, ALU.add))
            rank = PS[:, 0, 0:nt * EXP].rearrange("p (t e) -> p t e", t=nt)
            ch(V.tensor_scalar(v["big"], rank, float(P), None, ALU.is_ge))
            ch(V.tensor_tensor(v["big"], v["big"], bcast_mid(v["hi"], nt), ALU.mult))
            ch(V.tensor_tensor(v["dst"], rank, v["big"], ALU.add))
            ch(V.tensor_tensor(v["dst"], v["dst"], bcast_mid(v["io128"], nt), ALU.add))
            for j, m in enumerate(("M1", "M2")):
                ch(V.tensor_tensor(v[m], v[m], v["dst"], ALU.mult))
                ch(V.tensor_reduce(v["d1"], v[m], AXX, ALU.add))
                ch(V.tensor_copy(dsti[:, j, 0:nt], v["d1"]))
                ch(V.tensor_scalar(v["ii"][:, 0, 0:nt], dsti[:, j, 0:nt], 127, None, ALU.bitwise_and))
                ch(V.tensor_scalar(v["ii"][:, 1, 0:nt], dsti[:, j, 0:nt], 7, None, ALU.arith_shift_right))
                ch(V.tensor_copy(v["pp"], v["ii"][:, 0, 0:nt]))
                ch(V.tensor_copy(v["bb"], v["ii"][:, 1, 0:nt]))
                ch(V.scalar_tensor_tensor(out=v["pp"], in0=v["pp"], scalar=float(BLK), in1=v["bb"], op0=ALU.mult, op1=ALU.add))
                ins = V.tensor_copy(posi[:, j, 0:nt], v["pp"])
                if j == 0:
                    ch(ins)
            ins.then_inc(S(f"{n}_pos"), 1)
            ch(V.tensor_tensor(v["cmp"], bcast_mid(v["cum"], OVF), bcast_in(cst[:, C_IO:C_IO + OVF], EXP), ALU.is_le))
            ch(V.tensor_reduce(v["eo"], v["cmp"], AXX, ALU.add))
            ch(V.tensor_scalar(v["eo"], v["eo"], float(EXP - 1), None, ALU.min))
            ch(V.tensor_copy(ctl[:, 1:1 + OVF], v["eo"]))
            V.tensor_copy(ctl[:, 0:1], v["cum"][:, EXP - 1:EXP]).then_inc(S(f"{n}_ctl"), 1)

        def route_act(act, l):
            n, v = f"r{l}", route_views(l)
            act.wait_ge(*done(f"{n}_g", 1))
            nc.scalar.activation(v["e4"], v["e4"], ACT.Exp).then_inc(S(f"{n}_e"), 1)
            act.wait_ge(*done(f"{n}_x", 1))
            nc.scalar.activation(v["ex"], v["ex"], ACT.Exp).then_inc(S(f"{n}_e"), 1)

        def route_pe(pe, l):
            n, nt, v = f"r{l}", tiles_of(l), route_views(l)
            pe.wait_ge(*done(f"{n}_c", 1))
            for t in range(nt):
                o = PS[:, 0, t * EXP:t * EXP + EXP]
                nc.tensor.matmul(o, cst[:, C_TRI:C_TRI + P], v["M"][:, t, :], start=True, stop=False)
                nc.tensor.matmul(o, cst[:, C_ONE:C_ONE + P], v["C"][:, t, :], start=False, stop=True)
            nc.tensor.matmul(PS[:, 1, 0:EXP], cst[:, C_ONE:C_ONE + P], v["C"][:, nt, :], start=True, stop=True).then_inc(S(f"{n}_mm"), 1)

        def route_pool(pool, l):
            n, nt = f"r{l}", tiles_of(l)
            pool.wait_ge(*done(f"{n}_pos", 1))
            pool.wait_ge(*done("zeros_out", 64))
            for j in range(2):
                for t in range(nt):
                    pool.indirect_dma_start(out=slot_tok[l], out_offset=bass.IndirectOffsetOnAxis(ap=posi[:, j, t:t + 1], axis=0),
                                            in_=toki[:, t:t + 1], in_offset=None).then_inc(S(f"{n}_st"), 16)
            pool.wait_ge(*done(f"{n}_st", 16 * 2 * nt))
            pool.dma_start(idx, slot_tok[l].rearrange("(p b) o -> p (b o)", b=BLK)).then_inc(S(f"{n}_idx"), 16)
            pool.wait_ge(*done(f"{n}_idx", 16))
            pool.wait_ge(*done(f"o{l}_h2o", 16 * nt))

        def positive(value):
            return not isinstance(value, int) or value > 0

        class Steps:

            def __init__(self, n):
                self.n = n

            def turn(self, pe, e, s, i):
                n = self.n
                pe.wait_ge(*done(f"{n}_hb{s}", 16 * (i + 1)))
                if positive(e):
                    pe.wait_ge(*done(f"{n}_hbT", e))
                for k in range(KC):
                    tr = nc.tensor.transpose(PS[:, k // 4, (k % 4) * P:(k % 4 + 1) * P],
                                             hb[s].rearrange("p (m k) -> p k m", k=KC)[:, k, :], ident)
                tr.then_inc(S(f"{n}_tr"), 1)

            def half(self, pe, e, s, i, up):
                n = self.n
                if not up:
                    pe.wait_ge(*done(f"{n}_hbT", e + 1))
                    pe.wait_ge(*done(f"{n}_wg{s}", 16 * (i + 1)))
                    if positive(e):
                        pe.wait_ge(*done(f"{n}_silu", e))
                else:
                    if positive(e):
                        pe.wait_ge(*done(f"{n}_mul", e))
                for k in range(KC):
                    mm = nc.tensor.matmul(PS[:, 2 + up, :], hbT[s][:, k, :], wgu[s][:, k, up * 512:up * 512 + 512],
                                          start=(k == 0), stop=(k == KC - 1))
                if up:
                    mm.then_inc(S(f"{n}_gu"), 1)

            def turn_gu(self, pe, e, s):
                n = self.n
                pe.wait_ge(*done(f"{n}_mul", e + 1))
                if positive(e):
                    pe.wait_ge(*done(f"{n}_guT", e))
                for k in range(4):
                    tr = nc.tensor.transpose(PS[:, 4, k * P:k * P + P], gub[s].rearrange("p (m k) -> p k m", k=4)[:, k, :], ident)
                tr.then_inc(S(f"{n}_gt"), 1)

            def down(self, pe, e, s, i):
                n = self.n
                pe.wait_ge(*done(f"{n}_guT", e + 1))
                pe.wait_ge(*done(f"{n}_wd{s}", 16 * (i + 1)))
                if positive(e):
                    pe.wait_ge(*done(f"{n}_y", e))
                for c in range(2):
                    for k in range(4):
                        mm = nc.tensor.matmul(PS[:, 5 + c, :], guT[s][:, k, :], wdn[s][:, k, c * 512:c * 512 + 512],
                                              start=(k == 0), stop=(k == 3))
                mm.then_inc(S(f"{n}_dn"), 1)

            def silu(self, act, e, s):
                n = self.n
                act.wait_ge(*done(f"{n}_gu", e + 1))
                if positive(e - 1):
                    act.wait_ge(*done(f"{n}_mul", e - 1))
                nc.scalar.activation(sg[s], PS[:, 2, :], ACT.Silu).then_inc(S(f"{n}_silu"), 1)

            def store(self, act, e, s, i, row):
                n = self.n
                act.wait_ge(*done(f"{n}_dn", e + 1))
                if positive(16 * i):
                    act.wait_ge(*done(f"{n}_yo{s}", 16 * i))
                nc.scalar.activation(yb[s], PS[:, 5:7, :].rearrange("p b n -> p (b n)"), ACT.Copy).then_inc(S(f"{n}_y"), 1)
                act.wait_ge(*done(f"{n}_y", e + 1))
                act.dma_start(yd[bass.ds(row, P), :], yb[s]).then_inc(S(f"{n}_yo{s}"), 16)

            def rows_in(self, dve, e, s, gu_done):
                n = self.n
                dve.wait_ge(*done(f"{n}_tr", e + 1))
                if positive(gu_done):
                    dve.wait_ge(*done(f"{n}_gu", gu_done))
                nc.vector.tensor_copy(hbT[s].rearrange("p k n -> p (k n)"), PS[:, 0:2, :].rearrange("p b n -> p (b n)")).then_inc(S(f"{n}_hbT"), 1)

            def mul(self, dve, e, s, gt_done):
                n = self.n
                dve.wait_ge(*done(f"{n}_silu", e + 1))
                if positive(gt_done):
                    dve.wait_ge(*done(f"{n}_gt", gt_done))
                nc.vector.tensor_tensor(gub[s], PS[:, 3, :], sg[s], ALU.mult).then_inc(S(f"{n}_mul"), 1)

            def gu_in(self, dve, e, s, dn_done):
                n = self.n
                dve.wait_ge(*done(f"{n}_gt", e + 1))
                if positive(dn_done):
                    dve.wait_ge(*done(f"{n}_dn", dn_done))
                nc.vector.tensor_copy(guT[s].rearrange("p k n -> p (k n)"), PS[:, 4, :]).then_inc(S(f"{n}_guT"), 1)

            def gather(self, pool, e, s, col, tr_done):
                n = self.n
                if positive(tr_done):
                    pool.wait_ge(*done(f"{n}_tr", tr_done))
                nc.gpsimd.tensor_copy(idxc[s], idx[:, bass.ds(col, 1)])
                pool.drain()
                pool.indirect_dma_start(out=hb[s], out_offset=None, in_=h2d,
                                        in_offset=bass.IndirectOffsetOnAxis(ap=idxc[s], axis=0)).then_inc(S(f"{n}_hb{s}"), 16)

        def wg_src(l, e):
            return A["expert_w_gu"][l, bass.ds(e, 1)].rearrange("e (p k) n -> p (e k n)", k=KC)

        def wd_src(l, e):
            return A["expert_w_down"][l, bass.ds(e, 1)].rearrange("e (p k) n -> p (e k n)", k=4)

        def moe_sp(sp, l):
            n = f"m{l}"

            def load(e, s):
                if positive(e - 1):
                    sp.wait_ge(*done(f"{n}_gu", e - 1))
                sp.dma_start(wgu[s].rearrange("p k n -> p (k n)"), wg_src(l, e)).then_inc(S(f"{n}_wg{s}"), 16)
                if positive(e - 1):
                    sp.wait_ge(*done(f"{n}_dn", e - 1))
                sp.dma_start(wdn[s].rearrange("p k n -> p (k n)"), wd_src(l, e)).then_inc(S(f"{n}_wd{s}"), 16)
            load(0, 0)
            load(1, 1)
            with sp.Fori(1, EXP // 2) as i:
                load(2 * i, 0)
                load(2 * i + 1, 1)

        def overflow(eng, l, body):
            eng.wait_ge(*done(f"r{l}_ctl", 1))
            count = eng.value_load(ctl[0:1, 0:1], min_val=0, max_val=OVF)
            with eng.Fori(0, OVF) as b:
                with eng.If(count > b):
                    body(b)

        def moe_pe(pe, l):
            k = Steps(f"m{l}")

            def body(e, s, i, first=False):
                j = i if s == 1 else i - 1
                nx = i if s == 0 else i + 1
                k.half(pe, e, s, i, 0)
                if not first:
                    k.turn_gu(pe, e - 1, 1 - s)
                k.turn(pe, e + 1, 1 - s, nx)
                k.half(pe, e, s, i, 1)
                if not first:
                    k.down(pe, e - 1, 1 - s, j)
            k.turn(pe, 0, 0, 0)
            body(0, 0, 0, first=True)
            body(1, 1, 0)
            body(2, 0, 1)
            with pe.Fori(1, EXP // 2 - 1) as i:
                body(2 * i + 1, 1, i)
                body(2 * i + 2, 0, i + 1)
            last, h = EXP - 1, EXP // 2 - 1
            k.half(pe, last, 1, h, 0)
            k.turn_gu(pe, last - 1, 0)
            k.half(pe, last, 1, h, 1)
            k.down(pe, last - 1, 0, h)
            k.turn_gu(pe, last, 1)
            k.down(pe, last, 1, h)

            def block(b):
                e, i = EXP + b, EXP // 2 + b
                k.turn(pe, e, 0, i)
                k.half(pe, e, 0, i, 0)
                k.half(pe, e, 0, i, 1)
                k.turn_gu(pe, e, 0)
                k.down(pe, e, 0, i)
            overflow(pe, l, block)

        def moe_act(act, l):
            k = Steps(f"m{l}")
            k.silu(act, 0, 0)
            k.silu(act, 1, 1)
            k.store(act, 0, 0, 0, 0)
            k.silu(act, 2, 0)
            k.store(act, 1, 1, 0, P)
            with act.Fori(1, EXP // 2 - 1) as i:
                k.silu(act, 2 * i + 1, 1)
                k.store(act, 2 * i, 0, i, 2 * i * P)
                k.silu(act, 2 * i + 2, 0)
                k.store(act, 2 * i + 1, 1, i, (2 * i + 1) * P)
            h = EXP // 2 - 1
            k.silu(act, EXP - 1, 1)
            k.store(act, EXP - 2, 0, h, (EXP - 2) * P)
            k.store(act, EXP - 1, 1, h, (EXP - 1) * P)

            def block(b):
                k.silu(act, EXP + b, 0)
                k.store(act, EXP + b, 0, EXP // 2 + b, (EXP + b) * P)
            act.wait_ge(*done(f"m{l}_yo1", 8 * EXP))
            overflow(act, l, block)
            act.wait_ge(*done(f"m{l}_yo0", act.value_load(ctl[0:1, 0:1], min_val=0, max_val=OVF) * 16 + 8 * EXP))
            nc.scalar.activation(ssq[:, 0:1], ssq[:, 0:1], ACT.Copy).then_inc(S(f"m{l}_all"), 1)

        def moe_dve(dve, l):
            k = Steps(f"m{l}")
            k.rows_in(dve, 0, 0, 0)
            k.rows_in(dve, 1, 1, 0)
            k.mul(dve, 0, 0, 0)

            def pair(i):
                e = 2 * i + 1
                k.gu_in(dve, e - 1, 0, 2 * i)
                k.rows_in(dve, e + 1, 0, e)
                k.mul(dve, e, 1, 2 * i)
                k.gu_in(dve, e, 1, 2 * i)
                k.rows_in(dve, e + 2, 1, e + 1)
                k.mul(dve, e + 1, 0, e)
            pair(0)
            with dve.Fori(1, EXP // 2 - 1) as i:
                pair(i)
            last = EXP - 1
            k.gu_in(dve, last - 1, 0, last - 2)
            k.mul(dve, last, 1, last - 1)
            k.gu_in(dve, last, 1, last - 1)

            def block(b):
                e = EXP + b
                k.rows_in(dve, e, 0, e)
                k.mul(dve, e, 0, e)
                k.gu_in(dve, e, 0, e)
            overflow(dve, l, block)

        def moe_pool(pool, l):
            k = Steps(f"m{l}")
            k.gather(pool, 0, 0, 0, 0)
            k.gather(pool, 1, 1, 1, 0)
            with pool.Fori(1, EXP // 2) as i:
                k.gather(pool, 2 * i, 0, 2 * i, 2 * i - 1)
                k.gather(pool, 2 * i + 1, 1, 2 * i + 1, 2 * i)
            pool.wait_ge(*done(f"m{l}_tr", EXP))
            overflow(pool, l, lambda b: k.gather(pool, EXP + b, 0, EXP + b, EXP + b))

        def moe_sp_all(sp, l):
            moe_sp(sp, l)
            sp.wait_ge(*done(f"m{l}_dn", EXP))

            def block(b):
                e = sp.value_load(ctl[0:1, bass.ds(b + 1, 1)], min_val=0, max_val=EXP - 1)
                sp.wait_ge(*done(f"m{l}_dn", EXP + b))
                sp.dma_start(wgu[0].rearrange("p k n -> p (k n)"), wg_src(l, e)).then_inc(S(f"m{l}_wg0"), 16)
                sp.dma_start(wdn[0].rearrange("p k n -> p (k n)"), wd_src(l, e)).then_inc(S(f"m{l}_wd0"), 16)
            overflow(sp, l, block)

        def cmb_pool(pool, l):
            n = f"c{l}"
            pool.wait_ge(*done(f"m{l}_all", 1))
            for t in range(tiles_of(l)):
                if t >= 3:
                    pool.wait_ge(*done(f"{n}_used", t - 2))
                for j in range(2):
                    pool.indirect_dma_start(out=yg[t % 3][j], out_offset=None, in_=yd,
                                            in_offset=bass.IndirectOffsetOnAxis(ap=dsti[:, j, t:t + 1], axis=0)).then_inc(S(f"{n}_y{t % 3}"), 16)

        def cmb_sp(sp, l):
            n = f"c{l}"
            for s in range(2):
                sp.dma_start(g2row[:, s, :], mod[l, s, 5 * D:6 * D].partition_broadcast(P)).then_inc(S(f"{n}_g"), 16)
            if l == 1:
                sp.dma_start(fgrow, A["final_g"].partition_broadcast(P)).then_inc(S(f"{n}_g"), 16)
                for t in range(XT):
                    sp.wait_ge(*done("fin", t + 1))
                    sp.dma_start(out[0, t * P:t * P + P, :], outb[t % 2]).then_inc(S(f"out{t % 2}"), 16)
                for q in range(2):
                    sp.wait_ge(*done(f"out{q}", 16 * (XT // 2)))

        def cmb_dve(dve, l):
            n = f"c{l}"
            ch = chain(dve)
            dve.wait_ge(*done(f"{n}_g", 32 if l == 0 else 48))
            for t in range(tiles_of(l)):
                dve.wait_ge(*done(f"{n}_y{t % 3}", 32 * (t // 3 + 1)))
                y1, y2 = yg[t % 3]
                ch(nc.vector.tensor_scalar(cmb, y1, wgt[:, 0, t:t + 1], None, ALU.mult))
                nc.vector.scalar_tensor_tensor(out=cmb, in0=y2, scalar=wgt[:, 1, t:t + 1], in1=cmb, op0=ALU.mult, op1=ALU.add)\
                    .then_inc(S(f"{n}_used"), 1)
                dve.wait_ge(*done(f"{n}_used", t + 1))
                ch(nc.vector.tensor_tensor(cmb, cmb, g2row[:, 0 if t < XT else 1, :], ALU.mult))
                ins = nc.vector.tensor_tensor(XR[:, t, :], XR[:, t, :], cmb, ALU.add)
                if l == 0:
                    ch(ins)
                    continue
                ins.then_inc(S("fin_x"), 1)
                r = ssq[:, t:t + 1]
                dve.wait_ge(*done("fin_ss", t + 1))
                nc.vector.tensor_scalar(r, r, 1.0 / D, EPS, ALU.mult, ALU.add).then_inc(S("fin_ms"), 1)
                dve.wait_ge(*done("fin_rt", t + 1))
                ch(nc.vector.reciprocal(r, r))
                if t >= 2:
                    dve.wait_ge(*done(f"out{t % 2}", 16 * (t // 2)))
                nc.vector.scalar_tensor_tensor(out=outb[t % 2], in0=XR[:, t, :], scalar=r, in1=fgrow, op0=ALU.mult, op1=ALU.mult)\
                    .then_inc(S("fin"), 1)

        def cmb_act(act, l):
            if l == 0:
                return
            for t in range(XT):
                act.wait_ge(*done("fin_x", t + 1))
                nc.scalar.activation(junk, XR[:, t, :], ACT.Square, accum_out=ssq[:, t:t + 1]).then_inc(S("fin_ss"), 1)
                act.wait_ge(*done("fin_ms", t + 1))
                nc.scalar.activation(ssq[:, t:t + 1], ssq[:, t:t + 1], ACT.Sqrt).then_inc(S("fin_rt"), 1)

        na, sw = units_na(), units_swa()
        block = ctx.enter_context(nc.Block())

        MEET = ["ada", "n1", "proj", "core", "projb", "toep", "att", "out", "route", "moe", "cmb",
                "n1b", "projc", "attb", "outb", "routeb", "moeb"]
        num = {m: i + 1 for i, m in enumerate(MEET)}

        def dbg(sp):
            if "dbg" in A:
                for a, b in DBG:
                    sp.dma_start(A["dbg"][:, a:b], ar[:, a:b]).then_inc(S("dbg_out"), 16)
                sp.wait_ge(*done("dbg_out", 16 * len(DBG)))

        @block.sync
        def _(sp):
            ada_sp(sp)
            after_meet(sp, num["ada"])
            if STAGE < 2:
                return dbg(sp)
            n1_sp(sp, 0)
            proj_sp(sp, pa)
            sp.wait_ge(*done("phase", 4 * num["proj"]))
            if STAGE < 3:
                sp.wait_ge(*done("skew_out", 16 * NAH))
                return dbg(sp)
            sp.dma_start(gain, A["ret_gn"][0].partition_broadcast(P)).then_inc(S("gain_in"), 16)
            proj_sp(sp, pb)
            after_meet(sp, num["projb"])
            if STAGE < 4:
                sp.wait_ge(*done("skew_out", 16 * NAH))
                return dbg(sp)
            sp.dma_start(BAND, A["band"]).then_inc(S("band_in0"), 16)
            sp.wait_ge(*done("skew_out", 16 * NAH))
            for q in range(2):
                sp.dma_start(TOEP[64 * q:64 * q + 64], skew[:, :, 1 - q:19 - q, :]).then_inc(S("toep_in"), 16)
            after_meet(sp, num["att"])
            if STAGE < 5:
                return dbg(sp)
            out_sp(sp, 0)
            after_meet(sp, num["out"])
            if STAGE < 6:
                after_meet(sp, num["route"])
                return dbg(sp)
            moe_sp_all(sp, 0)
            after_meet(sp, num["moe"])
            cmb_sp(sp, 0)
            after_meet(sp, num["cmb"])
            if STAGE < 7:
                return dbg(sp)
            sp.dma_start(COS, A["rope"].rearrange("p (t f n) -> p t f n", t=XT, f=2)).then_inc(S("cos_in1"), 16)
            proj_sp(sp, pc)
            after_meet(sp, num["projc"])
            sp.dma_start(BAND, A["band"]).then_inc(S("band_in1"), 16)
            sp.dma_start(sinkr, A["swa_sink"][0].partition_broadcast(P)).then_inc(S("sink_in"), 16)
            after_meet(sp, num["attb"])
            if STAGE < 8:
                return dbg(sp)
            out_sp(sp, 1)
            after_meet(sp, num["outb"])
            moe_sp_all(sp, 1)
            after_meet(sp, num["moeb"])
            cmb_sp(sp, 1)

        @block.tensor
        def _(pe):
            ada_pe(pe)
            meet(pe, num["ada"])
            if STAGE < 2:
                return
            n1_pe(pe, 0)
            meet(pe, num["n1"])
            proj_pe(pe, pa)
            meet(pe, num["proj"])
            if STAGE < 3:
                return
            core_pe(pe)
            meet(pe, num["core"])
            proj_pe(pe, pb)
            meet(pe, num["projb"])
            if STAGE < 4:
                return
            meet(pe, num["toep"])
            att_pe(pe, na, "na")
            meet(pe, num["att"])
            if STAGE < 5:
                return
            out_pe(pe, 0)
            meet(pe, num["out"])
            route_pe(pe, 0)
            meet(pe, num["route"])
            if STAGE < 6:
                return
            moe_pe(pe, 0)
            meet(pe, num["moe"])
            meet(pe, num["cmb"])
            if STAGE < 7:
                return
            n1_pe(pe, 1)
            meet(pe, num["n1b"])
            proj_pe(pe, pc)
            meet(pe, num["projc"])
            att_pe(pe, sw, "sw")
            meet(pe, num["attb"])
            if STAGE < 8:
                return
            out_pe(pe, 1)
            meet(pe, num["outb"])
            route_pe(pe, 1)
            meet(pe, num["routeb"])
            moe_pe(pe, 1)
            meet(pe, num["moeb"])

        @block.scalar
        def _(act):
            ada_act(act)
            meet(act, num["ada"])
            if STAGE < 2:
                return
            n1_act(act, 0)
            meet(act, num["n1"])
            proj_act(act, pa)
            meet(act, num["proj"])
            if STAGE < 3:
                return
            core_act(act)
            meet(act, num["core"])
            proj_act(act, pb)
            meet(act, num["projb"])
            if STAGE < 4:
                return
            meet(act, num["toep"])
            att_act(act, na, "na")
            meet(act, num["att"])
            if STAGE < 5:
                return
            out_act(act, 0)
            meet(act, num["out"])
            route_act(act, 0)
            meet(act, num["route"])
            if STAGE < 6:
                return
            moe_act(act, 0)
            meet(act, num["moe"])
            meet(act, num["cmb"])
            if STAGE < 7:
                return
            n1_act(act, 1)
            meet(act, num["n1b"])
            proj_act(act, pc)
            meet(act, num["projc"])
            att_act(act, sw, "sw")
            meet(act, num["attb"])
            if STAGE < 8:
                return
            out_act(act, 1)
            meet(act, num["outb"])
            route_act(act, 1)
            meet(act, num["routeb"])
            moe_act(act, 1)
            meet(act, num["moeb"])
            cmb_act(act, 1)

        @block.vector
        def _(dve):
            ada_dve(dve)
            meet(dve, num["ada"])
            if STAGE < 2:
                return
            n1_dve(dve, 0)
            meet(dve, num["n1"])
            dve.wait_ge(*done("cos_in0", 16))
            proj_dve(dve, pa)
            meet(dve, num["proj"])
            if STAGE < 3:
                return
            scan(dve, nc.vector, 0)
            dve.wait_ge(*done("gain_in", 16))
            core_dve(dve)
            meet(dve, num["core"])
            proj_dve(dve, pb)
            meet(dve, num["projb"])
            if STAGE < 4:
                return
            dve.wait_ge(*done("toep_in", 32))
            tv = R(0, NAH * 18 * 64).rearrange("p (j c) -> p j c", c=64)
            nc.vector.scalar_tensor_tensor(out=tv, in0=tv, scalar=1.0 / SCALE, in1=bcast_mid(cst[:, C_COL:C_COL + 64], NAH * 18),
                                           op0=ALU.mult, op1=ALU.add).then_inc(S("toep"), 1)
            meet(dve, num["toep"])
            dve.wait_ge(*done("band_in0", 16))
            att_dve(dve, na, "na")
            meet(dve, num["att"])
            if STAGE < 5:
                return
            out_dve(dve, 0)
            meet(dve, num["out"])
            route_dve(dve, 0)
            meet(dve, num["route"])
            if STAGE < 6:
                return
            moe_dve(dve, 0)
            meet(dve, num["moe"])
            cmb_dve(dve, 0)
            meet(dve, num["cmb"])
            if STAGE < 7:
                return
            n1_dve(dve, 1)
            meet(dve, num["n1b"])
            dve.wait_ge(*done("cos_in1", 16))
            proj_dve(dve, pc)
            meet(dve, num["projc"])
            dve.wait_ge(*done("band_in1", 16))
            att_dve(dve, sw, "sw")
            meet(dve, num["attb"])
            if STAGE < 8:
                return
            out_dve(dve, 1)
            meet(dve, num["outb"])
            route_dve(dve, 1)
            meet(dve, num["routeb"])
            moe_dve(dve, 1)
            meet(dve, num["moeb"])
            cmb_dve(dve, 1)

        @block.gpsimd
        def _(pool):
            meet(pool, num["ada"])
            if STAGE < 2:
                return
            meet(pool, num["n1"])
            proj_pool(pool)
            meet(pool, num["proj"])
            if STAGE < 3:
                return
            scan(pool, nc.gpsimd, 1)
            meet(pool, num["core"])
            meet(pool, num["projb"])
            if STAGE < 4:
                return
            meet(pool, num["toep"])
            att_pool(pool, na, "na")
            meet(pool, num["att"])
            if STAGE < 5:
                return
            meet(pool, num["out"])
            route_pool(pool, 0)
            meet(pool, num["route"])
            if STAGE < 6:
                return
            moe_pool(pool, 0)
            meet(pool, num["moe"])
            cmb_pool(pool, 0)
            meet(pool, num["cmb"])
            if STAGE < 7:
                return
            meet(pool, num["n1b"])
            meet(pool, num["projc"])
            meet(pool, num["attb"])
            if STAGE < 8:
                return
            meet(pool, num["outb"])
            route_pool(pool, 1)
            meet(pool, num["routeb"])
            moe_pool(pool, 1)
            meet(pool, num["moeb"])
            cmb_pool(pool, 1)


_INS = ['x', 'c', 'ctx', 'c_ctx', 'ada_w', 'ada_b', 'norm_g', 'final_g', 'ab_w_in', 'ab_w_out', 'ret_decay', 'ret_gn',
        'na_rpb', 'swa_w_in', 'swa_w_out', 'swa_sink', 'router_g_w', 'router_g_b', 'router_e_w', 'router_e_b',
        'expert_w_gu', 'expert_w_down']
DBG = None


def kernel(**inputs):
    import numpy as _np
    import concourse.bacc as _bacc
    from concourse import mybir as _mybir
    from concourse.bass_utils import run_bass_kernel_spmd as _run

    nc = _bacc.Bacc("TRN2", target_bir_lowering=False, num_devices=1)
    arrays, args = {}, {}
    cst, band, rope = tables()
    for name, a in [(n, inputs[n]) for n in _INS] + [("cst", cst), ("band", band), ("rope", rope)]:
        a = _np.ascontiguousarray(a)
        arrays[f"in_{name}_dram"] = a
        args[name] = nc.dram_tensor(f"in_{name}_dram", a.shape, _mybir.dt.from_np(a.dtype), kind="ExternalInput").ap()
    if DBG:
        args["dbg"] = nc.dram_tensor("dbg", (P, 51456), F32, kind="ExternalOutput").ap()
    out = nc.dram_tensor("out_0_dram", (1, SEQ, D), F32, kind="ExternalOutput").ap()
    program(nc, args, out)
    r = _run(nc, [arrays], core_ids=[0])
    return r.results[0]["out_0_dram"]
```

```python
from contextlib import ExitStack

import numpy as np

import concourse.bass as bass
from concourse import mybir

ALU = mybir.AluOpType
ACT = mybir.ActivationFunctionType
AXX = mybir.AxisListType.X
F32 = mybir.dt.float32
I32 = mybir.dt.int32

P = 128
D = 1024
KC = D // P
SEQ = 1024
CTX = 256
XT = SEQ // P
CT = CTX // P
NT = XT + CT
TOK = SEQ + CTX
GRID_W = 64
HD = 64
SCALE = HD ** -0.5
NEG = -1e30
NAH = 8
SWH = 16
EXP = 32
GRP = 4
FF = 512
TOPK = 2
OVF = 2 * TOK // P
BLK = EXP + OVF
NLOG = GRP + EXP
EPS = 1e-6
GN_EPS = 1e-5
STAGE = 99

C_ID, C_RF, C_RB, C_DI, C_TRI, C_ONE = 0, 128, 256, 384, 512, 640
C_COL = 768
C_ROW = C_COL + 64
C_PQ = C_ROW + 80
C_PK = C_PQ + 16
C_IO = C_PK + 16
C_IG = C_IO + 32
C_TOK = C_IG + 32
C_HALF = C_TOK + NT
C_SL = C_HALF + 2
C_N = C_SL + P


def key_tiles(t):
    first = min(max(2 * t - 4, 0), 8) // 2
    last = (min(max(2 * t + 1 - 4, 0), 8) + 7) // 2
    return first, last - first + 1


def tables():
    c = np.zeros((P, C_N), np.float32)
    p = np.arange(P)
    c[:, C_ID:C_ID + P] = np.eye(P)
    rel = p[None, :] - p[:, None]
    c[:, C_RF:C_RF + P] = np.maximum(rel, 0)
    c[:, C_RB:C_RB + P] = np.maximum(-rel, 0)
    c[:, C_DI:C_DI + P] = (1 + np.eye(P)) * SCALE
    c[:, C_TRI:C_TRI + P] = p[:, None] < p[None, :]
    c[:, C_ONE:C_ONE + P] = 1
    qc = p % GRID_W
    kc = np.arange(GRID_W)[None, :]
    win = np.clip(qc - 8, 0, GRID_W - 16)[:, None]
    c[:, C_COL:C_COL + 64] = np.where((kc >= win) & (kc < win + 16), 0, NEG)
    for t in range(XT):
        r = 2 * t + p // GRID_W
        rs = np.clip(r - 4, 0, 8)[:, None]
        kr = 2 * key_tiles(t)[0] + np.arange(10)[None, :]
        c[:, C_ROW + 10 * t:C_ROW + 10 * t + 10] = np.where((kr >= rs) & (kr < rs + 8), 0, NEG)
    kk = np.arange(384)[None, :] - P
    band = np.zeros((P, 256 + 384 + 256), np.float32)
    band[:, 256:640] = np.where(np.abs(p[:, None] - kk) <= P, 0, NEG)
    for d in range(2):
        c[:, C_PQ + d:C_PQ + 16:2] = (p + 1 if d == 0 else P - p)[:, None]
        c[:, C_PK + d:C_PK + 16:2] = (P - 1 - p if d == 0 else p)[:, None]
    c[:, C_IO:C_IO + 32] = np.arange(32)
    c[:, C_IG:C_IG + 32] = np.arange(32) // 8
    c[:, C_TOK:C_TOK + NT] = np.arange(NT)[None, :] * P + p[:, None]
    c[:, C_SL:C_SL + P] = np.arange(P)
    c[:, C_HALF] = p < 64
    c[:, C_HALF + 1] = p >= 64
    inv = (np.float32(10000.0) ** (-np.arange(16, dtype=np.float32) / np.float32(16))).astype(np.float32)
    tok = np.arange(SEQ)
    ang = np.stack([(tok // GRID_W).astype(np.float32)[:, None] * inv,
                    (tok % GRID_W).astype(np.float32)[:, None] * inv], 1)
    cos, sin = np.cos(ang), np.sin(ang)
    rope = np.stack([np.stack([cos, cos], 2).reshape(SEQ, 64), np.stack([-sin, sin], 2).reshape(SEQ, 64)], 1)
    rope = rope.reshape(XT, P, P).transpose(1, 0, 2).reshape(P, XT * P)
    return c, band, np.ascontiguousarray(rope.astype(np.float32))


def program(nc, A, out):
    with ExitStack() as ctx:
        def sb(name, shape, dt=F32):
            return ctx.enter_context(nc.sbuf_tensor(name, shape, dt))

        def sem(name):
            return ctx.enter_context(nc.semaphore(name))

        def dram(name, shape, dt=F32):
            return nc.dram_tensor(name, shape, dt, kind="Internal").ap()

        SLOT0, ROWS, SLOT1, WR, TR, END = 10240, 20480, 23552, 35840, 44032, 51456
        ar = sb("ar", [P, END])
        cst = sb("cst", [P, C_N])
        colab = sb("colab", [P, 2, 2, 2, KC])
        dec = sb("dec", [P, 10, 16])
        ssq = sb("ssq", [P, 16])
        PS = ctx.enter_context(nc.psum_tensor("PS", [P, 8, 512], F32))

        def R(a, n):
            return ar[:, a:a + n]

        ident = cst[:, C_ID:C_ID + P]
        mod = dram("mod", (2, 2, 6 * D))
        h2d = dram("h2d", (TOK, D))
        yd = dram("yd", (BLK * P, D))
        rpbp = dram("rpbp", (NAH, 19, 127))
        skew = dram("skew", (GRID_W, NAH, 19, GRID_W))

        XR = R(0, NT * D).rearrange("p (t n) -> p t n", t=NT)
        hT = [R(0, KC * TOK).rearrange("p (k n) -> p k n", k=KC),
              R(SLOT0, KC * TOK).rearrange("p (k n) -> p k n", k=KC)]
        RG = R(10240, NT * 512).rearrange("p (t n) -> p t n", t=NT)
        NO = R(15360, NT * 512).rearrange("p (t n) -> p t n", t=NT)
        RV = NO
        QT = R(20480, 4 * TOK).rearrange("p (k n) -> p k n", k=4)
        KT = R(25600, 4 * TOK).rearrange("p (k n) -> p k n", k=4)
        ST = R(30720, NT * 512).rearrange("p (t n) -> p t n", t=NT)
        NV = ST
        QT1 = R(23552, 8 * SEQ).rearrange("p (k n) -> p k n", k=8)
        KT1 = R(31744, 2 * TOK).rearrange("p (k n) -> p k n", k=2)
        V1 = R(34304, NT * 256).rearrange("p (t n) -> p t n", t=NT)
        AO = R(10240, XT * D).rearrange("p (t n) -> p t n", t=XT)
        Wring = [[R(35840 + 4096 * i, 4096).rearrange("p (k n) -> p k n", k=KC) for i in range(2)],
                 [R(36864 + 4096 * i, 4096).rearrange("p (k n) -> p k n", k=KC) for i in range(2)]]
        COS = R(TR + 1024, 1024).rearrange("p (t f n) -> p t f n", t=XT, f=2)
        DM = R(TR, 1024)
        gain = R(TR + 6912, 512)
        xbuf = [R(TR + 2304 + 1024 * i, D) for i in range(3)]
        xn = [[R(TR + 5376 + 1024 * i, D) for i in range(2)], [R(ROWS + 1024 * i, D) for i in range(2)]]
        stages = {b: [R(b + 512 * i, 512) for i in range(2)] for b in (TR + 2304, TR + 1024)}
        rt1, rt2 = R(TR + 3328, 512), R(TR + 3840, 512)
        v2 = [R(TR + 4352 + 1024 * i, 1024) for i in range(2)]
        sm = [R(TR + 2304 + 1024 * i, 1024) for i in range(2)]
        txb = R(TR + 4352, 1024)
        ob, cb, sqb = R(TR + 5376, 512), R(TR + 5888, 512), R(TR + 6400, 512)
        run = [[sm[d][:, 256 * i:256 * i + 256] for i in range(2)] for d in range(2)]
        runt = [sm[d][:, 512:768] for d in range(2)]
        TOEP = R(0, NAH * 18 * 64).rearrange("p (h j c) -> p h j c", h=NAH, j=18)
        biasb = [R(TR + 3712 + 896 * i, 896) for i in range(2)]
        sxb = [[R(a, 896) for a in (TR, TR + 896, 9216)], [R(ROWS + 896 * i, 896) for i in range(3)]]
        ptb = [[R(TR + 5504 + 896 * i, 896) for i in range(2)], [R(18432 + 896 * i, 896) for i in range(2)]]
        atts = R(TR + 7168 + 150, 67)
        BAND = R(TR + 2304, 896)
        QZ = R(TR + 3200, 512).rearrange("p (half i n) -> p half i n", half=2, i=2)
        WO = [R(a, KC * D).rearrange("p (k n) -> p k n", k=KC) for a in (WR, WR + 1024)]
        rows = R(ROWS, 3 * D).rearrange("p (j n) -> p j n", j=3)
        tmpb = [[R(a + 512 * i, 512) for i in range(2)] for a in (TR, WR)]
        rw = R(TR + 1024, KC * NLOG).rearrange("p (k n) -> p k n", k=KC)
        rb = R(TR + 1312, NLOG)
        LG = R(TR + 1348, NT * NLOG).rearrange("p (t n) -> p t n", t=NT)
        junk = R(TR + 1708, D)
        PERS = TR + 7168
        wgt = R(PERS, 2 * NT).rearrange("p (j t) -> p j t", j=2)
        dsti = R(PERS + 20, 2 * NT).bitcast(I32).rearrange("p (j t) -> p j t", j=2)
        idx = R(PERS + 70, BLK).bitcast(I32)
        idxc = [R(PERS + 122 + i, 1).bitcast(I32) for i in range(2)]
        ctl = R(PERS + 124, 1 + OVF).bitcast(I32)
        mixT = [R(TR + 3072 + 1024 * i, D).rearrange("p (k n) -> p k n", k=KC) for i in range(2)]
        h2 = R(TR + 5120, D)
        h2T = R(TR + 6144, D).rearrange("p (k n) -> p k n", k=KC)
        slot = [SLOT1, SLOT0]
        wgu = [R(s, KC * D).rearrange("p (k n) -> p k n", k=KC) for s in slot]
        wdn = [R(s + KC * D, 4 * D).rearrange("p (k n) -> p k n", k=4) for s in slot]
        hb = [R(WR + 1024 * i, D) for i in range(2)]
        hbT = [R(WR + 2048 + 1024 * i, D).rearrange("p (k n) -> p k n", k=KC) for i in range(2)]
        sg = [R(WR + 4096 + 512 * i, 512) for i in range(2)]
        gub = [R(WR + 5120 + 512 * i, 512) for i in range(2)]
        guT = [R(TR + 3072 + 512 * i, 512).rearrange("p (k n) -> p k n", k=4) for i in range(2)]
        yb = [R(WR + 6144 + 1024 * i, D) for i in range(2)]
        yg = [[R(SLOT1 + 2048 * i + 1024 * j, D) for j in range(2)] for i in range(3)]
        cmb = R(SLOT1 + 6144, D)
        sqj = [R(34816, D), R(SLOT1 + 7168, D)]
        g2row = R(TR + 4352, 2 * D).rearrange("p (s n) -> p s n", s=2)
        fgrow = R(TR + 1024, D)
        outb = [R(SLOT0 + 1024 * i, D) for i in range(2)]

        names = {}

        shared = {}

        def share(names_, before, after, total):
            for x in names_:
                shared[x.format(after)] = (x.format(before), total)

        def S(name):
            if name in shared:
                return S(shared[name][0])
            if name not in names:
                names[name] = sem(name)
            return names[name]

        def done(name, count):
            at = name
            while at in shared:
                at, more = shared[at]
                count = count + more
            return S(name), count

        share(("ss{}", "n1_ms{}", "n1_rt{}", "n1_tr{}", "n1_ea{}", "n1_ed{}", "xn{}"), 0, 1, NT)
        share(("{}_s", "{}_bs", "{}_m", "{}_e", "{}_t", "{}_pt", "{}_v", "{}_qz"), "na", "sw", NT * NAH)
        share(("{}_o",), "na", "sw", NT)
        share(("{}_mt", "{}_me", "{}_h2", "{}_ht", "{}_he", "{}_r", "{}_lg", "{}_x", "{}_ss", "{}_ms", "{}_rt"), "o0", "o1", NT)
        share(("{}_mm", "{}_pe"), "o0", "o1", 2 * NT)
        share(("{}_rows",), "o0", "o1", 32)
        share(("{}_w",), "o0", "o1", 64)
        share(("{}_wo",), "o0", "o1", 16)
        share(("{}_h2o",), "o0", "o1", 16 * NT)
        share(("{}_ctl", "{}_c", "{}_mm", "{}_g", "{}_x", "{}_idx", "{}_st"), "r0", "r1", 1)
        share(("{}_e", "{}_pos"), "r0", "r1", 2)
        share(("{}_wg1", "{}_wd1", "{}_hb1", "{}_yo1"), "m0", "m1", 8 * EXP)
        share(("{}_g",), "c0", "c1", 32)
        share(("{}_used", "{}_sc", "{}_x"), "c0", "c1", NT)
        for q in range(3):
            share((f"{{}}_y{q}",), "c0", "c1", 32 * len(range(q, NT, 3)))

        chains = {}

        class Chain:

            def __init__(self, eng, name):
                self.eng, self.sem, self.n = eng, S(name), 0

            def __call__(self, ins):
                self.n += 1
                ins.then_inc(self.sem, 1)
                self.eng.wait_ge(self.sem, self.n)

        def chain(eng):
            key = str(eng.engine)
            if key not in chains:
                chains[key] = Chain(eng, "chain_" + key.split(".")[-1])
            return chains[key]

        def bcast_mid(ap, n):
            return ap.unsqueeze(1).to_broadcast([ap.shape[0], n, ap.shape[1]])

        def bcast_in(ap, n):
            return ap.unsqueeze(len(ap.shape)).to_broadcast(list(ap.shape) + [n])

        def meet(eng, k):
            eng.drain().then_inc(S("phase"), 1)
            eng.wait_ge(*done("phase", 4 * k))

        def after_meet(eng, k):
            eng.wait_ge(*done("phase", 4 * k))

        M_ADA, M_N1, M_PROJ, M_CORE, M_PROJB, M_ATT, M_OUT, M_ROUTE, M_MOE, M_CMB = range(1, 11)
        M2 = {0: 0, 1: 8}

        NADA = 12
        adaw = [R(a, 4096).rearrange("p (k n) -> p k n", k=KC) for a in (20480, 24576, 15360)]
        modrow = [ar[0:2, a:a + 6144] for a in (0, 28672)]
        ngrow = ar[0:2, 10240:10240 + 4 * D].rearrange("p (l j n) -> p l j n", l=2, j=2)
        cin = R(14336, 16).rearrange("p (s k) -> p s k", s=2)
        sT = R(14352, 16).rearrange("p (k s) -> p k s", k=KC)
        zero = R(6144, 2560)

        def ada_slot(l, c):
            return (c % 3, c // 3 + 1) if l == 0 else (c % 2, NADA // 3 + c // 2 + 1)

        def ada_bank(l, c):
            return c % 2 if l == 0 else 6 + c % 2

        def ada_load(sp, l, c):
            q, _ = ada_slot(l, c)
            if l == 0 and c >= 3:
                sp.wait_ge(*done("ada_mm", c - 2))
            if l == 1:
                sp.wait_ge(*done("ada_mm", NADA - 2 + c if c < 2 else NADA + c - 1))
            sp.dma_start(adaw[q], A["ada_w"][l].rearrange("(p k) n -> p k n", k=KC)[:, :, c * 512:c * 512 + 512])\
                .then_inc(S(f"ada_in{q}"), 16)

        def ada_out(sp, l):
            sp.wait_ge(*done("mod_rows", 4 * (l + 1)))
            sp.dma_start(mod[l], modrow[l]).then_inc(S("mod_out"), 16)
            sp.wait_ge(*done("mod_out", 16 * (l + 1)))
            for s in range(2):
                sp.dma_start(colab[:, l, s], mod[l, s, 0:2 * D].rearrange("(j p k) -> p j k", j=2, k=KC))\
                    .then_inc(S("cols_in"), 16)

        def ada_sp(sp):
            sp.dma_start(cin[:, 0, :], A["c"][0].rearrange("(p k) -> p k", k=KC)).then_inc(S("cond"), 16)
            sp.dma_start(cin[:, 1, :], A["c_ctx"].rearrange("(p k) -> p k", k=KC)).then_inc(S("cond"), 16)
            ada_load(sp, 0, 0)
            sp.dma_start(cst[:, :], A["cst"]).then_inc(S("consts"), 16)
            sp.dma_start(dec[:, 0, :].rearrange("p (d h) -> p d h", d=2),
                         A["ret_decay"][0].partition_broadcast(P)).then_inc(S("consts"), 16)
            sp.dma_start(ngrow, A["norm_g"].partition_broadcast(2)).then_inc(S("consts"), 16)
            for l in range(2):
                sp.dma_start(modrow[l], A["ada_b"][l].partition_broadcast(2)).then_inc(S("consts"), 16)
            for c in range(1, NADA):
                ada_load(sp, 0, c)
            for t in range(3):
                n1_load(sp, t)
            sp.wait_ge(*done("zeroed", 1))
            sp.dma_start(rpbp.rearrange("h a b -> h (a b)"), zero[0:NAH, 0:19 * 127]).then_inc(S("zeros_out"), 16)
            ada_load(sp, 1, 0)
            ada_load(sp, 1, 1)
            sp.wait_ge(*done("zeros_out", 16))
            ada_out(sp, 0)
            proj_sp(sp, pa, (0,))
            for t in range(3, NT + 3):
                if t < NT:
                    n1_load(sp, t)
                ada_load(sp, 1, t - 1)
            proj_sp(sp, pa, (1,))
            sp.dma_start(COS, A["rope"].rearrange("p (t f n) -> p t f n", t=XT, f=2)).then_inc(S("cos_in0"), 16)
            ada_out(sp, 1)
            sp.dma_start(rpbp[:, 2:17, 48:79], A["na_rpb"][0]).then_inc(S("rpb_out"), 16)
            sp.wait_ge(*done("rpb_out", 16))
            for h in range(NAH):
                src = bass.AP(tensor=rpbp.tensor, offset=h * 19 * 127 + 63, ap=[[127, 19], [-1, GRID_W], [1, GRID_W]])
                sp.dma_start(skew[:, h].rearrange("q j k -> j q k"), src).then_inc(S("skew_out"), 16)

        def ada_act(act):
            act.wait_ge(*done("cond", 32))
            nc.scalar.activation(sT.rearrange("p k s -> p s k"), cin, ACT.Silu).then_inc(S("silu_c"), 1)
            act.wait_ge(*done("consts", 16 * 5))
            ch = chain(act)
            E, U, LN, LGM = dec[:, 1], dec[:, 2], dec[:, 3], dec[:, 5]
            ch(nc.scalar.activation(E.rearrange("p (q r d) -> p q r d", q=2, r=4), dec[:, 0].rearrange("p (d r q) -> p q r d", d=2, r=4), ACT.Exp,
                                    scale=-float(np.log(2.0))))
            ch(nc.scalar.activation(U, E, ACT.Copy, scale=-1.0, bias=1.0))
            nc.scalar.activation(LN, U, ACT.Ln).then_inc(S("dec_ln"), 1)
            act.wait_ge(*done("dec_pos", 1))
            for j in (6, 7, 8):
                nc.scalar.activation(dec[:, j], dec[:, j], ACT.Exp)
            nc.scalar.activation(DM, DM, ACT.Exp).then_inc(S("dec_exp"), 1)

        def ada_product(pe, l, c):
            n, (q, fills) = l * NADA + c, ada_slot(l, c)
            pe.wait_ge(*done(f"ada_in{q}", 16 * fills))
            if n >= 2:
                pe.wait_ge(*done("ada_ev", n - 1))
            for k in range(KC):
                mm = nc.tensor.matmul(PS[0:2, ada_bank(l, c), :], sT[:, k, :], adaw[q][:, k, :],
                                      start=(k == 0), stop=(k == KC - 1))
            mm.then_inc(S("ada_mm"), 1)

        def ada_pe(pe):
            pe.wait_ge(*done("silu_c", 1))
            for c in range(NADA):
                ada_product(pe, 0, c)

        def ada_evict(dve, l, c):
            n = l * NADA + c
            dve.wait_ge(*done("ada_mm", n + 1))
            m = modrow[l][:, c * 512:c * 512 + 512]
            nc.vector.tensor_tensor(m, PS[0:2, ada_bank(l, c), :], m, ALU.add).then_inc(S("ada_ev"), 1)
            if c == NADA - 1:
                dve.wait_ge(*done("ada_ev", n + 1))
                for j in range(2):
                    m = modrow[l][:, (3 * j + 1) * D:(3 * j + 2) * D]
                    nc.vector.scalar_tensor_tensor(out=m, in0=m, scalar=1.0, in1=ngrow[:, l, j, :],
                                                   op0=ALU.add, op1=ALU.mult).then_inc(S("mod_rows"), 2)

        def ada_dve(dve):
            dve.wait_ge(*done("consts", 16 * 5))
            nc.vector.memset(zero, 0.0).then_inc(S("zeroed"), 1)
            ch = chain(dve)
            dve.wait_ge(*done("dec_ln", 1))
            E, U, LN, T, LGM = dec[:, 1], dec[:, 2], dec[:, 3], dec[:, 4], dec[:, 5]
            ch(nc.vector.tensor_scalar(T, U, -1.0, 1.0, ALU.mult, ALU.add))
            ch(nc.vector.tensor_scalar(dec[:, 9], T, 0.0, None, ALU.is_equal))
            ch(nc.vector.tensor_tensor(T, T, dec[:, 9], ALU.add))
            ch(nc.vector.reciprocal(T, T))
            ch(nc.vector.tensor_tensor(LN, LN, T, ALU.mult))
            ch(nc.vector.tensor_tensor(LN, LN, dec[:, 9], ALU.subtract))
            ch(nc.vector.tensor_tensor(LGM, LN, E, ALU.mult))
            nc.vector.tensor_tensor(dec[:, 6], LGM, cst[:, C_PQ:C_PQ + 16], ALU.mult)
            nc.vector.tensor_tensor(dec[:, 7], LGM, cst[:, C_PK:C_PK + 16], ALU.mult)
            nc.vector.tensor_scalar(dec[:, 8], LGM, float(P), None, ALU.mult)
            for h in range(8):
                last = nc.vector.tensor_scalar(DM[:, h * P:h * P + P], cst[:, C_RF:C_RF + P], LGM[:, 2 * h:2 * h + 1], None, ALU.mult)
            ch(last)
            for h in range(8):
                d = DM[:, h * P:h * P + P]
                last = nc.vector.scalar_tensor_tensor(out=d, in0=cst[:, C_RB:C_RB + P], scalar=LGM[:, 2 * h + 1:2 * h + 2],
                                                      in1=d, op0=ALU.mult, op1=ALU.add)
            last.then_inc(S("dec_pos"), 1)
            dve.wait_ge(*done("dec_exp", 1))
            DV = DM.rearrange("p (h n) -> p h n", h=8)
            ch(nc.vector.tensor_tensor(DV, DV, bcast_mid(cst[:, C_DI:C_DI + P], 8), ALU.mult))
            nc.vector.tensor_scalar(dec[:, 7], dec[:, 7], SCALE, None, ALU.mult)
            for q in range(2):
                half = slice(64 * q, 64 * q + 64)
                last = nc.vector.tensor_copy(dec[half, 9, 0:8].rearrange("p (r d) -> p r d", d=2),
                                             dec[half, 8, 8 * q:8 * q + 8].rearrange("p (r d) -> p r d", d=2))
            ch(last)
            for c in range(NADA):
                ada_evict(dve, 0, c)

        def n1_load(sp, t):
            if t >= 3:
                sp.wait_ge(*done("xn0", t - 2))
            src = A["x"][0, t * P:t * P + P] if t < XT else A["ctx"][0, (t - XT) * P:(t - XT + 1) * P]
            sp.dma_start(xbuf[t % 3], src).then_inc(S(f"x_in{t % 3}"), 16)

        def n1_src(l, t):
            return xbuf[t % 3] if l == 0 else XR[:, t, :]

        def n1_act(act, l):
            def squares(t):
                if l == 0:
                    act.wait_ge(*done(f"x_in{t % 3}", 16 * (t // 3 + 1)))
                nc.scalar.activation(sqj[l], n1_src(l, t), ACT.Square,
                                     accum_out=ssq[:, t:t + 1]).then_inc(S(f"ss{l}"), 1)

            def root(t):
                act.wait_ge(*done(f"n1_ms{l}", t + 1))
                nc.scalar.activation(ssq[:, t:t + 1], ssq[:, t:t + 1], ACT.Sqrt).then_inc(S(f"n1_rt{l}"), 1)

            def evict(t):
                act.wait_ge(*done(f"n1_tr{l}", t + 1))
                s = 0 if t < XT else 1
                for k in range(KC // 2):
                    last = nc.scalar.activation(hT[l][:, k, t * P:t * P + P], PS[:, 2 * (t % 2) + k // 4, (k % 4) * P:(k % 4 + 1) * P],
                                                ACT.Identity, bias=colab[:, l, s, 0, k:k + 1], scale=colab[:, l, s, 1, k:k + 1])
                last.then_inc(S(f"n1_ea{l}"), 1)
            scale = cmb_scale(act, 0)

            def ahead(t):
                if t < NT:
                    if l == 1:
                        if t + 1 < NT:
                            scale(t + 1)
                        act.wait_ge(*done("c0_x", t + 1))
                    squares(t)
                    root(t)
            if l == 1:
                scale(0)
            ahead(0)
            ahead(1)
            act.wait_ge(*done("cols_in", 32 * (l + 1)))
            evict(0)

            def before(i):
                ahead(i + 2)
                if i + 1 < NT:
                    evict(i + 1)
                if l == 0 and i == NT:
                    act.wait_ge(*done("mod_out", 32))
            proj_act(act, (pa, pc)[l], before=before)

        def n1_dve(dve, l):
            ch = chain(dve)

            def norm(t):
                r = ssq[:, t:t + 1]
                dve.wait_ge(*done(f"ss{l}", t + 1))
                nc.vector.tensor_scalar(r, r, 1.0 / D, EPS, ALU.mult, ALU.add).then_inc(S(f"n1_ms{l}"), 1)
                dve.wait_ge(*done(f"n1_rt{l}", t + 1))
                ch(nc.vector.reciprocal(r, r))
                if t >= 2:
                    dve.wait_ge(*done(f"n1_tr{l}", t - 1))
                nc.vector.tensor_scalar(xn[l][t % 2], n1_src(l, t), r, None, ALU.mult).then_inc(S(f"xn{l}"), 1)

            def evict(t):
                dve.wait_ge(*done(f"n1_tr{l}", t + 1))
                s = 0 if t < XT else 1
                for k in range(KC // 2, KC):
                    last = nc.vector.tensor_scalar(hT[l][:, k, t * P:t * P + P], PS[:, 2 * (t % 2) + k // 4, (k % 4) * P:(k % 4 + 1) * P],
                                                   colab[:, l, s, 1, k:k + 1], colab[:, l, s, 0, k:k + 1], ALU.mult, ALU.add)
                last.then_inc(S(f"n1_ed{l}"), 1)
            combine = cmb_tile(dve, 0)

            def ahead(t):
                if t < NT:
                    if l == 1:
                        combine(t)
                    norm(t)
            ahead(0)
            ahead(1)
            if l == 0:
                ada_evict(dve, 1, 0)
                ada_evict(dve, 1, 1)
            dve.wait_ge(*done("cols_in", 32 * (l + 1)))
            evict(0)

            def before(i):
                ahead(i + 2)
                if i + 1 < NT:
                    evict(i + 1)
                if l == 0 and i < NT:
                    ada_evict(dve, 1, i + 2)
                if i == (NT, 0)[l]:
                    dve.wait_ge(*done(f"cos_in{l}", 16))
            proj_dve(dve, (pa, pc)[l], before)

        def n1_pe(pe, l):
            def turn(t):
                pe.wait_ge(*done(f"xn{l}", t + 1))
                if t >= 2:
                    pe.wait_ge(*done(f"n1_ea{l}", t - 1))
                    pe.wait_ge(*done(f"n1_ed{l}", t - 1))
                xv = xn[l][t % 2].rearrange("p (m k) -> p k m", k=KC)
                for k in range(KC):
                    tr = nc.tensor.transpose(PS[:, 2 * (t % 2) + k // 4, (k % 4) * P:(k % 4 + 1) * P], xv[:, k, :], ident)
                tr.then_inc(S(f"n1_tr{l}"), 1)
            if l == 0:
                ada_product(pe, 1, 0)
                ada_product(pe, 1, 1)
            turn(0)

            def before(i):
                if i + 1 < NT:
                    turn(i + 1)
                if i < NT:
                    if l == 0:
                        ada_product(pe, 1, i + 2)
                    pe.wait_ge(*done(f"n1_ea{l}", i + 1))
                    pe.wait_ge(*done(f"n1_ed{l}", i + 1))
            proj_pe(pe, (pa, pc)[l], before)

        class Proj:
            def __init__(self, name, w, wring, kinds, l, before, stage=stages[TR + 2304], turned_banks=(6, 7)):
                self.stage, self.turned_banks = stage, turned_banks
                self.before = before
                self.name, self.w, self.ring, self.l = name, w, wring, l
                self.units, self.kinds = [], kinds
                n_act = n_dve = n_t = 0
                for c, (kind, col) in enumerate(kinds):
                    for t in range(XT if kind in ("q0", "q1") else NT):
                        rope = kind in ("rk", "rq", "q0", "q1", "kv") and t < XT
                        by_dve = rope or kind == "kv"
                        turned = kind not in ("rv", "rg", "nv")
                        u = dict(c=c, kind=kind, t=t, rope=rope, by_dve=by_dve, turned=turned, j=n_t)
                        if by_dve:
                            n_dve += 1
                            u["ev"] = (f"{name}_ed", n_dve)
                        else:
                            n_act += 1
                            u["ev"] = (f"{name}_ea", n_act)
                        n_t += turned
                        self.units.append(u)

            def loaded(self, c):
                return 16 * (self.before[c % 2] + c // 2 + 1)

            def last_of(self, c):
                return max(i for i, u in enumerate(self.units) if u["c"] == c)

        pa = Proj("pa", A["ab_w_in"][0], Wring[0], [("rv", 1024), ("rk", 512), ("rq", 0), ("rg", 1536)], 0, (0, 0))
        pb = Proj("pb", A["ab_w_in"][0], Wring[0], [("nk", 2560), ("nv", 3072), ("nq", 2048)], 0, (2, 2),
                  stage=stages[TR + 1024], turned_banks=(6,))
        pc = Proj("pc", A["swa_w_in"][0], Wring[1], [("kv", 1024), ("q0", 0), ("q1", 512)], 1, (4, 3))

        for before, after in ((pa, pb), (pb, pc)):
            a, b = before.name, after.name
            share(("{}_mm",), a, b, len(before.units))
            share(("{}_tr", "{}_te"), a, b, sum(u["turned"] for u in before.units))
            share(("{}_ed",), a, b, sum(u["by_dve"] for u in before.units))
            share(("{}_ea",), a, b, sum(not u["by_dve"] for u in before.units))

        def proj_sp(sp, pr, chunks=None):
            for c, (kind, col) in enumerate(pr.kinds):
                if chunks is not None and c not in chunks:
                    continue
                if c >= 2:
                    sp.wait_ge(*done(f"{pr.name}_mm", pr.last_of(c - 2) + 1))
                sp.dma_start(pr.ring[c % 2], pr.w.rearrange("(p k) n -> p k n", k=KC)[:, :, col:col + 512])\
                    .then_inc(S(f"w_in{c % 2}"), 16)

        def proj_pe(pe, pr, before=None, after=None):
            n, stage, nb = pr.name, pr.stage, len(pr.turned_banks)

            def turn(u):
                sname, cnt = u["ev"]
                pe.wait_ge(*done(sname, cnt))
                if u["j"] >= nb:
                    pe.wait_ge(*done(f"{n}_te", u["j"] - nb + 1))
                st = stage[u["j"] % 2]
                for r in range(2 if u["kind"] == "kv" else 4):
                    tr = nc.tensor.transpose(PS[:, pr.turned_banks[u["j"] % nb], r * P:r * P + P], st[:, r * P:r * P + P], ident)
                if u["kind"] == "rk":
                    tr.then_inc(S(f"{n}_tr"), 1)
                    t = u["t"]
                    pe.wait_ge(*done("v2", t + 1))
                    if t >= 2:
                        pe.wait_ge(*done("kv_ev", t - 1))
                    for h in range(8):
                        q = 64 * (h % 2)
                        mm = nc.tensor.matmul(PS[q:q + 64, t % 2, (h // 2) * P:(h // 2 + 1) * P], st[:, h * 64:h * 64 + 64],
                                              v2[t % 2][:, 64 * 8 * (h % 2) + (h // 2) * P:][:, 0:P], start=True, stop=True)
                    mm.then_inc(S("kv_mm"), 1)
                else:
                    tr.then_inc(S(f"{n}_tr"), 1)

            for i, u in enumerate(pr.units):
                if before:
                    before(i)
                if u["t"] == 0:
                    pe.wait_ge(*done(f"w_in{u['c'] % 2}", pr.loaded(u["c"])))
                if i >= 2:
                    pe.wait_ge(*done(pr.units[i - 2]["ev"][0], pr.units[i - 2]["ev"][1]))
                for k in range(KC):
                    mm = nc.tensor.matmul(PS[:, 4 + i % 2, :], hT[pr.l][:, k, u["t"] * P:u["t"] * P + P],
                                          pr.ring[u["c"] % 2][:, k, :], start=(k == 0), stop=(k == KC - 1))
                mm.then_inc(S(f"{n}_mm"), 1)
                if i and pr.units[i - 1]["turned"]:
                    turn(pr.units[i - 1])
                if after:
                    after(i)
            if pr.units[-1]["turned"]:
                turn(pr.units[-1])

        def stage_free(eng, n, j, kind_before):
            if j >= 2:
                eng.wait_ge(*done(f"{n}_tr", j - 1))
            if kind_before is not None:
                eng.wait_ge(*done("kv_mm", kind_before))

        def kv_before(pr, i):
            j, seen = pr.units[i]["j"], 0
            for u in pr.units[:i]:
                if u["turned"] and u["j"] <= j - 2 and u["kind"] == "rk":
                    seen = u["t"] + 1
            return seen or None

        def proj_act(act, pr, before=None):
            n, stage, nb = pr.name, pr.stage, len(pr.turned_banks)

            def evict(i, u):
                act.wait_ge(*done(f"{n}_mm", i + 1))
                src, t = PS[:, 4 + i % 2, :], u["t"]
                if u["turned"]:
                    stage_free(act, n, u["j"], kv_before(pr, i))
                    ins = nc.scalar.activation(stage[u["j"] % 2], src, ACT.Copy)
                elif u["kind"] == "rg":
                    ins = nc.scalar.activation(RG[:, t, :], src, ACT.Silu)
                else:
                    ins = nc.scalar.activation((RV if u["kind"] == "rv" else NV)[:, t, :], src, ACT.Copy)
                ins.then_inc(S(f"{n}_ea"), 1)

            def evict_turned(u):
                act.wait_ge(*done(f"{n}_tr", u["j"] + 1))
                t, src = u["t"], PS[:, pr.turned_banks[u["j"] % nb], :]
                cols = slice(t * P, t * P + P)
                k = u["kind"]
                if k == "kv":
                    dst, src = KT1[:, :, cols], src[:, 0:256].rearrange("p (r n) -> p r n", r=2)
                else:
                    dst = QT1[:, 4 * (k == "q1"):4 * (k == "q1") + 4, cols] if k[0] == "q" else \
                        (KT if k[1] == "k" else QT)[:, :, cols]
                    src = src.rearrange("p (r n) -> p r n", r=4)
                nc.scalar.activation(dst, src, ACT.Copy).then_inc(S(f"{n}_te"), 1)
                if k == "rk":
                    act.wait_ge(*done("kv_mm", t + 1))
                    nc.scalar.activation(ST[:, t, :], PS[:, t % 2, :], ACT.Copy).then_inc(S("kv_ev"), 1)

            for i, u in enumerate(pr.units):
                if before:
                    before(i)
                if not u["by_dve"]:
                    evict(i, u)
                if i and pr.units[i - 1]["turned"]:
                    evict_turned(pr.units[i - 1])
            if pr.units[-1]["turned"]:
                evict_turned(pr.units[-1])

        def proj_dve(dve, pr, before=None):
            n, stage = pr.name, pr.stage
            ch = chain(dve)
            for i, u in enumerate(pr.units):
                if before:
                    before(i)
                if not u["by_dve"]:
                    continue
                dve.wait_ge(*done(f"{n}_mm", i + 1))
                nh = 4 if u["kind"] == "kv" else 8
                src = PS[:, 4 + i % 2, :]
                st = stage[u["j"] % 2]
                if u["kind"] == "kv":
                    nc.vector.tensor_copy(V1[:, u["t"], :], src[:, 256:512])
                if u["rope"]:
                    w = nh * 64
                    c, s = COS[:, u["t"], 0, :], COS[:, u["t"], 1, :]
                    sv = src[:, 0:w].rearrange("p (h a f i) -> p h a f i", h=nh, a=2, f=2)
                    tv = rt2[:, 0:w].rearrange("p (h a f i) -> p h a f i", h=nh, a=2, f=2)
                    s4 = s.rearrange("p (a f i) -> p a f i", a=2, f=2)
                    nc.vector.tensor_tensor(rt1[:, 0:w].rearrange("p (h n) -> p h n", h=nh), src[:, 0:w].rearrange("p (h n) -> p h n", h=nh),
                                            bcast_mid(c, nh), ALU.mult)
                    for f in range(2):
                        last = nc.vector.tensor_tensor(tv[:, :, :, f, :], sv[:, :, :, 1 - f, :],
                                                       s4[:, :, f, :].unsqueeze(1).to_broadcast([P, nh, 2, 16]), ALU.mult)
                    ch(last)
                    stage_free(dve, n, u["j"], kv_before(pr, i))
                    if u["kind"] == "kv":
                        ins = nc.vector.tensor_tensor(st[:, 0:w], rt1[:, 0:w], rt2[:, 0:w], ALU.add)
                    elif u["kind"] in ("q0", "q1"):
                        by = lambda a: a.rearrange("p (j g d) -> p j g d", j=2, g=4)
                        ins = nc.vector.tensor_tensor(st.rearrange("p (g j d) -> p j g d", g=4, j=2), by(rt1), by(rt2), ALU.add)
                    else:
                        ins = nc.vector.tensor_tensor(st, rt1, rt2, ALU.add)
                else:
                    stage_free(dve, n, u["j"], kv_before(pr, i))
                    ins = nc.vector.tensor_copy(st[:, 0:256], src[:, 0:256])
                ins.then_inc(S(f"{n}_ed"), 1)
                if u["rope"]:
                    dve.wait_ge(*done(f"{n}_ed", u["ev"][1]))

        def proj_pool(pool):
            pool.wait_ge(*done("n1_tr0", NT))
            for t in range(NT):
                pool.wait_ge(*done("pa_ea", t + 1))
                if t >= 2:
                    pool.wait_ge(*done("kv_mm", t - 1))
                for q in range(2):
                    kd = dec[:, 7, 8 * q:8 * q + 8].rearrange("p (r d) -> p r d", d=2)
                    vv = RV[:, t, :].rearrange("p (r q e) -> p r q e", r=4, q=2)[:, :, q, :]
                    last = nc.gpsimd.tensor_tensor(v2[t % 2][:, 512 * q:512 * q + 512].rearrange("p (r d e) -> p r d e", r=4, d=2),
                                                   vv.unsqueeze(2).to_broadcast([P, 4, 2, 64]), bcast_in(kd, 64), ALU.mult)
                last.then_inc(S("v2"), 1)

        def scan(eng, ne, d):
            ch = chain(eng)
            eng.wait_ge(*done("kv_ev", NT))
            eng.wait_ge(*done("pa_tr", 2 * NT))
            seq = [8, 9] + list(range(XT)) if d == 0 else [9, 8] + list(range(XT - 1, -1, -1))
            cd = dec[:, 9, 0:8].rearrange("p (r d) -> p r d", d=2)[:, :, d]
            ch(ne.memset(run[d][0], 0.0))
            for i, t in enumerate(seq):
                old, new = run[d][i % 2].rearrange("p (r e) -> p r e", r=4), run[d][1 - i % 2].rearrange("p (r e) -> p r e", r=4)
                st = ST[:, t, :].rearrange("p (r d e) -> p r d e", r=4, d=2)[:, :, d, :]
                tmp = runt[d].rearrange("p (r e) -> p r e", r=4)
                if i < NT - 1:
                    ch(ne.tensor_tensor(tmp, old, bcast_in(cd, 64), ALU.mult))
                    ch(ne.tensor_tensor(new, tmp, st, ALU.add))
                ch(ne.tensor_copy(st, old))
            eng.drain().then_inc(S("states"), 1)

        def core_pe(pe):
            def scores(t):
                if t >= 1:
                    pe.wait_ge(*done("sm", t))
                for h in range(8):
                    q, r = 64 * (h % 2), h // 2
                    mm = nc.tensor.matmul(PS[:, h % 2, r * P:r * P + P], KT[q:q + 64, r, t * P:t * P + P],
                                          QT[q:q + 64, r, t * P:t * P + P], start=True, stop=True)
                mm.then_inc(S("core_s"), 1)

            def cross(t):
                if t >= 1:
                    pe.wait_ge(*done("tx", t))
                for h in range(8):
                    q, r = 64 * (h % 2), h // 2
                    mm = nc.tensor.matmul(PS[:, 2 + h % 2, r * P:r * P + P], QT[q:q + 64, r, t * P:t * P + P],
                                          ST[q:q + 64, t, r * P:r * P + P], start=True, stop=True)
                mm.then_inc(S("core_x"), 1)

            def inner(t):
                pe.wait_ge(*done("sm", t + 1))
                if t >= 1:
                    pe.wait_ge(*done("core_o1", t))
                for h in range(8):
                    mm = nc.tensor.matmul(PS[:, 7, h * 64:h * 64 + 64], sm[t % 2][:, (h % 2) * 512 + (h // 2) * P:][:, 0:P],
                                          RV[:, t, h * 64:h * 64 + 64], start=True, stop=True)
                mm.then_inc(S("core_o"), 1)
            pe.wait_ge(*done("states", 2))

            def before(i):
                if i < NT:
                    scores(i)
                    cross(i)

            def after(i):
                if i < NT:
                    inner(i)
            proj_pe(pe, pb, before, after)

        def core_dve(dve):
            ch = chain(dve)
            mu, var = ssq[:, 0:8], ssq[:, 8:16]
            H = lambda a: a.rearrange("p (h e) -> p h e", h=8)
            dve.wait_ge(*done("states", 2))

            def decay(t):
                dve.wait_ge(*done("core_s", t + 1))
                if t >= 2:
                    dve.wait_ge(*done("core_o", t - 1))
                nc.vector.tensor_tensor(sm[t % 2], PS[:, 0:2, :].rearrange("p b n -> p (b n)"), DM, ALU.mult).then_inc(S("sm"), 1)
            decay(0)
            for t in range(NT):
                dve.wait_ge(*done("core_x", t + 1))
                nc.vector.tensor_tensor(txb.rearrange("p (h e) -> p h e", e=64),
                                        PS[:, 2:4, :].rearrange("p b (h e) -> p (b h) e", e=64),
                                        bcast_in(dec[:, 6], 64), ALU.mult).then_inc(S("tx"), 1)
                dve.wait_ge(*done("tx", t + 1))
                dve.wait_ge(*done("core_o", t + 1))
                tx4 = txb.rearrange("p (q r d e) -> p r q d e", q=2, r=4, d=2)
                ob4 = ob.rearrange("p (r q e) -> p r q e", r=4, q=2)
                nc.vector.tensor_tensor(ob4, PS[:, 7, :].rearrange("p (r q e) -> p r q e", r=4, q=2), tx4[:, :, :, 0, :], ALU.add).then_inc(S("core_o1"), 1)
                dve.wait_ge(*done("core_o1", t + 1))
                ch(nc.vector.tensor_tensor(ob4, ob4, tx4[:, :, :, 1, :], ALU.add))
                ch(nc.vector.tensor_reduce(mu, H(ob), AXX, ALU.add))
                ch(nc.vector.tensor_scalar(mu, mu, 1.0 / HD, None, ALU.mult))
                nc.vector.tensor_tensor(H(cb), H(ob), bcast_in(mu, 64), ALU.subtract).then_inc(S("core_c"), 1)
                if t + 1 < NT:
                    decay(t + 1)
                dve.wait_ge(*done("core_sq", t + 1))
                ch(nc.vector.tensor_reduce(var, H(sqb), AXX, ALU.add))
                nc.vector.tensor_scalar(var, var, 1.0 / HD, GN_EPS, ALU.mult, ALU.add).then_inc(S("core_v"), 1)
                dve.wait_ge(*done("core_rt", t + 1))
                ch(nc.vector.reciprocal(var, var))
                ch(nc.vector.tensor_tensor(H(cb), H(cb), bcast_in(var, 64), ALU.mult))
                ch(nc.vector.tensor_tensor(cb, cb, gain, ALU.mult))
                ch(nc.vector.tensor_tensor(RG[:, t, :], RG[:, t, :], cb, ALU.mult))

        def core_act(act):
            def normalise(t):
                act.wait_ge(*done("core_c", t + 1))
                nc.scalar.activation(sqb, cb, ACT.Square).then_inc(S("core_sq"), 1)
                act.wait_ge(*done("core_v", t + 1))
                nc.scalar.activation(ssq[:, 8:16], ssq[:, 8:16], ACT.Sqrt).then_inc(S("core_rt"), 1)

            def before(i):
                if 1 <= i <= NT:
                    normalise(i - 1)
            proj_act(act, pb, before=before)

        def units_na():
            us = []
            for t in range(XT):
                b, nb = key_tiles(t)
                for h in range(NAH):
                    q, r = h % 2, h // 2
                    us.append(dict(
                        layer=0, half=q, q=QT[:, r, t * P:t * P + P],
                        ks=[(KT[:, r, SEQ:TOK], 0), (KT[:, r, b * P:b * P + 256], 256), (KT[:, r, b * P + 256:(b + nb) * P], 512)],
                        n=256 + nb * P, nbias=(h, 2 * b - 2 * t + 8, t, 2 * nb), bias=None, sink=None,
                        vs=[NV[:, kt, h * 64:h * 64 + 64] for kt in [8, 9] + list(range(b, b + nb))],
                        h=h, out=NO[:, t, :]))
            for t in range(XT, NT):
                for h in range(NAH):
                    q, r = h % 2, h // 2
                    us.append(dict(layer=0, half=q, q=QT[:, r, t * P:t * P + P], ks=[(KT[:, r, SEQ:TOK], 0)], n=256, nbias=None,
                                   bias=BAND[:, 0:256], sink=None, vs=[NV[:, kt, h * 64:h * 64 + 64] for kt in (8, 9)],
                                   h=h, out=NO[:, t, :]))
            return us

        def units_swa():
            us = []
            for t in range(XT):
                lo, hi = max(t - 1, 0), min(t + 1, XT - 1)
                loc = (hi - lo + 1) * P
                for h in range(SWH):
                    kv = h // 4
                    r = kv // 2
                    near = KT1[:, r, lo * P:hi * P + P]
                    if t == XT - 1:
                        ks, mcol, kts = [(KT1[:, r, SEQ:TOK], 0), (near, 256)], 0, [8, 9, lo, hi]
                    elif t == 0:
                        ks, mcol, kts = [(near, 0), (KT1[:, r, SEQ:TOK], 256)], 256 + P, [lo, hi, 8, 9]
                    else:
                        ks = [(near, 0), (KT1[:, r, SEQ:SEQ + P], 384), (KT1[:, r, SEQ + P:TOK], 512)]
                        mcol, kts = 256, [lo, t, hi, 8, 9]
                    us.append(dict(layer=1, half=kv % 2, q=QT1[:, 4 * (h // 8) + h % 4, t * P:t * P + P], ks=ks, n=loc + 256, nbias=None,
                                   bias=BAND[:, mcol:mcol + loc + 256], sink=h,
                                   vs=[V1[:, kt, kv * 64:kv * 64 + 64] for kt in kts],
                                   h=h % 8, out=AO[:, t, (h // 8) * 512:(h // 8) * 512 + 512]))
            return us

        nmax = atts[:, 0:16].rearrange("p (g h) -> p g h", g=2)
        sums = atts[:, 16:32].rearrange("p (g h) -> p g h", g=2)
        sinkr = atts[:, 32:48]
        sinke = atts[:, 48:64].rearrange("p (g h) -> p g h", g=2)
        amx = atts[:, 64:67]

        def psS(i, a, b):
            return PS[:, 2 * (i % 2):2 * (i % 2) + 2, :].rearrange("p b n -> p (b n)")[:, a:b]

        PT2 = PS[:, 4:6, :].rearrange("p b n -> p (b n)")

        def number_queries(us):
            of = ([], [])
            for i, u in enumerate(us):
                same = of[u["half"]]
                u["qz"] = QZ[:, u["half"], len(same) % 2, :]
                u["user"] = same[-2] if len(same) >= 2 else None
                same.append(i)

        def att_pool(pool, us, n):
            for i, u in enumerate(us):
                if u["user"] is not None:
                    pool.wait_ge(*done(f"{n}_s", u["user"] + 1))
                nc.gpsimd.tensor_scalar(u["qz"], u["q"], cst[:, C_HALF + u["half"]:C_HALF + u["half"] + 1], None, ALU.mult)\
                    .then_inc(S(f"{n}_qz"), 1)
                if u["nbias"] is None:
                    continue
                h, j0, t, rows_ = u["nbias"]
                if i < NAH:
                    pool.wait_ge(*done("toep", i + 1))
                if i == 0:
                    for b in biasb:
                        nc.gpsimd.memset(b[:, 0:256], 0.0)
                if i >= 2:
                    pool.wait_ge(*done(f"{n}_bs", i - 1))
                nc.gpsimd.tensor_tensor(biasb[i % 2][:, 256:256 + 64 * rows_].rearrange("p (j c) -> p j c", c=64), TOEP[:, h, j0:j0 + rows_, :],
                                        bcast_in(cst[:, C_ROW + 10 * t:C_ROW + 10 * t + rows_], 64), ALU.add).then_inc(S(f"{n}_bias"), 1)

        def att_pe(pe, us, n):
            def scores(i):
                u = us[i]
                if i >= 2:
                    pe.wait_ge(*done(f"{n}_bs", i - 1))
                pe.wait_ge(*done(f"{n}_qz", i + 1))
                for k, c in u["ks"]:
                    mm = nc.tensor.matmul(psS(i, c, c + k.shape[1]), u["qz"], k, start=True, stop=True)
                mm.then_inc(S(f"{n}_s"), 1)

            def turn(i):
                pe.wait_ge(*done(f"{n}_e", i + 1))
                if i >= 1:
                    pe.wait_ge(*done(f"{n}_pt", i))
                for c in range(us[i]["n"] // P):
                    tr = nc.tensor.transpose(PT2[:, c * P:c * P + P], sxb[us[0]["layer"]][i % 3][:, c * P:c * P + P], ident)
                tr.then_inc(S(f"{n}_t"), 1)

            def values(i):
                u, g = us[i], i // 8
                pe.wait_ge(*done(f"{n}_pt", i + 1))
                if i % 8 == 0 and g >= 2:
                    pe.wait_ge(*done(f"{n}_o", g - 1))
                m = len(u["vs"])
                for c, v in enumerate(u["vs"]):
                    mm = nc.tensor.matmul(PS[:, 6 + g % 2, u["h"] * 64:u["h"] * 64 + 64], ptb[us[0]["layer"]][i % 2][:, c * P:c * P + P], v,
                                          start=(c == 0), stop=(c == m - 1))
                mm.then_inc(S(f"{n}_v"), 1)
            for i in range(len(us) + 3):
                if i < len(us):
                    scores(i)
                if 2 <= i < len(us) + 2:
                    turn(i - 2)
                if i >= 3:
                    values(i - 3)

        def att_dve(dve, us, n):
            ch = chain(dve)

            def soft(i):
                u, g = us[i], i // 8
                nb = sum(1 for v in us[:i + 1] if v["nbias"] is not None)
                dve.wait_ge(*done(f"{n}_s", i + 1))
                if i >= 3:
                    dve.wait_ge(*done(f"{n}_t", i - 2))
                x = sxb[us[0]["layer"]][i % 3]
                if u["nbias"] is not None:
                    dve.wait_ge(*done(f"{n}_bias", nb))
                b = biasb[(nb - 1) % 2] if u["nbias"] is not None else u["bias"]
                m = amx[:, i % 3:i % 3 + 1]
                if i >= 3:
                    dve.wait_ge(*done(f"{n}_m", i - 2))
                nc.vector.tensor_tensor_reduce(out=x[:, 0:u["n"]], in0=psS(i, 0, u["n"]), in1=b[:, 0:u["n"]], scale=SCALE, scalar=-3e38,
                                               op0=ALU.add, op1=ALU.max, accum_out=m).then_inc(S(f"{n}_bs"), 1)
                dve.wait_ge(*done(f"{n}_bs", i + 1))
                if i % 8 == 0 and g >= 2:
                    dve.wait_ge(*done(f"{n}_o", g - 1))
                nm = nmax[:, g % 2, u["h"]:u["h"] + 1]
                if u["sink"] is None:
                    ins = nc.vector.tensor_scalar(nm, m, -1.0, None, ALU.mult)
                else:
                    ins = nc.vector.tensor_scalar(nm, m, sinkr[:, u["sink"]:u["sink"] + 1], -1.0, ALU.max, ALU.mult)
                ins.then_inc(S(f"{n}_m"), 1)
                if u["sink"] is not None and i % 8 == 7:
                    dve.wait_ge(*done(f"{n}_m", i + 1))
                    hs = u["sink"] - 7
                    nc.vector.tensor_tensor(sinke[:, g % 2, :], nmax[:, g % 2, :], sinkr[:, hs:hs + 8], ALU.add).then_inc(S(f"{n}_ks"), 1)

            def table(h):
                dve.wait_ge(*done(f"toep_in{h % 2}", 32 * (h // 2 + 1)))
                nc.vector.scalar_tensor_tensor(out=TOEP[:, h], in0=TOEP[:, h], scalar=1.0 / SCALE, in1=bcast_mid(cst[:, C_COL:C_COL + 64], 18),
                                               op0=ALU.mult, op1=ALU.add).then_inc(S("toep"), 1)

            def finish(g):
                u = us[8 * g]
                dve.wait_ge(*done(f"{n}_e", 8 * g + 8))
                s = sums[:, g % 2, :]
                if u["sink"] is not None:
                    dve.wait_ge(*done(f"{n}_ke", g + 1))
                    ch(nc.vector.tensor_tensor(s, s, sinke[:, g % 2, :], ALU.add))
                ch(nc.vector.reciprocal(s, s))
                dve.wait_ge(*done(f"{n}_v", 8 * g + 8))
                nc.vector.tensor_tensor(u["out"].rearrange("p (h e) -> p h e", h=8), PS[:, 6 + g % 2, :].rearrange("p (h e) -> p h e", h=8),
                                        bcast_in(s, 64), ALU.mult).then_inc(S(f"{n}_o"), 1)
                dve.wait_ge(*done(f"{n}_o", g + 1))
            if us[0]["sink"] is not None:
                dve.wait_ge(*done("sink_in", 16))
            if us[0]["layer"] == 0:
                table(0)
            for i in range(len(us)):
                if us[0]["layer"] == 0 and i + 1 < NAH:
                    table(i + 1)
                soft(i)
                if i % 8 == 3 and i > 8:
                    finish(i // 8 - 1)
            finish(len(us) // 8 - 1)

        def att_act(act, us, n):
            def evict(i):
                act.wait_ge(*done(f"{n}_t", i + 1))
                if i >= 2:
                    act.wait_ge(*done(f"{n}_v", i - 1))
                nc.scalar.activation(ptb[us[0]["layer"]][i % 2][:, 0:us[i]["n"]], PT2[:, 0:us[i]["n"]], ACT.Copy).then_inc(S(f"{n}_pt"), 1)

            def exps(i):
                u, g = us[i], i // 8
                act.wait_ge(*done(f"{n}_m", i + 1))
                if i % 8 == 0 and g >= 2:
                    act.wait_ge(*done(f"{n}_o", g - 1))
                x = sxb[us[0]["layer"]][i % 3][:, 0:u["n"]]
                nc.scalar.activation(x, x, ACT.Exp, bias=nmax[:, g % 2, u["h"]:u["h"] + 1],
                                     accum_out=sums[:, g % 2, u["h"]:u["h"] + 1]).then_inc(S(f"{n}_e"), 1)
                if u["sink"] is not None and i % 8 == 7:
                    act.wait_ge(*done(f"{n}_ks", g + 1))
                    nc.scalar.activation(sinke[:, g % 2, :], sinke[:, g % 2, :], ACT.Exp).then_inc(S(f"{n}_ke"), 1)
            for i in range(len(us) + 2):
                if i >= 2:
                    evict(i - 2)
                if i < len(us):
                    exps(i)

        def out_tiles(l):
            return ([8, 9] + list(range(XT))) if l == 0 else list(range(XT))

        def out_weights(sp, l):
            w = A["ab_w_out"][0] if l == 0 else A["swa_w_out"][0]
            sp.dma_start(WO[l], w.rearrange("(k p) n -> p k n", p=P)).then_inc(S(f"o{l}_wo"), 16)

        def out_sp(sp, l):
            n = f"o{l}"
            with nc.allow_non_contiguous_dma("the router's weights, of few columns"):
                sp.dma_start(rw[:, :, 0:GRP], A["router_g_w"][l].rearrange("(k p) n -> p k n", p=P)).then_inc(S(f"{n}_w"), 16)
                sp.dma_start(rw[:, :, GRP:NLOG], A["router_e_w"][l].rearrange("(k p) n -> p k n", p=P)).then_inc(S(f"{n}_w"), 16)
            sp.dma_start(rb[:, 0:GRP], A["router_g_b"][l].partition_broadcast(P)).then_inc(S(f"{n}_w"), 16)
            sp.dma_start(rb[:, GRP:NLOG], A["router_e_b"][l].partition_broadcast(P)).then_inc(S(f"{n}_w"), 16)

            def load_rows(s):
                sp.dma_start(rows[:, 0:3, :], mod[l, s, 2 * D:5 * D].rearrange("(j n) -> j n", j=3).partition_broadcast(P))\
                    .then_inc(S(f"{n}_rows"), 16)
            if l == 0:
                load_rows(1)
                sp.dma_start(XR[:, XT:NT, :], A["ctx"][0].rearrange("(t p) n -> p t n", p=P)).then_inc(S("o0_ctx_in"), 16)
                sp.dma_start(XR[:, 0:XT, :], A["x"][0].rearrange("(t p) n -> p t n", p=P)).then_inc(S("o0_x_in"), 16)
            else:
                load_rows(0)
            moe_load(sp, l)(0, 0)
            for i, t in enumerate(out_tiles(l)):
                sp.wait_ge(*done(f"{n}_h2", i + 1))
                sp.dma_start(h2d[t * P:t * P + P, :], h2).then_inc(S(f"{n}_h2o"), 16)
                if l == 0 and i == 1:
                    load_rows(0)
            sp.wait_ge(*done(f"{n}_h2o", 16 * len(out_tiles(l))))

        def out_pe(pe, l):
            n, ts = f"o{l}", out_tiles(l)

            def mix(i, k):
                if l == 1:
                    return AO[:, ts[i], k * P:k * P + P]
                return (RG if k < 4 else NO)[:, ts[i], (k % 4) * P:(k % 4 + 1) * P]

            def turn(i):
                if i >= 1:
                    pe.wait_ge(*done(f"{n}_me", i))
                for k in range(KC):
                    tr = nc.tensor.transpose(PS[:, k // 4, (k % 4) * P:(k % 4 + 1) * P], mix(i, k), ident)
                tr.then_inc(S(f"{n}_mt"), 1)

            def product(i):
                pe.wait_ge(*done(f"{n}_me", i + 1))
                pe.wait_ge(*done(f"{n}_wo", 16))
                for half in range(2):
                    if i >= 1:
                        pe.wait_ge(*done(f"{n}_pe", 2 * (i - 1) + half + 1))
                    for k in range(KC):
                        mm = nc.tensor.matmul(PS[:, 2 + half, :], mixT[i % 2][:, k, :], WO[l][:, k, half * 512:half * 512 + 512],
                                              start=(k == 0), stop=(k == KC - 1))
                    mm.then_inc(S(f"{n}_mm"), 1)

            def turn2(i):
                pe.wait_ge(*done(f"{n}_h2", i + 1))
                if i >= 1:
                    pe.wait_ge(*done(f"{n}_he", i))
                for k in range(KC):
                    tr = nc.tensor.transpose(PS[:, 6 + k // 4, (k % 4) * P:(k % 4 + 1) * P], h2[:, k * P:k * P + P], ident)
                tr.then_inc(S(f"{n}_ht"), 1)

            def router(i):
                pe.wait_ge(*done(f"{n}_w", 64))
                pe.wait_ge(*done(f"{n}_he", i + 1))
                if i >= 2:
                    pe.wait_ge(*done(f"{n}_lg", i - 1))
                for k in range(KC):
                    mm = nc.tensor.matmul(PS[:, 4 + i % 2, 0:NLOG], h2T[:, k, :], rw[:, k, :], start=(k == 0), stop=(k == KC - 1))
                mm.then_inc(S(f"{n}_r"), 1)
            turn(0)
            for i in range(len(ts) + 2):
                if i + 1 < len(ts):
                    turn(i + 1)
                if i < len(ts):
                    product(i)
                if i >= 2:
                    router(i - 2)
                if 1 <= i <= len(ts):
                    turn2(i - 1)

        def out_act(act, l):
            n, ts = f"o{l}", out_tiles(l)

            def evict_mix(i):
                act.wait_ge(*done(f"{n}_mt", i + 1))
                if i >= 2:
                    act.wait_ge(*done(f"{n}_mm", 2 * (i - 1)))
                nc.scalar.activation(mixT[i % 2].rearrange("p k n -> p (k n)"), PS[:, 0:2, :].rearrange("p b n -> p (b n)"), ACT.Copy)\
                    .then_inc(S(f"{n}_me"), 1)

            def stats(i):
                act.wait_ge(*done(f"{n}_x", i + 1))
                nc.scalar.activation(junk, XR[:, ts[i], :], ACT.Square, accum_out=ssq[:, i:i + 1]).then_inc(S(f"{n}_ss"), 1)
                act.wait_ge(*done(f"{n}_ms", i + 1))
                nc.scalar.activation(ssq[:, i:i + 1], ssq[:, i:i + 1], ACT.Sqrt).then_inc(S(f"{n}_rt"), 1)

            def evict_h2(i):
                act.wait_ge(*done(f"{n}_ht", i + 1))
                if i >= 1:
                    act.wait_ge(*done(f"{n}_r", i))
                nc.scalar.activation(h2T.rearrange("p k n -> p (k n)"), PS[:, 6:8, :].rearrange("p b n -> p (b n)"), ACT.Copy)\
                    .then_inc(S(f"{n}_he"), 1)
            evict_mix(0)
            evict_mix(1)
            for i in range(len(ts)):
                stats(i)
                if i + 2 < len(ts):
                    evict_mix(i + 2)
                evict_h2(i)

        def out_dve(dve, l):
            n, ts = f"o{l}", out_tiles(l)
            ch = chain(dve)

            def logits(i):
                dve.wait_ge(*done(f"{n}_r", i + 1))
                nc.vector.tensor_tensor(LG[:, ts[i], :], PS[:, 4 + i % 2, 0:NLOG], rb, ALU.add).then_inc(S(f"{n}_lg"), 1)
            for i, t in enumerate(ts):
                if l == 0:
                    dve.wait_ge(*done("o0_x_in" if t < XT else "o0_ctx_in", 16))
                dve.wait_ge(*done(f"{n}_rows", 32 if (l == 0 and i >= 2) else 16))
                for half in range(2):
                    dve.wait_ge(*done(f"{n}_mm", 2 * i + half + 1))
                    c = slice(half * 512, half * 512 + 512)
                    nc.vector.tensor_tensor(tmpb[l][half], PS[:, 2 + half, :], rows[:, 0, c], ALU.mult).then_inc(S(f"{n}_pe"), 1)
                    dve.wait_ge(*done(f"{n}_pe", 2 * i + half + 1))
                    ins = nc.vector.tensor_tensor(XR[:, t, c], XR[:, t, c], tmpb[l][half], ALU.add)
                    if half == 0:
                        ch(ins)
                    else:
                        ins.then_inc(S(f"{n}_x"), 1)
                r = ssq[:, i:i + 1]
                dve.wait_ge(*done(f"{n}_ss", i + 1))
                nc.vector.tensor_scalar(r, r, 1.0 / D, EPS, ALU.mult, ALU.add).then_inc(S(f"{n}_ms"), 1)
                dve.wait_ge(*done(f"{n}_rt", i + 1))
                ch(nc.vector.reciprocal(r, r))
                if i >= 1:
                    dve.wait_ge(*done(f"{n}_ht", i))
                    dve.wait_ge(*done(f"{n}_h2o", 16 * i))
                ch(nc.vector.scalar_tensor_tensor(out=h2, in0=XR[:, t, :], scalar=r, in1=rows[:, 2, :], op0=ALU.mult, op1=ALU.mult))
                nc.vector.tensor_tensor(h2, h2, rows[:, 1, :], ALU.add).then_inc(S(f"{n}_h2"), 1)
                if i >= 1:
                    logits(i - 1)
            logits(len(ts) - 1)

        def tiles_of(l):
            return NT if l == 0 else XT

        def route_views(l):
            nt = tiles_of(l)
            v = {}
            at = WR
            for name, w in (("M1", EXP), ("M2", EXP), ("lm", EXP), ("eq", EXP), ("cand", EXP), ("M", EXP), ("dst", EXP), ("big", EXP), ("g4", GRP), ("e4", GRP)):
                v[name] = R(at, nt * w).rearrange("p (t e) -> p t e", t=nt)
                at += NT * w
            v["C"] = R(at, (NT + 1) * EXP).rearrange("p (t e) -> p t e", t=NT + 1)
            at += (NT + 1) * EXP
            for name in ("gm", "gi", "gs", "gw", "m1", "e1", "m2", "e2", "ex", "rr", "d1", "d2", "pp", "bb"):
                v[name] = R(at, nt)
                at += NT
            v["cnti"] = R(at, EXP).bitcast(I32)
            at += EXP
            for name in ("nov", "cum", "hi", "io128"):
                v[name] = R(at, EXP)
                at += EXP
            v["cmp"] = R(at, OVF * EXP).rearrange("p (b e) -> p b e", b=OVF)
            at += OVF * EXP
            v["eo"] = R(at, OVF)
            at += OVF
            v["ii"] = R(at, 2 * NT).bitcast(I32).rearrange("p (j t) -> p j t", j=2)
            at += 2 * NT
            for j in range(2):
                v[f"onp{j}"] = R(at, nt * P).rearrange("p (t n) -> p t n", t=nt)
                at += NT * P
                v[f"onb{j}"] = R(at, nt * BLK).rearrange("p (t n) -> p t n", t=nt)
                at += NT * BLK
            assert at <= TR
            return v

        def route_dve(dve, l):
            n, nt, v = f"r{l}", tiles_of(l), route_views(l)
            ch = chain(dve)
            V = nc.vector
            iota = bcast_mid(cst[:, C_IO:C_IO + EXP], nt)
            lg, le = LG[:, 0:nt, 0:GRP], LG[:, 0:nt, GRP:NLOG]

            def first_max(x, width, m, e):
                ch(V.tensor_reduce(v[m], x, AXX, ALU.max))
                q, c = (v["eq"], v["cand"]) if width == EXP else (v["g4"], v["e4"])
                ch(V.tensor_tensor(q, x, bcast_in(v[m], width), ALU.is_equal))
                ch(V.tensor_scalar(q, q, -100.0, 100.0, ALU.mult, ALU.add))
                ch(V.tensor_tensor(c, q, bcast_mid(cst[:, C_IO:C_IO + width], nt), ALU.add))
                ch(V.tensor_reduce(v[e], c, AXX, ALU.min))

            first_max(lg, GRP, "gm", "gi")
            V.tensor_tensor(v["e4"], lg, bcast_in(v["gm"], GRP), ALU.subtract).then_inc(S(f"{n}_g"), 1)
            ch(V.tensor_tensor(v["eq"], bcast_mid(cst[:, C_IG:C_IG + EXP], nt), bcast_in(v["gi"], EXP), ALU.is_equal))
            ch(V.tensor_scalar(v["eq"], v["eq"], -NEG, NEG, ALU.mult, ALU.add))
            ch(V.tensor_tensor(v["lm"], le, v["eq"], ALU.add))
            first_max(v["lm"], EXP, "m1", "e1")
            ch(V.tensor_tensor(v["M1"], iota, bcast_in(v["e1"], EXP), ALU.is_equal))
            ch(V.tensor_scalar(v["eq"], v["M1"], 3 * NEG, None, ALU.mult))
            ch(V.tensor_tensor(v["lm"], v["lm"], v["eq"], ALU.add))
            first_max(v["lm"], EXP, "m2", "e2")
            ch(V.tensor_tensor(v["M2"], iota, bcast_in(v["e2"], EXP), ALU.is_equal))
            V.tensor_tensor(v["ex"], v["m2"], v["m1"], ALU.subtract).then_inc(S(f"{n}_x"), 1)
            ch(V.tensor_tensor(v["M"], v["M1"], v["M2"], ALU.add))
            ch(V.memset(v["C"][:, 0, :], 0.0))
            for t in range(nt):
                ins = V.tensor_tensor(v["C"][:, t + 1, :], v["C"][:, t, :], v["M"][:, t, :], ALU.add)
                if t < nt - 1:
                    ch(ins)
            ins.then_inc(S(f"{n}_c"), 1)
            dve.wait_ge(*done(f"{n}_e", 2))
            ch(V.tensor_reduce(v["gs"], v["e4"], AXX, ALU.add))
            ch(V.reciprocal(v["gw"], v["gs"]))
            ch(V.tensor_scalar(v["rr"], v["ex"], 1.0, None, ALU.add))
            ch(V.reciprocal(v["rr"], v["rr"]))
            ch(V.tensor_tensor(wgt[:, 0, 0:nt], v["gw"], v["rr"], ALU.mult))
            ch(V.tensor_tensor(wgt[:, 1, 0:nt], wgt[:, 0, 0:nt], v["ex"], ALU.mult))
            dve.wait_ge(*done(f"{n}_mm", 1))
            ch(V.tensor_scalar(v["cnti"], PS[:, 1, 0:EXP], -1.0, 0.0, ALU.add, ALU.max))
            ch(V.tensor_scalar(v["cnti"], v["cnti"], 7, None, ALU.arith_shift_right))
            ch(V.tensor_copy(v["nov"], v["cnti"]))
            ch(V.tensor_tensor_scan(v["cum"], cst[:, C_ONE:C_ONE + EXP], v["nov"], 0.0, ALU.mult, ALU.add))
            ch(V.tensor_scalar(v["io128"], cst[:, C_IO:C_IO + EXP], float(P), None, ALU.mult))
            ch(V.tensor_tensor(v["hi"], v["cum"], v["nov"], ALU.subtract))
            ch(V.scalar_tensor_tensor(out=v["hi"], in0=v["hi"], scalar=float(P), in1=v["io128"], op0=ALU.mult, op1=ALU.subtract))
            ch(V.tensor_scalar(v["hi"], v["hi"], float((EXP - 1) * P), None, ALU.add))
            rank = PS[:, 0, 0:nt * EXP].rearrange("p (t e) -> p t e", t=nt)
            ch(V.tensor_scalar(v["big"], rank, float(P), None, ALU.is_ge))
            ch(V.tensor_tensor(v["big"], v["big"], bcast_mid(v["hi"], nt), ALU.mult))
            ch(V.tensor_tensor(v["dst"], rank, v["big"], ALU.add))
            ch(V.tensor_tensor(v["dst"], v["dst"], bcast_mid(v["io128"], nt), ALU.add))
            for j, m in enumerate(("M1", "M2")):
                ch(V.tensor_tensor(v[m], v[m], v["dst"], ALU.mult))
                ch(V.tensor_reduce(v["d1"], v[m], AXX, ALU.add))
                ch(V.tensor_copy(dsti[:, j, 0:nt], v["d1"]))
                ch(V.tensor_scalar(v["ii"][:, 0, 0:nt], dsti[:, j, 0:nt], 127, None, ALU.bitwise_and))
                ch(V.tensor_scalar(v["ii"][:, 1, 0:nt], dsti[:, j, 0:nt], 7, None, ALU.arith_shift_right))
                ch(V.tensor_copy(v["pp"], v["ii"][:, 0, 0:nt]))
                ch(V.tensor_copy(v["bb"], v["ii"][:, 1, 0:nt]))
                ch(V.tensor_tensor(v[f"onp{j}"], bcast_mid(cst[:, C_SL:C_SL + P], nt), bcast_in(v["pp"], P), ALU.is_equal))
                ch(V.tensor_tensor(v[f"onb{j}"], bcast_mid(cst[:, C_SL:C_SL + BLK], nt), bcast_in(v["bb"], BLK), ALU.is_equal))
                V.tensor_tensor(v[f"onb{j}"], v[f"onb{j}"], bcast_in(cst[:, C_TOK:C_TOK + nt], BLK), ALU.mult).then_inc(S(f"{n}_pos"), 1)
            dve.wait_ge(*done(f"{n}_st", 1))
            nc.vector.tensor_copy(idx, PS[:, 2, 0:BLK]).then_inc(S(f"{n}_idx"), 1)
            ch(V.tensor_tensor(v["cmp"], bcast_mid(v["cum"], OVF), bcast_in(cst[:, C_IO:C_IO + OVF], EXP), ALU.is_le))
            ch(V.tensor_reduce(v["eo"], v["cmp"], AXX, ALU.add))
            ch(V.tensor_scalar(v["eo"], v["eo"], float(EXP - 1), None, ALU.min))
            ch(V.tensor_copy(ctl[:, 1:1 + OVF], v["eo"]))
            V.tensor_copy(ctl[:, 0:1], v["cum"][:, EXP - 1:EXP]).then_inc(S(f"{n}_ctl"), 1)

        def route_act(act, l):
            n, v = f"r{l}", route_views(l)
            act.wait_ge(*done(f"{n}_g", 1))
            nc.scalar.activation(v["e4"], v["e4"], ACT.Exp).then_inc(S(f"{n}_e"), 1)
            act.wait_ge(*done(f"{n}_x", 1))
            nc.scalar.activation(v["ex"], v["ex"], ACT.Exp).then_inc(S(f"{n}_e"), 1)

        def route_pe(pe, l):
            n, nt, v = f"r{l}", tiles_of(l), route_views(l)
            pe.wait_ge(*done(f"{n}_c", 1))
            flat = lambda a: a.rearrange("p t e -> p (t e)")
            nc.tensor.matmul(PS[:, 0, 0:nt * EXP], cst[:, C_TRI:C_TRI + P], flat(v["M"]), start=True, stop=False)
            nc.tensor.matmul(PS[:, 0, 0:nt * EXP], cst[:, C_ONE:C_ONE + P], flat(v["C"][:, 0:nt, :]), start=False, stop=True)
            nc.tensor.matmul(PS[:, 1, 0:EXP], cst[:, C_ONE:C_ONE + P], v["C"][:, nt, :], start=True, stop=True).then_inc(S(f"{n}_mm"), 1)
            for j in range(2):
                pe.wait_ge(*done(f"{n}_pos", j + 1))
                for t in range(nt):
                    mm = nc.tensor.matmul(PS[:, 2, 0:BLK], v[f"onp{j}"][:, t, :], v[f"onb{j}"][:, t, :],
                                          start=(j == 0 and t == 0), stop=(j == 1 and t == nt - 1))
            mm.then_inc(S(f"{n}_st"), 1)

        def route_pool(pool, l):
            n, nt = f"r{l}", tiles_of(l)
            pool.wait_ge(*done(f"{n}_idx", 1))
            pool.wait_ge(*done(f"o{l}_h2o", 16 * nt))

        def positive(value):
            return not isinstance(value, int) or value > 0

        class Steps:

            def __init__(self, n):
                self.n = n

            def turn(self, pe, e, s, i):
                n = self.n
                pe.wait_ge(*done(f"{n}_hb{s}", 16 * (i + 1)))
                if positive(e):
                    pe.wait_ge(*done(f"{n}_hbT", e))
                for k in range(KC):
                    tr = nc.tensor.transpose(PS[:, k // 4, (k % 4) * P:(k % 4 + 1) * P],
                                             hb[s].rearrange("p (m k) -> p k m", k=KC)[:, k, :], ident)
                tr.then_inc(S(f"{n}_tr"), 1)

            def half(self, pe, e, s, i, up):
                n = self.n
                if not up:
                    pe.wait_ge(*done(f"{n}_hbT", e + 1))
                    pe.wait_ge(*done(f"{n}_wg{s}", 16 * (i + 1)))
                    if positive(e):
                        pe.wait_ge(*done(f"{n}_silu", e))
                else:
                    if positive(e):
                        pe.wait_ge(*done(f"{n}_mul", e))
                for k in range(KC):
                    mm = nc.tensor.matmul(PS[:, 2 + up, :], hbT[s][:, k, :], wgu[s][:, k, up * 512:up * 512 + 512],
                                          start=(k == 0), stop=(k == KC - 1))
                if up:
                    mm.then_inc(S(f"{n}_gu"), 1)

            def turn_gu(self, pe, e, s):
                n = self.n
                pe.wait_ge(*done(f"{n}_mul", e + 1))
                if positive(e):
                    pe.wait_ge(*done(f"{n}_guT", e))
                for k in range(4):
                    tr = nc.tensor.transpose(PS[:, 4, k * P:k * P + P], gub[s].rearrange("p (m k) -> p k m", k=4)[:, k, :], ident)
                tr.then_inc(S(f"{n}_gt"), 1)

            def down(self, pe, e, s, i):
                n = self.n
                pe.wait_ge(*done(f"{n}_guT", e + 1))
                pe.wait_ge(*done(f"{n}_wd{s}", 16 * (i + 1)))
                if positive(e):
                    pe.wait_ge(*done(f"{n}_y", e))
                for c in range(2):
                    for k in range(4):
                        mm = nc.tensor.matmul(PS[:, 5 + c, :], guT[s][:, k, :], wdn[s][:, k, c * 512:c * 512 + 512],
                                              start=(k == 0), stop=(k == 3))
                mm.then_inc(S(f"{n}_dn"), 1)

            def silu(self, act, e, s):
                n = self.n
                act.wait_ge(*done(f"{n}_gu", e + 1))
                if positive(e - 1):
                    act.wait_ge(*done(f"{n}_mul", e - 1))
                nc.scalar.activation(sg[s], PS[:, 2, :], ACT.Silu).then_inc(S(f"{n}_silu"), 1)

            def store(self, act, e, s, i, row):
                n = self.n
                act.wait_ge(*done(f"{n}_dn", e + 1))
                if positive(16 * i):
                    act.wait_ge(*done(f"{n}_yo{s}", 16 * i))
                nc.scalar.activation(yb[s], PS[:, 5:7, :].rearrange("p b n -> p (b n)"), ACT.Copy).then_inc(S(f"{n}_y"), 1)
                act.wait_ge(*done(f"{n}_y", e + 1))
                act.dma_start(yd[bass.ds(row, P), :], yb[s]).then_inc(S(f"{n}_yo{s}"), 16)

            def rows_in(self, dve, e, s, gu_done):
                n = self.n
                dve.wait_ge(*done(f"{n}_tr", e + 1))
                if positive(gu_done):
                    dve.wait_ge(*done(f"{n}_gu", gu_done))
                nc.vector.tensor_copy(hbT[s].rearrange("p k n -> p (k n)"), PS[:, 0:2, :].rearrange("p b n -> p (b n)")).then_inc(S(f"{n}_hbT"), 1)

            def mul(self, dve, e, s, gt_done):
                n = self.n
                dve.wait_ge(*done(f"{n}_silu", e + 1))
                if positive(gt_done):
                    dve.wait_ge(*done(f"{n}_gt", gt_done))
                nc.vector.tensor_tensor(gub[s], PS[:, 3, :], sg[s], ALU.mult).then_inc(S(f"{n}_mul"), 1)

            def gu_in(self, dve, e, s, dn_done):
                n = self.n
                dve.wait_ge(*done(f"{n}_gt", e + 1))
                if positive(dn_done):
                    dve.wait_ge(*done(f"{n}_dn", dn_done))
                nc.vector.tensor_copy(guT[s].rearrange("p k n -> p (k n)"), PS[:, 4, :]).then_inc(S(f"{n}_guT"), 1)

            def gather(self, pool, e, s, col, tr_done):
                n = self.n
                if positive(tr_done):
                    pool.wait_ge(*done(f"{n}_tr", tr_done))
                if isinstance(col, int):
                    column = idx[:, col:col + 1]
                else:
                    column = idxc[s]
                    nc.gpsimd.tensor_copy(column, idx[:, bass.ds(col, 1)])
                    pool.drain()
                pool.indirect_dma_start(out=hb[s], out_offset=None, in_=h2d,
                                        in_offset=bass.IndirectOffsetOnAxis(ap=column, axis=0)).then_inc(S(f"{n}_hb{s}"), 16)

        def wg_src(l, e):
            return A["expert_w_gu"][l, bass.ds(e, 1)].rearrange("e (p k) n -> p (e k n)", k=KC)

        def wd_src(l, e):
            return A["expert_w_down"][l, bass.ds(e, 1)].rearrange("e (p k) n -> p (e k n)", k=4)

        def moe_load(sp, l):
            n = f"m{l}"

            def load(e, s):
                if positive(e - 1):
                    sp.wait_ge(*done(f"{n}_gu", e - 1))
                sp.dma_start(wgu[s].rearrange("p k n -> p (k n)"), wg_src(l, e)).then_inc(S(f"{n}_wg{s}"), 16)
                if positive(e - 1):
                    sp.wait_ge(*done(f"{n}_dn", e - 1))
                sp.dma_start(wdn[s].rearrange("p k n -> p (k n)"), wd_src(l, e)).then_inc(S(f"{n}_wd{s}"), 16)
            return load

        def moe_sp_rest(sp, load):
            with sp.Fori(1, EXP // 2) as i:
                load(2 * i, 0)
                load(2 * i + 1, 1)

        def overflow(eng, l, body):
            eng.wait_ge(*done(f"r{l}_ctl", 1))
            count = eng.value_load(ctl[0:1, 0:1], min_val=0, max_val=OVF)
            with eng.If(count > 0):
                with eng.Fori(0, OVF) as b:
                    with eng.If(count > b):
                        body(b)

        def moe_pe(pe, l):
            k = Steps(f"m{l}")

            def body(e, s, i, first=False):
                j = i if s == 1 else i - 1
                nx = i if s == 0 else i + 1
                k.half(pe, e, s, i, 0)
                if not first:
                    k.turn_gu(pe, e - 1, 1 - s)
                k.turn(pe, e + 1, 1 - s, nx)
                k.half(pe, e, s, i, 1)
                if not first:
                    k.down(pe, e - 1, 1 - s, j)
            k.turn(pe, 0, 0, 0)
            body(0, 0, 0, first=True)
            body(1, 1, 0)
            body(2, 0, 1)
            with pe.Fori(1, EXP // 2 - 1) as i:
                body(2 * i + 1, 1, i)
                body(2 * i + 2, 0, i + 1)
            last, h = EXP - 1, EXP // 2 - 1
            k.half(pe, last, 1, h, 0)
            k.turn_gu(pe, last - 1, 0)
            k.half(pe, last, 1, h, 1)
            k.down(pe, last - 1, 0, h)
            k.turn_gu(pe, last, 1)
            k.down(pe, last, 1, h)

            def block(b):
                e, i = EXP + b, EXP // 2 + b
                k.turn(pe, e, 0, i)
                k.half(pe, e, 0, i, 0)
                k.half(pe, e, 0, i, 1)
                k.turn_gu(pe, e, 0)
                k.down(pe, e, 0, i)
            overflow(pe, l, block)

        def moe_act(act, l):
            k = Steps(f"m{l}")
            k.silu(act, 0, 0)
            k.silu(act, 1, 1)
            k.store(act, 0, 0, 0, 0)
            k.silu(act, 2, 0)
            k.store(act, 1, 1, 0, P)
            with act.Fori(1, EXP // 2 - 1) as i:
                k.silu(act, 2 * i + 1, 1)
                k.store(act, 2 * i, 0, i, 2 * i * P)
                k.silu(act, 2 * i + 2, 0)
                k.store(act, 2 * i + 1, 1, i, (2 * i + 1) * P)
            h = EXP // 2 - 1
            k.silu(act, EXP - 1, 1)
            k.store(act, EXP - 2, 0, h, (EXP - 2) * P)
            k.store(act, EXP - 1, 1, h, (EXP - 1) * P)

            def block(b):
                k.silu(act, EXP + b, 0)
                k.store(act, EXP + b, 0, EXP // 2 + b, (EXP + b) * P)
            act.wait_ge(*done(f"m{l}_yo1", 8 * EXP))
            overflow(act, l, block)
            act.wait_ge(*done(f"m{l}_yo0", act.value_load(ctl[0:1, 0:1], min_val=0, max_val=OVF) * 16 + 8 * EXP))
            nc.scalar.activation(ssq[:, 0:1], ssq[:, 0:1], ACT.Copy).then_inc(S(f"m{l}_all"), 1)

        def moe_dve(dve, l):
            k = Steps(f"m{l}")
            k.rows_in(dve, 0, 0, 0)
            k.rows_in(dve, 1, 1, 0)
            k.mul(dve, 0, 0, 0)

            def pair(i):
                e = 2 * i + 1
                k.gu_in(dve, e - 1, 0, 2 * i)
                k.rows_in(dve, e + 1, 0, e)
                k.mul(dve, e, 1, 2 * i)
                k.gu_in(dve, e, 1, 2 * i)
                k.rows_in(dve, e + 2, 1, e + 1)
                k.mul(dve, e + 1, 0, e)
            pair(0)
            with dve.Fori(1, EXP // 2 - 1) as i:
                pair(i)
            last = EXP - 1
            k.gu_in(dve, last - 1, 0, last - 2)
            k.mul(dve, last, 1, last - 1)
            k.gu_in(dve, last, 1, last - 1)

            def block(b):
                e = EXP + b
                k.rows_in(dve, e, 0, e)
                k.mul(dve, e, 0, e)
                k.gu_in(dve, e, 0, e)
            overflow(dve, l, block)

        def moe_pool(pool, l):
            k = Steps(f"m{l}")
            k.gather(pool, 0, 0, 0, 0)
            k.gather(pool, 1, 1, 1, 0)
            with pool.Fori(1, EXP // 2) as i:
                k.gather(pool, 2 * i, 0, 2 * i, 2 * i - 1)
                k.gather(pool, 2 * i + 1, 1, 2 * i + 1, 2 * i)
            pool.wait_ge(*done(f"m{l}_tr", EXP))
            overflow(pool, l, lambda b: k.gather(pool, EXP + b, 0, EXP + b, EXP + b))

        def moe_sp_all(sp, l):
            load = moe_load(sp, l)
            load(1, 1)
            sp.wait_ge(*done(f"r{l}_idx", 1))
            cmb_sp(sp, l)
            moe_sp_rest(sp, load)
            sp.wait_ge(*done(f"m{l}_dn", EXP))

            def block(b):
                e = sp.value_load(ctl[0:1, bass.ds(b + 1, 1)], min_val=0, max_val=EXP - 1)
                sp.wait_ge(*done(f"m{l}_dn", EXP + b))
                sp.dma_start(wgu[0].rearrange("p k n -> p (k n)"), wg_src(l, e)).then_inc(S(f"m{l}_wg0"), 16)
                sp.dma_start(wdn[0].rearrange("p k n -> p (k n)"), wd_src(l, e)).then_inc(S(f"m{l}_wd0"), 16)
            overflow(sp, l, block)

        def cmb_pool(pool, l):
            n = f"c{l}"
            pool.wait_ge(*done(f"m{l}_all", 1))
            for t in range(tiles_of(l)):
                if t >= 3:
                    pool.wait_ge(*done(f"{n}_used", t - 2))
                for j in range(2):
                    pool.indirect_dma_start(out=yg[t % 3][j], out_offset=None, in_=yd,
                                            in_offset=bass.IndirectOffsetOnAxis(ap=dsti[:, j, t:t + 1], axis=0)).then_inc(S(f"{n}_y{t % 3}"), 16)

        def cmb_sp(sp, l):
            n = f"c{l}"
            for s in range(2):
                sp.dma_start(g2row[:, s, :], mod[l, s, 5 * D:6 * D].partition_broadcast(P)).then_inc(S(f"{n}_g"), 16)
            if l == 1:
                sp.dma_start(fgrow, A["final_g"].partition_broadcast(P)).then_inc(S(f"{n}_g"), 16)
            else:
                sp.dma_start(COS, A["rope"].rearrange("p (t f n) -> p t f n", t=XT, f=2)).then_inc(S("cos_in1"), 16)

        def final_sp(sp):
            for t in range(XT):
                sp.wait_ge(*done("fin", t + 1))
                sp.dma_start(out[0, t * P:t * P + P, :], outb[t % 2]).then_inc(S(f"out{t % 2}"), 16)
            for q in range(2):
                sp.wait_ge(*done(f"out{q}", 16 * (XT // 2)))

        def cmb_tile(dve, l):
            n = f"c{l}"
            ch = chain(dve)

            def combine(t):
                if t == 0:
                    dve.wait_ge(*done(f"{n}_g", 32 if l == 0 else 48))
                dve.wait_ge(*done(f"{n}_sc", t + 1))
                y1, y2 = yg[t % 3]
                if t >= 1:
                    dve.wait_ge(*done(f"{n}_x", t))
                nc.vector.scalar_tensor_tensor(out=cmb, in0=y2, scalar=wgt[:, 1, t:t + 1], in1=y1, op0=ALU.mult, op1=ALU.add)\
                    .then_inc(S(f"{n}_used"), 1)
                dve.wait_ge(*done(f"{n}_used", t + 1))
                ch(nc.vector.tensor_tensor(cmb, cmb, g2row[:, 0 if t < XT else 1, :], ALU.mult))
                nc.vector.tensor_tensor(XR[:, t, :], XR[:, t, :], cmb, ALU.add).then_inc(S(f"{n}_x"), 1)
            return combine

        def cmb_scale(act, l):
            n = f"c{l}"

            def scale(t):
                act.wait_ge(*done(f"{n}_y{t % 3}", 32 * (t // 3 + 1)))
                y1 = yg[t % 3][0]
                nc.scalar.activation(y1, y1, ACT.Copy, scale=wgt[:, 0, t:t + 1]).then_inc(S(f"{n}_sc"), 1)
            return scale

        def final_dve(dve):
            ch = chain(dve)
            combine = cmb_tile(dve, 1)
            combine(0)
            for t in range(XT):
                if t + 1 < XT:
                    combine(t + 1)
                r = ssq[:, t:t + 1]
                dve.wait_ge(*done("fin_ss", t + 1))
                nc.vector.tensor_scalar(r, r, 1.0 / D, EPS, ALU.mult, ALU.add).then_inc(S("fin_ms"), 1)
                dve.wait_ge(*done("fin_rt", t + 1))
                ch(nc.vector.reciprocal(r, r))
                if t >= 2:
                    dve.wait_ge(*done(f"out{t % 2}", 16 * (t // 2)))
                nc.vector.scalar_tensor_tensor(out=outb[t % 2], in0=XR[:, t, :], scalar=r, in1=fgrow, op0=ALU.mult, op1=ALU.mult)\
                    .then_inc(S("fin"), 1)

        def final_act(act):
            scale = cmb_scale(act, 1)
            scale(0)
            for t in range(XT):
                if t + 1 < XT:
                    scale(t + 1)
                act.wait_ge(*done("c1_x", t + 1))
                nc.scalar.activation(sqj[1], XR[:, t, :], ACT.Square, accum_out=ssq[:, t:t + 1]).then_inc(S("fin_ss"), 1)
                act.wait_ge(*done("fin_ms", t + 1))
                nc.scalar.activation(ssq[:, t:t + 1], ssq[:, t:t + 1], ACT.Sqrt).then_inc(S("fin_rt"), 1)

        na, sw = units_na(), units_swa()
        number_queries(na)
        number_queries(sw)
        block = ctx.enter_context(nc.Block())

        MEET = ["proj", "projb", "att", "out", "moe",
                "projc", "attb", "outb", "moeb"]
        num = {m: i + 1 for i, m in enumerate(MEET)}

        def dbg(sp):
            if "dbg" in A:
                for a, b in DBG:
                    sp.dma_start(A["dbg"][:, a:b], ar[:, a:b]).then_inc(S("dbg_out"), 16)
                sp.wait_ge(*done("dbg_out", 16 * len(DBG)))

        @block.sync
        def _(sp):
            ada_sp(sp)
            proj_sp(sp, pa, (2, 3))
            sp.wait_ge(*done("phase", 4 * num["proj"]))
            if STAGE < 3:
                sp.wait_ge(*done("skew_out", 16 * NAH))
                return dbg(sp)
            sp.dma_start(gain, A["ret_gn"][0].partition_broadcast(P)).then_inc(S("gain_in"), 16)
            proj_sp(sp, pb)
            after_meet(sp, num["projb"])
            if STAGE < 4:
                sp.wait_ge(*done("skew_out", 16 * NAH))
                return dbg(sp)
            sp.dma_start(BAND, A["band"]).then_inc(S("band_in0"), 16)
            sp.wait_ge(*done("skew_out", 16 * NAH))
            for h in range(NAH):
                if h >= 2:
                    sp.wait_ge(*done(f"toep_in{h % 2}", 32 * (h // 2)))
                for q in range(2):
                    sp.dma_start(TOEP[64 * q:64 * q + 64, h], skew[:, h, 1 - q:19 - q, :]).then_inc(S(f"toep_in{h % 2}"), 16)
            out_weights(sp, 0)
            sp.wait_ge(*done("band_in0", 16))
            for b in range(OVF):
                sp.dma_start(yd[(EXP + b) * P:(EXP + b + 1) * P, :].rearrange("p (c n) -> p c n", c=4),
                             BAND[:, 0:256].unsqueeze(1).to_broadcast([P, 4, 256])).then_inc(S("rows_zero"), 16)
            sp.wait_ge(*done("rows_zero", 16 * OVF))
            after_meet(sp, num["att"])
            if STAGE < 5:
                return dbg(sp)
            out_sp(sp, 0)
            after_meet(sp, num["out"])
            if STAGE < 6:
                return dbg(sp)
            moe_sp_all(sp, 0)
            after_meet(sp, num["moe"])
            sp.wait_ge(*done("c0_y0", 32))
            proj_sp(sp, pc, (0,))
            sp.wait_ge(*done("c0_used", 3))
            proj_sp(sp, pc, (1, 2))
            after_meet(sp, num["projc"])
            sp.dma_start(BAND, A["band"]).then_inc(S("band_in1"), 16)
            sp.dma_start(sinkr, A["swa_sink"][0].partition_broadcast(P)).then_inc(S("sink_in"), 16)
            out_weights(sp, 1)
            after_meet(sp, num["attb"])
            if STAGE < 8:
                return dbg(sp)
            out_sp(sp, 1)
            after_meet(sp, num["outb"])
            moe_sp_all(sp, 1)
            after_meet(sp, num["moeb"])
            final_sp(sp)

        @block.tensor
        def _(pe):
            ada_pe(pe)
            n1_pe(pe, 0)
            meet(pe, num["proj"])
            if STAGE < 3:
                return
            core_pe(pe)
            meet(pe, num["projb"])
            if STAGE < 4:
                return
            att_pe(pe, na, "na")
            meet(pe, num["att"])
            if STAGE < 5:
                return
            out_pe(pe, 0)
            meet(pe, num["out"])
            route_pe(pe, 0)
            moe_pe(pe, 0)
            meet(pe, num["moe"])
            n1_pe(pe, 1)
            meet(pe, num["projc"])
            att_pe(pe, sw, "sw")
            meet(pe, num["attb"])
            if STAGE < 8:
                return
            out_pe(pe, 1)
            meet(pe, num["outb"])
            route_pe(pe, 1)
            moe_pe(pe, 1)
            meet(pe, num["moeb"])

        @block.scalar
        def _(act):
            ada_act(act)
            n1_act(act, 0)
            meet(act, num["proj"])
            if STAGE < 3:
                return
            core_act(act)
            meet(act, num["projb"])
            if STAGE < 4:
                return
            att_act(act, na, "na")
            meet(act, num["att"])
            if STAGE < 5:
                return
            out_act(act, 0)
            meet(act, num["out"])
            route_act(act, 0)
            moe_act(act, 0)
            meet(act, num["moe"])
            n1_act(act, 1)
            meet(act, num["projc"])
            att_act(act, sw, "sw")
            meet(act, num["attb"])
            if STAGE < 8:
                return
            out_act(act, 1)
            meet(act, num["outb"])
            route_act(act, 1)
            moe_act(act, 1)
            meet(act, num["moeb"])
            final_act(act)

        @block.vector
        def _(dve):
            ada_dve(dve)
            n1_dve(dve, 0)
            scan(dve, nc.vector, 0)
            meet(dve, num["proj"])
            if STAGE < 3:
                return
            dve.wait_ge(*done("gain_in", 16))
            core_dve(dve)
            meet(dve, num["projb"])
            if STAGE < 4:
                return
            dve.wait_ge(*done("band_in0", 16))
            att_dve(dve, na, "na")
            meet(dve, num["att"])
            if STAGE < 5:
                return
            out_dve(dve, 0)
            meet(dve, num["out"])
            route_dve(dve, 0)
            moe_dve(dve, 0)
            meet(dve, num["moe"])
            n1_dve(dve, 1)
            meet(dve, num["projc"])
            dve.wait_ge(*done("band_in1", 16))
            att_dve(dve, sw, "sw")
            meet(dve, num["attb"])
            if STAGE < 8:
                return
            out_dve(dve, 1)
            meet(dve, num["outb"])
            route_dve(dve, 1)
            moe_dve(dve, 1)
            meet(dve, num["moeb"])
            final_dve(dve)

        @block.gpsimd
        def _(pool):
            proj_pool(pool)
            scan(pool, nc.gpsimd, 1)
            meet(pool, num["proj"])
            if STAGE < 3:
                return
            meet(pool, num["projb"])
            if STAGE < 4:
                return
            att_pool(pool, na, "na")
            meet(pool, num["att"])
            if STAGE < 5:
                return
            meet(pool, num["out"])
            route_pool(pool, 0)
            moe_pool(pool, 0)
            meet(pool, num["moe"])
            cmb_pool(pool, 0)
            meet(pool, num["projc"])
            att_pool(pool, sw, "sw")
            meet(pool, num["attb"])
            if STAGE < 8:
                return
            meet(pool, num["outb"])
            route_pool(pool, 1)
            moe_pool(pool, 1)
            meet(pool, num["moeb"])
            cmb_pool(pool, 1)


_INS = ['x', 'c', 'ctx', 'c_ctx', 'ada_w', 'ada_b', 'norm_g', 'final_g', 'ab_w_in', 'ab_w_out', 'ret_decay', 'ret_gn',
        'na_rpb', 'swa_w_in', 'swa_w_out', 'swa_sink', 'router_g_w', 'router_g_b', 'router_e_w', 'router_e_b',
        'expert_w_gu', 'expert_w_down']
DBG = None


def kernel(**inputs):
    import numpy as _np
    import concourse.bacc as _bacc
    from concourse import mybir as _mybir
    from concourse.bass_utils import run_bass_kernel_spmd as _run

    nc = _bacc.Bacc("TRN2", target_bir_lowering=False, num_devices=1)
    arrays, args = {}, {}
    cst, band, rope = tables()
    for name, a in [(n, inputs[n]) for n in _INS] + [("cst", cst), ("band", band), ("rope", rope)]:
        a = _np.ascontiguousarray(a)
        arrays[f"in_{name}_dram"] = a
        args[name] = nc.dram_tensor(f"in_{name}_dram", a.shape, _mybir.dt.from_np(a.dtype), kind="ExternalInput").ap()
    if DBG:
        args["dbg"] = nc.dram_tensor("dbg", (P, 51456), F32, kind="ExternalOutput").ap()
    out = nc.dram_tensor("out_0_dram", (1, SEQ, D), F32, kind="ExternalOutput").ap()
    program(nc, args, out)
    r = _run(nc, [arrays], core_ids=[0])
    return r.results[0]["out_0_dram"]
```
